# Optimizing a Trainium2 kernel written in Bass

```python
import math
import jax
import jax.numpy as jnp
from jax import lax
import numpy as np

D_MODEL = 1024
BATCH = 1
SEQ = 256
DEPTH = 1

GRID_W = 64
CTX_LEN = 256

N_MIXERS = 2
MIXER_DELTA = 0
MIXER_HYENA = 1
N_DELTA_LAYERS = (DEPTH - MIXER_DELTA + N_MIXERS - 1) // N_MIXERS
N_HYENA_LAYERS = (DEPTH - MIXER_HYENA + N_MIXERS - 1) // N_MIXERS

EPS = 1e-6

DN_HEAD_DIM = 128
DN_HEADS = D_MODEL // DN_HEAD_DIM
DN_INNER = DN_HEADS * DN_HEAD_DIM
DN_CONV = 5
DN_CHUNK = 64
DN_CHUNK_LOG2 = 6
DN_PROJ = 4 * DN_INNER + 4 * DN_HEADS

HY_WIDTH = D_MODEL
HY_SHORT = 3
HY_BANDS = 16
HY_EMB = 1 + 2 * HY_BANDS
HY_FF = 64
HY_FAST = 0.3
HY_SLOW = 1.5
HY_TARGET = 1e-2

PEER_HEADS = 8
PEER_NKEYS = 128
PEER_EXPERTS = PEER_NKEYS * PEER_NKEYS
PEER_DK = 256
PEER_TOPK = 16
PEER_BLOCK = 128


def _rmsnorm(x, g):
    xf = x.astype(jnp.float32)
    y = xf * lax.rsqrt(jnp.mean(xf * xf, axis=-1, keepdims=True) + EPS)
    return (y * g.astype(jnp.float32)).astype(x.dtype)

def _modulate(xn, shift, scale):
    return xn * (1 + scale) + shift

def _l2norm(x):
    xf = x.astype(jnp.float32)
    return xf * lax.rsqrt(jnp.sum(xf * xf, axis=-1, keepdims=True) + EPS)

def _rev(t):
    return jnp.flip(t, axis=2)

def _short_conv(x, w, n_rows):
    B, L, C = x.shape
    K = w.shape[0]
    xr = x.reshape(B * n_rows, L // n_rows, C)
    y = lax.conv_general_dilated(
        xr, w.astype(x.dtype)[:, None, :], window_strides=(1,),
        padding=[((K - 1) // 2, (K - 1) // 2)],
        dimension_numbers=('NWC', 'WIO', 'NWC'), feature_group_count=C)
    return y.reshape(B, L, C)

def _dn_inputs(hn, n_rows, w_in, conv_w, a_log, dt_bias):
    B, L, _ = hn.shape
    z = hn @ w_in
    qkv = jax.nn.silu(_short_conv(z[..., :3 * DN_INNER], conv_w, n_rows))
    gate = z[..., 3 * DN_INNER:4 * DN_INNER]
    ba = z[..., 4 * DN_INNER:].astype(jnp.float32).reshape(B, L, 2, 2, DN_HEADS)
    qkv = qkv.reshape(B, L, 3, DN_HEADS, DN_HEAD_DIM).transpose(2, 0, 3, 1, 4)
    q = _l2norm(qkv[0]) * (DN_HEAD_DIM ** -0.5)
    k = _l2norm(qkv[1])
    v = qkv[2].astype(jnp.float32)
    beta = jax.nn.sigmoid(ba[:, :, 0]).transpose(0, 2, 3, 1)
    g = (-jnp.exp(a_log.astype(jnp.float32)) *
         jax.nn.softplus(ba[:, :, 1] + dt_bias.astype(jnp.float32))).transpose(0, 2, 3, 1)
    return q, k, v, beta, g, gate

def _unit_lower_inverse(a):
    eye = jnp.eye(a.shape[-1], dtype=a.dtype)
    t = eye - a
    p = a
    for _ in range(DN_CHUNK_LOG2 - 1):
        p = p @ p
        t = t @ (eye + p)
    return t

def _gated_delta_chunked(k, v, beta, g, s0, q=None):
    f32 = jnp.float32
    with_out = q is not None
    B, H, L, DK = k.shape
    DV = v.shape[-1]
    C = DN_CHUNK
    n = L // C
    k = k.astype(f32).reshape(B, H, n, C, DK)
    v = v.astype(f32).reshape(B, H, n, C, DV)
    beta = beta.astype(f32).reshape(B, H, n, C)
    G = jnp.cumsum(g.astype(f32).reshape(B, H, n, C), axis=-1)
    incl = jnp.tril(jnp.ones((C, C), bool))
    strict = jnp.tril(jnp.ones((C, C), bool), -1)
    dmat = jnp.exp(jnp.where(incl, G[..., :, None] - G[..., None, :], -jnp.inf))
    kb = k * beta[..., None]
    a = jnp.where(strict, jnp.einsum('bhnid,bhnjd->bhnij', kb, k) * dmat, 0.0)
    t = _unit_lower_inverse(a)
    u = t @ (v * beta[..., None])
    w = t @ (kb * jnp.exp(G)[..., None])
    kd = k * jnp.exp(G[..., -1:] - G)[..., None]
    gl = jnp.exp(G[..., -1])
    xs = (jnp.moveaxis(w, 2, 0), jnp.moveaxis(u, 2, 0), jnp.moveaxis(kd, 2, 0), jnp.moveaxis(gl, 2, 0))
    if with_out:
        q = q.astype(f32).reshape(B, H, n, C, DK)
        qa = jnp.einsum('bhnid,bhnjd->bhnij', q, k) * dmat
        qg = q * jnp.exp(G)[..., None]
        xs = xs + (jnp.moveaxis(qg, 2, 0), jnp.moveaxis(qa, 2, 0))

    def step(s, inp):
        w_c, u_c, kd_c, gl_c = inp[:4]
        v_new = u_c - jnp.einsum('bhck,bhkv->bhcv', w_c, s)
        s_next = s * gl_c[..., None, None] + jnp.einsum('bhck,bhcv->bhkv', kd_c, v_new)
        if not with_out:
            return s_next, None
        qg_c, qa_c = inp[4:]
        o_c = jnp.einsum('bhck,bhkv->bhcv', qg_c, s) + jnp.einsum('bhij,bhjv->bhiv', qa_c, v_new)
        return s_next, o_c

    s_fin, o = lax.scan(step, s0.astype(f32), xs)
    if not with_out:
        return None, s_fin
    return jnp.moveaxis(o, 0, 2).reshape(B, H, L, DV), s_fin

def _gated_out(o, gate, g_norm, w_out):
    B, H, L, DV = o.shape
    o = jnp.swapaxes(o, 1, 2)
    on = o * lax.rsqrt(jnp.mean(o * o, axis=-1, keepdims=True) + EPS) * g_norm.astype(jnp.float32)
    y = on * jax.nn.silu(gate.astype(jnp.float32)).reshape(B, L, H, DV)
    return y.reshape(B, L, H * DV).astype(gate.dtype) @ w_out

def _deltanet(hn, hcn, n_rows, w_in, conv_w, a_log, dt_bias, o_norm_g, w_out, ctx_out):
    q, k, v, beta, g, gate = _dn_inputs(hn, n_rows, w_in, conv_w, a_log, dt_bias)
    qc, kc, vc, betac, gc, gatec = _dn_inputs(hcn, 1, w_in, conv_w, a_log, dt_bias)
    B = hn.shape[0]
    s0 = jnp.zeros((B, DN_HEADS, DN_HEAD_DIM, DN_HEAD_DIM), jnp.float32)
    oc_f, sc_f = _gated_delta_chunked(kc, vc, betac[:, 0], gc[:, 0], s0, qc if ctx_out else None)
    oc_b, sc_b = _gated_delta_chunked(_rev(kc), _rev(vc), _rev(betac[:, 1]), _rev(gc[:, 1]), s0,
                                      _rev(qc) if ctx_out else None)
    o_f, _ = _gated_delta_chunked(k, v, beta[:, 0], g[:, 0], sc_f, q)
    o_b, _ = _gated_delta_chunked(_rev(k), _rev(v), _rev(beta[:, 1]), _rev(g[:, 1]), sc_b, _rev(q))
    y = _gated_out(o_f + _rev(o_b), gate, o_norm_g, w_out)
    yc = _gated_out(oc_f + _rev(oc_b), gatec, o_norm_g, w_out) if ctx_out else None
    return y, yc

def _hyena_filters(L, w1, b1, w2, b2, w3, b3, w4, freq):
    f32 = jnp.float32
    D = w4.shape[-1] // 4
    pos = jnp.arange(L, dtype=f32)
    t = pos / max(L - 1, 1)
    ang = (2 * math.pi * pos / L)[:, None] * jnp.linspace(1e-4, HY_BANDS - 1, HY_BANDS, dtype=f32)[None]
    z = jnp.concatenate([t[:, None], jnp.cos(ang), -jnp.sin(ang)], axis=-1)
    fr = freq.astype(f32)
    hid = jnp.sin(fr * (z @ w1.astype(f32) + b1.astype(f32)))
    hid = jnp.sin(fr * (hid @ w2.astype(f32) + b2.astype(f32)))
    hid = jnp.sin(fr * (hid @ w3.astype(f32) + b3.astype(f32)))
    h = hid @ w4.astype(f32)
    deltas = jnp.abs(jnp.linspace(math.log(HY_TARGET) / HY_FAST, math.log(HY_TARGET) / HY_SLOW, D, dtype=f32))
    decay = jnp.exp(-t[:, None] * deltas[None])
    return (h.reshape(L, 2, 2, D) * decay[:, None, None, :]).transpose(1, 2, 0, 3)

def _long_conv(u, hf, hb, d):
    B, L, D = u.shape
    filt2 = jnp.concatenate([hf, jnp.zeros((1, D), jnp.float32), jnp.flip(hb[1:], axis=0)], axis=0)
    uf = jnp.fft.rfft(u.astype(jnp.float32), n=2 * L, axis=1)
    y = jnp.fft.irfft(uf * jnp.fft.rfft(filt2, axis=0)[None], n=2 * L, axis=1)[:, :L]
    return (y + u.astype(jnp.float32) * d.astype(jnp.float32)).astype(u.dtype)

def _hyena(hn, n_rows, w_in, conv_w, conv_b, f_w1, f_b1, f_w2, f_b2, f_w3, f_b3, f_w4, freq, skip, w_out):
    B, L, _ = hn.shape
    z = _short_conv(hn @ w_in, conv_w, n_rows) + conv_b.astype(hn.dtype)
    v, x1, x2 = jnp.split(z, 3, axis=-1)
    filt = _hyena_filters(L, f_w1, f_b1, f_w2, f_b2, f_w3, f_b3, f_w4, freq)
    z1 = x1 * _long_conv(v, filt[0, 0], filt[0, 1], skip[0])
    z2 = x2 * _long_conv(z1, filt[1, 0], filt[1, 1], skip[1])
    return z2 @ w_out

def _peer(x, w_q, sub_keys, u_tab, v_tab):
    B, L, D = x.shape
    T = B * L
    xt = x.reshape(T, D)
    q = (xt @ w_q).astype(jnp.float32).reshape(T, PEER_HEADS, 2, PEER_DK // 2)
    s = jnp.einsum('thpd,hpkd->thpk', q, sub_keys.astype(jnp.float32))
    s1, i1 = lax.top_k(s[:, :, 0], PEER_TOPK)
    s2, i2 = lax.top_k(s[:, :, 1], PEER_TOPK)
    n_cand = PEER_TOPK * PEER_TOPK
    cand_s = (s1[..., :, None] + s2[..., None, :]).reshape(T, PEER_HEADS, n_cand)
    cand_i = (i1[..., :, None] * PEER_NKEYS + i2[..., None, :]).reshape(T, PEER_HEADS, n_cand)
    top_s, pos = lax.top_k(cand_s, PEER_TOPK)
    idx = jnp.take_along_axis(cand_i, pos, axis=-1)
    gate = jax.nn.softmax(top_s, axis=-1)
    nb = T // PEER_BLOCK

    def expert_block(args):
        xb, ib, gb = args
        hid = jnp.einsum('td,thkd->thk', xb, u_tab[ib]).astype(jnp.float32)
        coef = (jax.nn.gelu(hid, approximate=False) * gb).astype(xb.dtype)
        return jnp.einsum('thk,thkd->td', coef, v_tab[ib])

    y = lax.map(expert_block, (xt.reshape(nb, PEER_BLOCK, D),
                               idx.reshape(nb, PEER_BLOCK, PEER_HEADS, PEER_TOPK),
                               gate.reshape(nb, PEER_BLOCK, PEER_HEADS, PEER_TOPK)))
    return y.reshape(B, L, D)

def first_inputs(seed: int = 0) -> dict:
    key = jax.random.key(seed)
    ks = iter(jax.random.split(key, 32))
    f32 = jnp.float32
    D = D_MODEL

    def nrm(shape, scale):
        return jax.random.normal(next(ks), shape, f32) * scale

    x = nrm((BATCH, SEQ, D), 1.0)
    c = nrm((BATCH, D), 1.0)
    ctx = nrm((BATCH, CTX_LEN, D), 1.0)
    c_ctx = nrm((D,), 1.0)
    ada_w = nrm((DEPTH, D, 6 * D), 0.5 * D ** -0.5)
    ada_b = nrm((DEPTH, 6 * D), 0.02)
    norm_g = 1.0 + nrm((DEPTH, 2, D), 0.02)
    dn_w_in = nrm((N_DELTA_LAYERS, D, DN_PROJ), D ** -0.5)
    dn_conv_w = nrm((N_DELTA_LAYERS, DN_CONV, 3 * DN_INNER), DN_CONV ** -0.5)
    dn_a_log = jnp.log(jax.random.uniform(next(ks), (N_DELTA_LAYERS, 2, DN_HEADS), f32, 1.0, 16.0))
    dt = jnp.exp(jax.random.uniform(next(ks), (N_DELTA_LAYERS, 2, DN_HEADS), f32,
                                    math.log(1e-3), math.log(1e-1)))
    dn_dt_bias = dt + jnp.log(-jnp.expm1(-dt))
    dn_norm_g = 1.0 + nrm((N_DELTA_LAYERS, DN_HEAD_DIM), 0.02)
    dn_w_out = nrm((N_DELTA_LAYERS, DN_INNER, D), DN_INNER ** -0.5)
    hy_w_in = nrm((N_HYENA_LAYERS, D, 3 * HY_WIDTH), D ** -0.5)
    hy_conv_w = nrm((N_HYENA_LAYERS, HY_SHORT, 3 * HY_WIDTH), HY_SHORT ** -0.5)
    hy_conv_b = nrm((N_HYENA_LAYERS, 3 * HY_WIDTH), 0.02)
    hy_f_w1 = nrm((N_HYENA_LAYERS, HY_EMB, HY_FF), HY_EMB ** -0.5)
    hy_f_b1 = nrm((N_HYENA_LAYERS, HY_FF), 0.02)
    hy_f_w2 = nrm((N_HYENA_LAYERS, HY_FF, HY_FF), HY_FF ** -0.5)
    hy_f_b2 = nrm((N_HYENA_LAYERS, HY_FF), 0.02)
    hy_f_w3 = nrm((N_HYENA_LAYERS, HY_FF, HY_FF), HY_FF ** -0.5)
    hy_f_b3 = nrm((N_HYENA_LAYERS, HY_FF), 0.02)
    hy_f_w4 = nrm((N_HYENA_LAYERS, HY_FF, 4 * HY_WIDTH), 0.02 * HY_FF ** -0.5)
    hy_freq = 1.0 + nrm((N_HYENA_LAYERS, HY_FF), 0.02)
    hy_skip = nrm((N_HYENA_LAYERS, 2, HY_WIDTH), 1.0)
    hy_w_out = nrm((N_HYENA_LAYERS, HY_WIDTH, D), HY_WIDTH ** -0.5)
    peer_w_q = nrm((DEPTH, D, PEER_HEADS * PEER_DK), D ** -0.5)
    peer_keys = nrm((DEPTH, PEER_HEADS, 2, PEER_NKEYS, PEER_DK // 2), (PEER_DK // 2) ** -0.5)
    peer_u = nrm((DEPTH, PEER_EXPERTS, D), D ** -0.5)
    peer_v = nrm((DEPTH, PEER_EXPERTS, D), PEER_HEADS ** -0.5)
    final_g = 1.0 + nrm((D,), 0.02)
    return {"x": x, "c": c, "ctx": ctx, "c_ctx": c_ctx,
            "ada_w": ada_w, "ada_b": ada_b, "norm_g": norm_g,
            "dn_w_in": dn_w_in, "dn_conv_w": dn_conv_w, "dn_a_log": dn_a_log, "dn_dt_bias": dn_dt_bias,
            "dn_norm_g": dn_norm_g, "dn_w_out": dn_w_out,
            "hy_w_in": hy_w_in, "hy_conv_w": hy_conv_w, "hy_conv_b": hy_conv_b,
            "hy_f_w1": hy_f_w1, "hy_f_b1": hy_f_b1, "hy_f_w2": hy_f_w2, "hy_f_b2": hy_f_b2,
            "hy_f_w3": hy_f_w3, "hy_f_b3": hy_f_b3, "hy_f_w4": hy_f_w4, "hy_freq": hy_freq,
            "hy_skip": hy_skip, "hy_w_out": hy_w_out,
            "peer_w_q": peer_w_q, "peer_keys": peer_keys, "peer_u": peer_u, "peer_v": peer_v,
            "final_g": final_g}

def first_block(x, c, ctx, c_ctx, ada_w, ada_b, norm_g,
              dn_w_in, dn_conv_w, dn_a_log, dn_dt_bias, dn_norm_g, dn_w_out,
              hy_w_in, hy_conv_w, hy_conv_b, hy_f_w1, hy_f_b1, hy_f_w2, hy_f_b2,
              hy_f_w3, hy_f_b3, hy_f_w4, hy_freq, hy_skip, hy_w_out,
              peer_w_q, peer_keys, peer_u, peer_v, final_g):
    f32 = jnp.float32
    B, L, D = x.shape
    rows = L // GRID_W
    silu_c = jax.nn.silu(c.astype(f32))
    silu_cc = jax.nn.silu(c_ctx.astype(f32))
    h, hc = x, ctx
    for i in range(DEPTH):
        kind = i % N_MIXERS
        j = i // N_MIXERS
        ctx_out = any(l % N_MIXERS == MIXER_DELTA for l in range(i + 1, DEPTH))
        ctx_in = kind == MIXER_DELTA or ctx_out
        w_ada = ada_w[i].astype(f32)
        b_ada = ada_b[i].astype(f32)
        mod = (silu_c @ w_ada + b_ada).astype(h.dtype).reshape(B, 6, 1, D)
        sh1, sc1, gt1, sh2, sc2, gt2 = [mod[:, m] for m in range(6)]
        hn = _modulate(_rmsnorm(h, norm_g[i, 0]), sh1, sc1)
        hcn = None
        if ctx_in:
            modc = (silu_cc @ w_ada + b_ada).astype(hc.dtype).reshape(6, D)
            hcn = _modulate(_rmsnorm(hc, norm_g[i, 0]), modc[0], modc[1])
        if kind == MIXER_DELTA:
            y, yc = _deltanet(hn, hcn, rows, dn_w_in[j], dn_conv_w[j], dn_a_log[j], dn_dt_bias[j],
                              dn_norm_g[j], dn_w_out[j], ctx_out)
        else:
            hy_args = (hy_w_in[j], hy_conv_w[j], hy_conv_b[j], hy_f_w1[j], hy_f_b1[j], hy_f_w2[j],
                       hy_f_b2[j], hy_f_w3[j], hy_f_b3[j], hy_f_w4[j], hy_freq[j], hy_skip[j], hy_w_out[j])
            y = _hyena(hn, rows, *hy_args)
            yc = _hyena(hcn, 1, *hy_args) if ctx_out else None
        h = h + gt1 * y
        peer_args = (peer_w_q[i], peer_keys[i], peer_u[i], peer_v[i])
        h = h + gt2 * _peer(_modulate(_rmsnorm(h, norm_g[i, 1]), sh2, sc2), *peer_args)
        if ctx_out:
            hc = hc + modc[2] * yc
            hc = hc + modc[5] * _peer(_modulate(_rmsnorm(hc, norm_g[i, 1]), modc[3], modc[4]), *peer_args)
    return _rmsnorm(h, final_g)


DEPTH_2 = 2

D_MIX = D_MODEL
SSD_WIDTH = D_MIX // 2
SSD_HEAD_DIM = 64
SSD_HEADS = SSD_WIDTH // SSD_HEAD_DIM
SSD_GROUPS = 2
SSD_STATE = 64
SSD_CONV = 4
SSD_CONV_DIM = SSD_WIDTH + 2 * SSD_GROUPS * SSD_STATE
SSD_CHUNK = 128
DT_MIN = 0.001
DT_MAX = 0.1
HGRN_WIDTH = D_MIX // 4
HGRN_HEAD_DIM = 64
HGRN_HEADS = HGRN_WIDTH // HGRN_HEAD_DIM
HGRN_CHUNK = 16
GATE_FLOOR = 1e-30
RET_WIDTH = D_MIX // 4
RET_HEAD_DIM = 64
RET_HEADS = RET_WIDTH // RET_HEAD_DIM
RET_CHUNK = 128
ROPE_BASE = 10000.0
IN_WIDTHS = (SSD_WIDTH, SSD_CONV_DIM, SSD_HEADS,
             HGRN_WIDTH, HGRN_WIDTH, HGRN_WIDTH, HGRN_WIDTH,
             RET_WIDTH, RET_WIDTH, RET_WIDTH, RET_WIDTH)
D_IN = SSD_WIDTH + SSD_CONV_DIM + SSD_HEADS + 4 * HGRN_WIDTH + 4 * RET_WIDTH
N_GROUPS = 4
EXPERTS_PER_GROUP = 8
N_EXPERTS = N_GROUPS * EXPERTS_PER_GROUP
TOP_K = 2
D_EXPERT = D_MODEL // 4
ADA_SCALE = 0.5


def rms(x):
    xf = x.astype(jnp.float32)
    return xf * lax.rsqrt(jnp.mean(xf * xf, axis=-1, keepdims=True) + EPS)

def rmsnorm(x, g):
    return rms(x) * g

def causal_depthwise_conv(x, w, bias):
    width, ch = w.shape
    out = lax.conv_general_dilated(
        x, w[:, None, :].astype(x.dtype), window_strides=(1,), padding=[(width - 1, 0)],
        dimension_numbers=('NWC', 'WIO', 'NWC'), feature_group_count=ch)
    return out + bias

def rotary(x, pos):
    half = x.shape[-1] // 2
    inv_freq = ROPE_BASE ** (-jnp.arange(half, dtype=jnp.float32) / half)
    ang = pos[:, None] * inv_freq[None, :]
    cos = jnp.cos(ang)[None, :, None, :]
    sin = jnp.sin(ang)[None, :, None, :]
    x1 = x[..., :half].astype(jnp.float32)
    x2 = x[..., half:].astype(jnp.float32)
    return jnp.concatenate([x1 * cos - x2 * sin, x1 * sin + x2 * cos], axis=-1)

def chunked_linear_recurrence(q, k, v, log_a, chunk):
    b, l, h, dk = q.shape
    dv = v.shape[-1]
    nc = l // chunk
    q, k, v, log_a = (t.astype(jnp.float32).reshape(b, nc, chunk, h, t.shape[-1])
                      for t in (q, k, v, log_a))
    cum = jnp.cumsum(log_a, axis=2)
    causal = jnp.tril(jnp.ones((chunk, chunk), dtype=bool))
    if log_a.shape[-1] == 1:
        cs = jnp.moveaxis(cum[..., 0], 2, 3)
        diff = cs[..., :, None] - cs[..., None, :]
        decay = jnp.where(causal, jnp.exp(jnp.where(causal, diff, 0.0)), 0.0)
        scores = jnp.einsum('bcthk,bcshk->bchts', q, k) * decay
    else:
        diff = cum[:, :, :, None] - cum[:, :, None]
        m = causal[:, :, None, None]
        decay = jnp.where(m, jnp.exp(jnp.where(m, diff, 0.0)), 0.0)
        scores = jnp.einsum('bcthk,bcshk,bctshk->bchts', q, k, decay)
    o_intra = jnp.einsum('bchts,bcshv->bcthv', scores, v)
    k_end = k * jnp.exp(cum[:, :, -1:] - cum)
    chunk_states = jnp.einsum('bcshk,bcshv->bchkv', k_end, v)
    chunk_decay = jnp.exp(cum[:, :, -1])

    def carry_state(s, inp):
        a, s_c = inp
        return a[..., None] * s + s_c, s

    _, s_prev = lax.scan(carry_state, jnp.zeros((b, h, dk, dv), jnp.float32),
                         (jnp.moveaxis(chunk_decay, 1, 0), jnp.moveaxis(chunk_states, 1, 0)))
    s_prev = jnp.moveaxis(s_prev, 0, 1)
    o_inter = jnp.einsum('bcthk,bchkv->bcthv', q * jnp.exp(cum), s_prev)
    return (o_intra + o_inter).reshape(b, l, h, dv)

def token_mixer(h, w_in, conv_w, conv_b, dt_bias, a_log, d_skip, ssd_norm_g,
                lower_bound, hgrn_norm_g, w_out):
    b, l, _ = h.shape
    proj = h @ w_in
    offsets = np.cumsum(IN_WIDTHS)[:-1].tolist()
    z, xbc, dt, hq, hf, hi, hg, rq, rk, rv, rg = jnp.split(proj, offsets, axis=-1)

    def heads(t, n):
        return t.reshape(b, l, n, -1)

    xbc = jax.nn.silu(causal_depthwise_conv(xbc, conv_w, conv_b))
    xs, bm, cm = jnp.split(xbc, [SSD_WIDTH, SSD_WIDTH + SSD_GROUPS * SSD_STATE], axis=-1)
    rep = SSD_HEADS // SSD_GROUPS
    xs = heads(xs, SSD_HEADS)
    bm = jnp.repeat(heads(bm, SSD_GROUPS), rep, axis=2)
    cm = jnp.repeat(heads(cm, SSD_GROUPS), rep, axis=2)
    dt = jax.nn.softplus(dt.astype(jnp.float32) + dt_bias)
    log_a = (dt * -jnp.exp(a_log.astype(jnp.float32)))[..., None]
    y = chunked_linear_recurrence(cm, bm, xs * dt[..., None], log_a, SSD_CHUNK)
    y = y + d_skip[:, None] * xs
    y = y * jax.nn.silu(heads(z, SSD_HEADS).astype(jnp.float32))
    y_ssd = rmsnorm(y.reshape(b, l, SSD_GROUPS, -1),
                    ssd_norm_g.reshape(SSD_GROUPS, -1)).reshape(b, l, SSD_WIDTH)

    raw = hf.astype(jnp.float32)
    forget = lower_bound + (1.0 - lower_bound) * jax.nn.sigmoid(raw)
    log_f = jnp.log(jnp.maximum(forget, GATE_FLOOR))
    k_in = 1.0 - forget
    o = chunked_linear_recurrence(heads(hq, HGRN_HEADS), heads(k_in, HGRN_HEADS),
                                  heads(hi, HGRN_HEADS), heads(log_f, HGRN_HEADS), HGRN_CHUNK)
    o = rmsnorm(o, hgrn_norm_g.reshape(HGRN_HEADS, HGRN_HEAD_DIM))
    o_hgrn = (o * jax.nn.sigmoid(heads(hg, HGRN_HEADS).astype(jnp.float32))).reshape(b, l, HGRN_WIDTH)

    pos = jnp.arange(l, dtype=jnp.float32)
    q_r = rotary(heads(rq, RET_HEADS), pos)
    k_r = rotary(heads(rk, RET_HEADS), pos) * RET_HEAD_DIM ** -0.5
    log_gamma = jnp.log1p(-jnp.exp2(-5.0 - jnp.arange(RET_HEADS, dtype=jnp.float32)))
    log_g = jnp.broadcast_to(log_gamma[:, None], (b, l, RET_HEADS, 1))
    o = chunked_linear_recurrence(q_r, k_r, heads(rv, RET_HEADS), log_g, RET_CHUNK)
    o_ret = (rms(o) * jax.nn.silu(heads(rg, RET_HEADS).astype(jnp.float32))).reshape(b, l, RET_WIDTH)

    mixed = jnp.concatenate([y_ssd, o_hgrn, o_ret], axis=-1).astype(h.dtype)
    return mixed @ w_out

def hierarchical_moe(h, w_grp, b_grp, w_exp, b_exp, w_gate, w_up, w_down):
    b, l, d = h.shape
    t = h.reshape(b * l, d)
    grp_logits = (t @ w_grp + b_grp).astype(jnp.float32)
    grp_prob = jax.nn.softmax(grp_logits, axis=-1)
    g_idx = jnp.argmax(grp_logits, axis=-1)
    p_grp = jnp.max(grp_prob, axis=-1, keepdims=True)
    exp_logits = (t @ w_exp + b_exp).astype(jnp.float32).reshape(-1, N_GROUPS, EXPERTS_PER_GROUP)
    in_grp = jnp.einsum('tg,tge->te', jax.nn.one_hot(g_idx, N_GROUPS, dtype=jnp.float32), exp_logits)
    top_logit, top_idx = lax.top_k(in_grp, TOP_K)
    weights = jax.nn.softmax(top_logit, axis=-1) * p_grp
    expert_id = g_idx[:, None] * EXPERTS_PER_GROUP + top_idx
    combine = jnp.einsum('tk,tke->te', weights,
                         jax.nn.one_hot(expert_id, N_EXPERTS, dtype=jnp.float32)).astype(t.dtype)
    y = jnp.zeros_like(t)
    for gi in range(N_GROUPS):
        sl = slice(gi * EXPERTS_PER_GROUP, (gi + 1) * EXPERTS_PER_GROUP)
        hid = jax.nn.silu(jnp.einsum('td,edf->tef', t, w_gate[sl])) * jnp.einsum('td,edf->tef', t, w_up[sl])
        y = y + jnp.einsum('tef,efd->td', hid * combine[:, sl, None], w_down[sl])
    return y.reshape(b, l, d)

def second_inputs(seed: int = 0) -> dict:
    key = jax.random.key(seed)
    ks = jax.random.split(key, 24)
    f32 = jnp.float32

    def nrm(k, shape, scale):
        return scale * jax.random.normal(k, shape, f32)

    dt0 = jnp.exp(jax.random.uniform(ks[9], (DEPTH_2, SSD_HEADS), f32, math.log(DT_MIN), math.log(DT_MAX)))
    return {
        'x': nrm(ks[0], (BATCH, SEQ, D_MODEL), 1.0),
        'c': nrm(ks[1], (BATCH, D_MODEL), 1.0),
        'norm_mix_g': 1.0 + nrm(ks[2], (DEPTH_2, D_MODEL), 0.02),
        'norm_ffn_g': 1.0 + nrm(ks[3], (DEPTH_2, D_MODEL), 0.02),
        'final_norm_g': 1.0 + nrm(ks[4], (D_MODEL,), 0.02),
        'w_ada': nrm(ks[5], (DEPTH_2, D_MODEL, 6 * D_MODEL), ADA_SCALE * D_MODEL ** -0.5),
        'b_ada': nrm(ks[6], (DEPTH_2, 6 * D_MODEL), 0.02),
        'w_in': nrm(ks[7], (DEPTH_2, D_MODEL, D_IN), D_MODEL ** -0.5),
        'conv_w': nrm(ks[8], (DEPTH_2, SSD_CONV, SSD_CONV_DIM), SSD_CONV ** -0.5),
        'conv_b': nrm(ks[10], (DEPTH_2, SSD_CONV_DIM), 0.02),
        'ssd_dt_bias': dt0 + jnp.log(-jnp.expm1(-dt0)),
        'ssd_a_log': jnp.log(jax.random.uniform(ks[11], (DEPTH_2, SSD_HEADS), f32, 1.0, 16.0)),
        'ssd_d': 1.0 + nrm(ks[12], (DEPTH_2, SSD_HEADS), 0.1),
        'ssd_norm_g': 1.0 + nrm(ks[13], (DEPTH_2, SSD_WIDTH), 0.02),
        'hgrn_lower_bounds': nrm(ks[14], (DEPTH_2, HGRN_WIDTH), 0.1),
        'hgrn_norm_g': 1.0 + nrm(ks[15], (DEPTH_2, HGRN_WIDTH), 0.02),
        'w_out': nrm(ks[16], (DEPTH_2, D_MIX, D_MODEL), D_MIX ** -0.5),
        'w_grp': nrm(ks[17], (DEPTH_2, D_MODEL, N_GROUPS), D_MODEL ** -0.5),
        'b_grp': nrm(ks[18], (DEPTH_2, N_GROUPS), 0.01),
        'w_exp': nrm(ks[19], (DEPTH_2, D_MODEL, N_EXPERTS), D_MODEL ** -0.5),
        'b_exp': nrm(ks[20], (DEPTH_2, N_EXPERTS), 0.01),
        'w_gate': nrm(ks[21], (DEPTH_2, N_EXPERTS, D_MODEL, D_EXPERT), D_MODEL ** -0.5),
        'w_up': nrm(ks[22], (DEPTH_2, N_EXPERTS, D_MODEL, D_EXPERT), D_MODEL ** -0.5),
        'w_down': nrm(ks[23], (DEPTH_2, N_EXPERTS, D_EXPERT, D_MODEL), D_EXPERT ** -0.5),
    }

def second_block(x, c, norm_mix_g, norm_ffn_g, final_norm_g, w_ada, b_ada, w_in, conv_w, conv_b,
              ssd_dt_bias, ssd_a_log, ssd_d, ssd_norm_g, hgrn_lower_bounds, hgrn_norm_g, w_out,
              w_grp, b_grp, w_exp, b_exp, w_gate, w_up, w_down):
    lb_soft = jax.nn.softmax(hgrn_lower_bounds.astype(jnp.float32), axis=0)
    lower_bound = jnp.cumsum(lb_soft, axis=0) - lb_soft[0]
    c_act = jax.nn.silu(c)
    for layer in range(DEPTH_2):
        mod = c_act @ w_ada[layer] + b_ada[layer]
        sh_mix, sc_mix, g_mix, sh_ffn, sc_ffn, g_ffn = jnp.split(mod[:, None, :], 6, axis=-1)
        h = (rmsnorm(x, norm_mix_g[layer]) * (1.0 + sc_mix) + sh_mix).astype(x.dtype)
        mixed = token_mixer(h, w_in[layer], conv_w[layer], conv_b[layer], ssd_dt_bias[layer],
                            ssd_a_log[layer], ssd_d[layer], ssd_norm_g[layer], lower_bound[layer],
                            hgrn_norm_g[layer], w_out[layer])
        x = x + (g_mix * mixed).astype(x.dtype)
        h = (rmsnorm(x, norm_ffn_g[layer]) * (1.0 + sc_ffn) + sh_ffn).astype(x.dtype)
        moe = hierarchical_moe(h, w_grp[layer], b_grp[layer], w_exp[layer], b_exp[layer],
                               w_gate[layer], w_up[layer], w_down[layer])
        x = x + (g_ffn * moe).astype(x.dtype)
    return rmsnorm(x, final_norm_g).astype(x.dtype)


def setup_inputs(seed=0):
    out = dict(first_inputs(seed))
    for name, value in second_inputs(seed + 1).items():
        if name != "x":
            out[name + "_2"] = value
    return out


def reference(
    x, c, ctx, c_ctx, ada_w, ada_b, norm_g, dn_w_in, dn_conv_w, dn_a_log, dn_dt_bias, dn_norm_g,
    dn_w_out, hy_w_in, hy_conv_w, hy_conv_b, hy_f_w1, hy_f_b1, hy_f_w2, hy_f_b2, hy_f_w3,
    hy_f_b3, hy_f_w4, hy_freq, hy_skip, hy_w_out, peer_w_q, peer_keys, peer_u, peer_v, final_g,
    c_2, norm_mix_g_2, norm_ffn_g_2, final_norm_g_2, w_ada_2, b_ada_2, w_in_2, conv_w_2,
    conv_b_2, ssd_dt_bias_2, ssd_a_log_2, ssd_d_2, ssd_norm_g_2, hgrn_lower_bounds_2,
    hgrn_norm_g_2, w_out_2, w_grp_2, b_grp_2, w_exp_2, b_exp_2, w_gate_2, w_up_2, w_down_2,
):
    x = first_block(
        x, c, ctx, c_ctx, ada_w, ada_b, norm_g, dn_w_in, dn_conv_w, dn_a_log, dn_dt_bias,
        dn_norm_g, dn_w_out, hy_w_in, hy_conv_w, hy_conv_b, hy_f_w1, hy_f_b1, hy_f_w2, hy_f_b2,
        hy_f_w3, hy_f_b3, hy_f_w4, hy_freq, hy_skip, hy_w_out, peer_w_q, peer_keys, peer_u,
        peer_v, final_g,
    )
    return second_block(
        x, c_2, norm_mix_g_2, norm_ffn_g_2, final_norm_g_2, w_ada_2, b_ada_2, w_in_2, conv_w_2,
        conv_b_2, ssd_dt_bias_2, ssd_a_log_2, ssd_d_2, ssd_norm_g_2, hgrn_lower_bounds_2,
        hgrn_norm_g_2, w_out_2, w_grp_2, b_grp_2, w_exp_2, b_exp_2, w_gate_2, w_up_2, w_down_2,
    )


_drawn_inputs = setup_inputs


def setup_inputs(seed=0):
    import zlib

    import numpy as np

    out = dict(_drawn_inputs(seed))
    spreads = {}
    factors = {'norm_g': 3.61,
     'dn_norm_g': 5.266,
     'norm_mix_g_2': 3.36,
     'norm_ffn_g_2': 3.298,
     'final_norm_g_2': 2.896,
     'conv_b_2': 6.155,
     'ssd_d_2': 2.807,
     'ssd_norm_g_2': 5.566,
     'hgrn_lower_bounds_2': 6.656,
     'hgrn_norm_g_2': 8.0,
     'b_grp_2': 6.705,
     'b_exp_2': 5.292}
    for name, (base, spread) in spreads.items():
        noise = np.random.default_rng([zlib.crc32(name.encode()), seed]).standard_normal(out[name].shape)
        drawn = base * np.exp(spread * noise) if base else spread * noise
        out[name] = jnp.asarray(drawn.astype(out[name].dtype))
    for name, factor in factors.items():
        out[name] = (out[name] * factor).astype(out[name].dtype)
    return out
```

```python
from contextlib import ExitStack

import numpy as np

import concourse.bass as bass
from concourse import mybir

F32 = mybir.dt.float32
U32 = mybir.dt.uint32
ALU = mybir.AluOpType
ACT = mybir.ActivationFunctionType
AX = mybir.AxisListType.X

P = 128
T = 256
NT = T // P
D = 1024
KC = D // P
EPS = 1e-6
CW = 512
SLOT = KC * CW
NRING = 3

DN_H = 8
DN_BLOCK = 64
ROWS, ROW_W = 4, 64
DN_TAPS = 5
DN_PAD = (DN_TAPS - 1) // 2
PH, NK, TOPK = 8, 128, 16
LAYERS = 2
SSD_H, HG_H, RE_H, HD = 8, 4, 4, 64
TAPS2 = 4
GATE_FLOOR = 1e-30
NGRP, EPG, NEXP, FE = 4, 8, 32, 256
LEVELS = 7
TRI = P * 3
NEG = -3.0e38



def shape_constants():
    i = np.arange(P)
    row, col = i[:, None], i[None, :]
    parts = {}
    parts["ident"] = row == col
    parts["ones"] = np.ones((P, P))
    parts["inc_f"] = row <= col
    parts["inc_b"] = row >= col
    parts["strict_f"] = row < col
    parts["strict_b"] = row > col
    same = row // DN_BLOCK == col // DN_BLOCK
    parts["block"] = same
    parts["off"] = ~same
    lm = [row == col]
    em = []
    for lev in range(LEVELS):
        half, size = 1 << lev, 2 << lev
        blk = row // size == col // size
        left_r, right_c = row % size < half, col % size >= half
        lm.append(blk & left_r & right_c)
        right = right_c & (row % size >= half) & (row <= col)
        left = ~right_c & left_r & (row > col)
        em.append(blk & (right | left))
    em.append(row > col)
    em.append(row <= col)
    parts["lev_mask"] = np.concatenate(lm, 1)
    parts["lev_sum"] = np.concatenate(em, 1)
    half = HD // 2
    inv = (np.float32(10000.0) ** (-np.arange(half, dtype=np.float32) / np.float32(half))).astype(np.float32)
    ang = (np.arange(T, dtype=np.float32)[:, None] * inv[None, :]).astype(np.float32)
    cos, sin = np.cos(ang.astype(np.float64)).T, np.sin(ang.astype(np.float64)).T
    parts["cos"] = np.tile(cos, (4, 1))
    parts["sin"] = np.tile(np.concatenate([-sin, sin], 0), (2, 1))
    lg = np.log1p(-np.exp2(-5.0 - np.arange(RE_H)))
    dd = []
    for h in range(RE_H):
        a = np.where(row <= col, np.exp(lg[h] * np.maximum(col - row, 0)), 0.0)
        b = np.exp(lg[h] * (col + P - row))
        dd += [a, b, a]
    parts["ret_decay"] = np.concatenate(dd, 1)
    parts["iota"] = np.broadcast_to(col, (P, P))
    out, at = [], {}
    n = 0
    for k, v in parts.items():
        at[k] = (n, v.shape[1])
        n += v.shape[1]
        out.append(v.astype(np.float32))
    return np.ascontiguousarray(np.concatenate(out, 1)), at


CONST, CAT = shape_constants()


class Steps:

    def __init__(self, sem, names):
        self.sem, self.names, self.at = sem, names, {n: i + 1 for i, n in enumerate(names)}
        assert len(self.at) == len(names)
        self.n = 0

    def mark(self, ins, name):
        assert self.names[self.n] == name, (self.n, self.names[self.n], name)
        self.n += 1
        ins.then_inc(self.sem, 1)

    def wait(self, eng, name):
        eng.wait_ge(self.sem, self.at[name])


class Chain:

    def __init__(self, eng, sem):
        self.eng, self.sem, self.n = eng, sem, 0

    def __call__(self, ins):
        self.n += 1
        ins.then_inc(self.sem, 1)
        self.eng.wait_ge(self.sem, self.n)


def bc(ap, axis, n):
    v = ap.unsqueeze(axis)
    shape = list(v.shape)
    shape[axis] = n
    return v.broadcast_to(shape)


def build(nc, io):
    ctx = ExitStack()
    with ctx:
        def sb(name, shape, dt=F32):
            return ctx.enter_context(nc.sbuf_tensor(name, shape, dt))

        def sem(name):
            return ctx.enter_context(nc.semaphore(name))

        ring = sb("ring", [P, NRING * SLOT + 32768])
        RB = NRING * SLOT
        cst = sb("cst", [P, 3 * P])
        ident, ones, iota = cst[:, 0:P], cst[:, P:2 * P], cst[:, 2 * P:3 * P]
        X = sb("X", [P, NT, D])
        hT = sb("hT", [P, KC, T])
        GT = sb("GT", [P, D])
        idx = sb("idx", [P, 3, T])
        sm = sb("sm", [P, 256])
        PS = ctx.enter_context(nc.psum_tensor("PS", [P, 8, 512], F32))

        def arena(off, *shape):
            n = int(np.prod(shape))
            v = ring[:, RB + off:RB + off + n]
            if len(shape) == 1:
                return v
            names = "abcd"[:len(shape)]
            return v.rearrange(f"p ({' '.join(names)}) -> p {' '.join(names)}",
                               **{names[i]: shape[i] for i in range(1, len(shape))})

        MOD = arena(26624, 6, D)

        s_bar = sem("s_bar")
        s_ring = [sem(f"s_ring{i}") for i in range(NRING)]
        s_v, s_a, s_g = sem("s_v"), sem("s_a"), sem("s_g")
        s_out = sem("s_out")
        s_cst = sem("s_cst")
        stream = []
        free_at = []
        stages = []

        def stage(name, **progs):
            stages.append((name, progs))

        def ring_load(src):
            n = len(free_at)
            free_at.append(None)

            def load(sp):
                if n >= NRING:
                    steps, name = free_at[n - NRING]
                    steps.wait(sp, name)
                sp.dma_start(ring[:, (n % NRING) * SLOT:(n % NRING + 1) * SLOT], src).then_inc(s_ring[n % NRING], 16)
            stream.append(load)
            return n

        def ring_loads(src, count):
            first = len(free_at)
            for j in range(count):
                ring_load(src[j])
            return first

        def slot(n):
            return ring[:, (n % NRING) * SLOT:(n % NRING) * SLOT + SLOT].rearrange("p (k c) -> p k c", k=KC)

        def ring_wait(eng, n):
            eng.wait_ge(s_ring[n % NRING], 16 * (n // NRING + 1))

        def ada_stage(tag, w_slots, b_dram, c_cols, c2_cols=None, modc=None):
            first = ring_loads(w_slots, 12)
            s_in = sem(f"{tag}_in")
            rep = arena(0, 2, KC, P)
            cc = sm[:, 0:2 * KC].rearrange("p (a k) -> p a k", a=2)
            n2 = 1 if c2_cols is None else 2
            mm_names = [(who, n) for n in range(12) for who in ("c", "ctx")[:n2 if n < 4 else 1]]
            pe_s = Steps(sem(f"{tag}_pe"), mm_names)
            dv_s = Steps(sem(f"{tag}_dve"), ["rep"] + mm_names)
            ac_s = Steps(sem(f"{tag}_act"), ["silu"])
            for n in range(12):
                free_at[first + n] = (pe_s, (("c", "ctx")[n2 - 1 if n < 4 else 0], n))

            def pool(e, c):
                e.dma_start(MOD.rearrange("p a b -> p (a b)"), b_dram.unsqueeze(0).broadcast_to([P, 6 * D])).then_inc(s_in, 16)
                e.dma_start(cc[:, 0, :], c_cols).then_inc(s_in, 16)
                if n2 == 2:
                    e.dma_start(modc.rearrange("p a b -> p (a b)"), b_dram[0:2 * D].unsqueeze(0).broadcast_to([P, 2 * D])).then_inc(s_in, 16)
                    e.dma_start(cc[:, 1, :], c2_cols).then_inc(s_in, 16)
                e.wait_ge(s_in, 32 * n2)

            def act(e, c):
                e.wait_ge(s_in, 32 * n2)
                ac_s.mark(nc.scalar.activation(cc[:, 0:n2, :], cc[:, 0:n2, :], ACT.Silu), "silu")
                return ac_s

            def dve(e, c):
                ac_s.wait(e, "silu")
                dv_s.mark(nc.vector.tensor_copy(rep[:, 0:n2], bc(cc[:, 0:n2, :], 3, P)), "rep")
                for i, (who, n) in enumerate(mm_names):
                    pe_s.wait(e, (who, n))
                    dst = (MOD if who == "c" else modc)[:, n // 2, (n % 2) * CW:(n % 2) * CW + CW]
                    dv_s.mark(nc.vector.tensor_tensor(dst, dst, PS[:, i % 4, :], ALU.add), (who, n))
                dv_s.wait(e, mm_names[-1])
                for m in (1, 4):
                    c(nc.vector.tensor_scalar_add(MOD[:, m, :], MOD[:, m, :], 1.0))
                if n2 == 2:
                    c(nc.vector.tensor_scalar_add(modc[:, 1, :], modc[:, 1, :], 1.0))

            def pe(e, c):
                dv_s.wait(e, "rep")
                for i, (who, n) in enumerate(mm_names):
                    ring_wait(e, first + n)
                    if i >= 4:
                        dv_s.wait(e, mm_names[i - 4])
                    for k in range(KC):
                        ins = nc.tensor.matmul(PS[:, i % 4, :], rep[:, int(who == "ctx"), k, :],
                                               slot(first + n)[:, k, :], start=(k == 0), stop=(k == KC - 1))
                    pe_s.mark(ins, (who, n))
                return pe_s

            stage(tag, pool=pool, act=act, dve=dve, pe=pe)

        def norm_T_stage(tag, srcs, g_dram, dest, off):
            n = len(srcs)
            gb = arena(off, D)
            A = arena(off + D, 2, D)
            sq = arena(off + 3 * D, D)
            HN = arena(off + 4 * D, n, D)
            s_in = sem(f"{tag}_in")
            ac_s = Steps(sem(f"{tag}_act"), [x for t in range(n) for x in (("ss", t), ("rt", t))] +
                         [("ev", t, 1) for t in range(n)])
            dv_s = Steps(sem(f"{tag}_dve"), [("hn", t) for t in range(n)] + [("ev", t, 0) for t in range(n)])
            pe_s = Steps(sem(f"{tag}_pe"), [("tr", t, b) for t in range(n) for b in range(2)])

            def pool(e, c):
                e.dma_start(gb, g_dram.unsqueeze(0).broadcast_to([P, D])).then_inc(s_in, 16)
                e.wait_ge(s_in, 16)

            def act(e, c):
                for t in range(n):
                    if t:
                        ac_s.wait(e, ("ss", t - 1))
                    ac_s.mark(nc.scalar.activation(sq, srcs[t][0], ACT.Square, accum_out=sm[:, t:t + 1]), ("ss", t))
                    ac_s.wait(e, ("ss", t))
                    ac_s.mark(nc.scalar.activation(sm[:, 8 + t:9 + t], sm[:, t:t + 1], ACT.Sqrt,
                                                   bias=eps_col, scale=1.0 / D), ("rt", t))
                for t in range(n):
                    pe_s.wait(e, ("tr", t, 1))
                    ac_s.mark(nc.scalar.copy(dest[:, 4:8, t * P:(t + 1) * P],
                                             PS[:, (2 * t + 1) % 8, :].rearrange("p (k t) -> p k t", k=4)),
                              ("ev", t, 1))
                return ac_s

            def dve(e, c):
                e.wait_ge(s_in, 16)
                for a in range(n // NT):
                    c(nc.vector.tensor_tensor(A[:, a, :], gb, srcs[a * NT][1], ALU.mult))
                for t, (rows, sc, sh) in enumerate(srcs):
                    ac_s.wait(e, ("rt", t))
                    c(nc.vector.reciprocal(sm[:, 16 + t:17 + t], sm[:, 8 + t:9 + t]))
                    c(nc.vector.scalar_tensor_tensor(HN[:, t, :], rows, sm[:, 16 + t:17 + t],
                                                     A[:, t // NT, :], ALU.mult, ALU.mult))
                    dv_s.mark(nc.vector.tensor_tensor(HN[:, t, :], HN[:, t, :], sh, ALU.add), ("hn", t))
                for t in range(n):
                    pe_s.wait(e, ("tr", t, 0))
                    dv_s.mark(nc.vector.tensor_copy(dest[:, 0:4, t * P:(t + 1) * P],
                                                    PS[:, (2 * t) % 8, :].rearrange("p (k t) -> p k t", k=4)),
                              ("ev", t, 0))
                return dv_s

            def pe(e, c):
                for t in range(n):
                    dv_s.wait(e, ("hn", t))
                    v = HN[:, t, :].rearrange("p (c k) -> p k c", k=KC)
                    for b in range(2):
                        for k in range(4):
                            ins = nc.tensor.transpose(PS[:, (2 * t + b) % 8, k * P:(k + 1) * P], v[:, 4 * b + k, :],
                                                      ident)
                        pe_s.mark(ins, ("tr", t, b))
                return pe_s

            stage(tag, pool=pool, act=act, dve=dve, pe=pe)

        eps_col = sm[:, 255:256]

        ctxr = arena(24576 - 2 * D, NT, D)
        modc = arena(24576 - 4 * D, 2, D)
        s_x = sem("s_x")

        def pool0(sp, c):
            for n, name in enumerate(("ident", "ones", "iota")):
                sp.dma_start(cst[:, n * P:(n + 1) * P], io["const"][:, CAT[name][0]:CAT[name][0] + P]).then_inc(s_cst, 16)
            sp.dma_start(X[:], io["x"].rearrange("o (t p) d -> p (o t) d", p=P)).then_inc(s_x, 16)
            sp.dma_start(ctxr, io["ctx"].rearrange("o (t p) d -> p (o t) d", p=P)).then_inc(s_x, 16)

            sp.wait_ge(s_x, 32)
            sp.wait_ge(s_cst, 48)

        def dve0(e, c):
            c(nc.vector.memset(eps_col, EPS))
            e.wait_ge(s_x, 32)

        def wait_cst(e, c):
            e.wait_ge(s_cst, 48)

        def act0(e, c):
            e.wait_ge(s_x, 32)

        stage("start", pool=pool0, dve=dve0, pe=wait_cst, act=act0)

        ada_stage("ada_a", io["ada_w"], io["ada_b"], io["c"], io["c_ctx"], modc)
        hnT = arena(0, KC, 2 * T)
        sc_x, sh_x, sc_c, sh_c = MOD[:, 1, :], MOD[:, 0, :], modc[:, 1, :], modc[:, 0, :]
        norm_T_stage("norm_a", [(X[:, 0, :], sc_x, sh_x), (X[:, 1, :], sc_x, sh_x),
                                (ctxr[:, 0, :], sc_c, sh_c), (ctxr[:, 1, :], sc_c, sh_c)],
                     io["norm_g0"], hnT, 4096)


        def out_proj_loads(after, src):
            k = [s[0] for s in stages].index(after) + 1
            stream.append(lambda sp: sp.wait_ge(s_bar, 4 * k))
            return ring_loads(src, 2)

        def out_proj_stage(tag, rows, rT, first, gain, tmp):
            tr = [("tr", t, b) for t in range(NT) for b in range(2)]
            mmn = [("mm", s, t) for s in range(2) for t in range(NT)]
            pe_s = Steps(sem(f"{tag}_pe"), tr + mmn)
            dv_s = Steps(sem(f"{tag}_dve"), tr[0::2] + mmn)
            ac_s = Steps(sem(f"{tag}_act"), tr[1::2])
            for s in range(2):
                free_at[first + s] = (pe_s, ("mm", s, NT - 1))

            def pe(e, c):
                for i, (_, t, b) in enumerate(tr):
                    v = rows[:, t, :].rearrange("p (c k) -> p k c", k=KC)
                    for k in range(4):
                        ins = nc.tensor.transpose(PS[:, i, k * P:(k + 1) * P], v[:, 4 * b + k, :], ident)
                    pe_s.mark(ins, tr[i])
                dv_s.wait(e, tr[2])
                ac_s.wait(e, tr[3])
                for i, (_, s, t) in enumerate(mmn):
                    ring_wait(e, first + s)
                    for k in range(KC):
                        ins = nc.tensor.matmul(PS[:, 4 + i, :], rT[:, k, t * P:(t + 1) * P], slot(first + s)[:, k, :],
                                               start=(k == 0), stop=(k == KC - 1))
                    pe_s.mark(ins, mmn[i])
                return pe_s

            def evac(op, i):
                _, t, b = tr[i]
                return op(rT[:, 4 * b:4 * b + 4, t * P:(t + 1) * P], PS[:, i, :].rearrange("p (k t) -> p k t", k=4))

            def act(e, c):
                for i in (1, 3):
                    pe_s.wait(e, tr[i])
                    ac_s.mark(evac(nc.scalar.copy, i), tr[i])
                return ac_s

            def dve(e, c):
                for i in (0, 2):
                    pe_s.wait(e, tr[i])
                    dv_s.mark(evac(nc.vector.tensor_copy, i), tr[i])
                for i, (_, s, t) in enumerate(mmn):
                    pe_s.wait(e, mmn[i])
                    cols = slice(s * CW, (s + 1) * CW)
                    c(nc.vector.tensor_tensor(tmp, PS[:, 4 + i, :], gain[:, cols], ALU.mult))
                    dv_s.mark(nc.vector.tensor_tensor(X[:, t, cols], X[:, t, cols], tmp, ALU.add), mmn[i])
                    dv_s.wait(e, mmn[i])
                return dv_s

            stage(tag, pe=pe, act=act, dve=dve)

        NQ = 4
        kT = arena(10240, DN_H, 2 * T)
        qT = arena(14336, DN_H, T)
        Krow = arena(16384, NQ, DN_H, P)
        Vrow = arena(20480, NQ, DN_H, P)
        gate = arena(24576, NT, D)
        vT = arena(4096, DN_H, 2 * T)
        XPAD = ROWS * (ROW_W + 2 * DN_PAD)
        CPAD = T + 2 * DN_PAD
        zpad = arena(16384, 2, XPAD + CPAD)
        conv = arena(16384 + 2 * (XPAD + CPAD), 2, 2 * T)
        cw = arena(19000, 24, DN_TAPS)
        wba = arena(19200, KC, 32)
        first_w = ring_loads(io["dn_w"], 8)
        s_dnin = sem("s_dnin")
        ba = sm[:, 0:NQ * 32].rearrange("p (t c) -> p t c", t=NQ)
        rows_ev = [("row", s, t) for s in range(2) for t in range(NT)]
        dn1_pe = Steps(sem("dn1_pe"), [("z", n) for n in range(24)] + rows_ev + ["ba"])
        dn1_ac = Steps(sem("dn1_act"), [x for n in range(24) for x in ([("pad", n)] + ([("silu", n - 1)] if n else []))] +
                       [("silu", 23)] + rows_ev)
        dn1_dv = Steps(sem("dn1_dve"), ["zero"] + [("conv", n) for n in range(24)] + ["ba"])
        for s in range(6):
            free_at[first_w + s] = (dn1_pe, ("z", 4 * s + 3))
        for s in range(2):
            free_at[first_w + 6 + s] = (dn1_pe, ("row", s, NT - 1))

        def pool_dn1(e, c):
            e.dma_start(cw, io["dn_cw"].rearrange("p (n t) -> p n t", n=24)).then_inc(s_dnin, 16)
            e.dma_start(wba, io["dn_wba"].rearrange("p (k n) -> p k n", k=KC)).then_inc(s_dnin, 16)
            e.wait_ge(s_dnin, 32)

        def pe_dn1(e, c):
            for n in range(24):
                s = n // 4
                ring_wait(e, first_w + s)
                if n >= 4:
                    dn1_ac.wait(e, ("pad", n - 4))
                w = slot(first_w + s)
                toks = T if n < DN_H else 2 * T
                for k in range(KC):
                    ins = nc.tensor.matmul(PS[:, n % 4, 0:toks], w[:, k, (n % 4) * P:(n % 4 + 1) * P],
                                           hnT[:, k, 0:toks], start=(k == 0), stop=(k == KC - 1))
                dn1_pe.mark(ins, ("z", n))
            for s in range(2):
                ring_wait(e, first_w + 6 + s)
                for t in range(NT):
                    for k in range(KC):
                        ins = nc.tensor.matmul(PS[:, 4 + 2 * s + t, :], hnT[:, k, t * P:(t + 1) * P],
                                               slot(first_w + 6 + s)[:, k, :], start=(k == 0), stop=(k == KC - 1))
                    dn1_pe.mark(ins, ("row", s, t))
            e.wait_ge(s_dnin, 32)
            dn1_ac.wait(e, ("pad", 20))
            for t in range(NQ):
                for k in range(KC):
                    ins = nc.tensor.matmul(PS[:, 0, t * 32:(t + 1) * 32], hnT[:, k, t * P:(t + 1) * P], wba[:, k, :],
                                           start=(k == 0), stop=(k == KC - 1))
            dn1_pe.mark(ins, "ba")
            return dn1_pe

        def pad_views(buf):
            return (buf[:, 0:XPAD].rearrange("p (r w) -> p r w", r=ROWS), buf[:, XPAD:XPAD + CPAD])

        def act_dn1(e, c):
            dn1_dv.wait(e, "zero")

            def silu(n):
                dn1_dv.wait(e, ("conv", n))
                toks = T if n < DN_H else 2 * T
                dest = (qT, kT, vT)[n // DN_H]
                dn1_ac.mark(nc.scalar.activation(dest[:, n % DN_H, :], conv[:, n % 2, 0:toks], ACT.Silu), ("silu", n))
            for n in range(24):
                dn1_pe.wait(e, ("z", n))
                if n >= 2:
                    dn1_dv.wait(e, ("conv", n - 2))
                xv, cv = pad_views(zpad[:, n % 2])
                ins = nc.scalar.copy(xv[:, :, DN_PAD:DN_PAD + ROW_W],
                                     PS[:, n % 4, 0:T].rearrange("p (r w) -> p r w", r=ROWS))
                if n >= DN_H:
                    ins = nc.scalar.copy(cv[:, DN_PAD:DN_PAD + T], PS[:, n % 4, T:2 * T])
                dn1_ac.mark(ins, ("pad", n))
                if n:
                    silu(n - 1)
            silu(23)
            for s in range(2):
                for t in range(NT):
                    dn1_pe.wait(e, ("row", s, t))
                    dn1_ac.mark(nc.scalar.activation(gate[:, t, s * CW:(s + 1) * CW], PS[:, 4 + 2 * s + t, :], ACT.Silu),
                                ("row", s, t))
            return dn1_ac

        def dve_dn1(e, c):
            dn1_dv.mark(nc.vector.memset(zpad, 0.0), "zero")
            e.wait_ge(s_dnin, 32)
            for n in range(24):
                dn1_ac.wait(e, ("pad", n))
                if n >= 2:
                    dn1_ac.wait(e, ("silu", n - 2))
                xv, cv = pad_views(zpad[:, n % 2])
                xo = conv[:, n % 2, 0:T].rearrange("p (r w) -> p r w", r=ROWS)
                co = conv[:, n % 2, T:2 * T]
                pairs = [(xo, xv)] + ([(co, cv)] if n >= DN_H else [])
                for j in range(DN_TAPS):
                    for o, v in pairs:
                        src = v[:, :, j:j + ROW_W] if o is xo else v[:, j:j + T]
                        tap = cw[:, n, j:j + 1]
                        if j == 0:
                            ins = nc.vector.tensor_scalar(o, src, tap, None, ALU.mult)
                        else:
                            ins = nc.vector.scalar_tensor_tensor(o, src, tap, o, ALU.mult, ALU.add)
                        if j == DN_TAPS - 1 and o is pairs[-1][0]:
                            dn1_dv.mark(ins, ("conv", n))
                        else:
                            c(ins)
            dn1_pe.wait(e, "ba")
            dn1_dv.mark(nc.vector.tensor_copy(ba, PS[:, 0, 0:NQ * 32].rearrange("p (t c) -> p t c", t=NQ)), "ba")
            return dn1_dv

        stage("dn_proj", pool=pool_dn1, pe=pe_dn1, act=act_dn1, dve=dve_dn1)

        masks = idx.rearrange("p a t -> p (a t)")
        MASK = {n: masks[:, i * P:(i + 1) * P]
                for i, n in enumerate(("inc_f", "inc_b", "strict_f", "strict_b", "block", "off"))}
        sq = hT.rearrange("p k t -> p (k t)")[:, 0:1024].rearrange("p (a c) -> p a c", a=2)
        rn = hT.rearrange("p k t -> p (k t)")[:, 1024:2048].rearrange("p (a c) -> p a c", a=2)
        units = [(qT[:, 2 * b:2 * b + 2, :], True) for b in range(4)] + [(kT[:, h, :], False) for h in range(DN_H)]
        NU = len(units)
        dec = arena(8192, 8, NQ, 16)
        beta, g16, Gc, Gtot, eG, ekd, egl, nbeG = [dec[:, j] for j in range(8)]
        scr = arena(8192 + 512, 4, NQ, 16)
        dtb, ala = arena(8192 + 768, 16), arena(8192 + 784, 16)
        s_dn2in = sem("s_dn2in")
        trs = [(w, t, b) for w in ("k", "v") for t in range(NQ) for b in range(2)]
        dn2_pe = Steps(sem("dn2_pe"), ["G"] + [("ss", i) for i in range(NU)] + trs)
        dn2_ac = Steps(sem("dn2_act"), ["beta", "alog", "abs_e", "ln"] + [x for i in range(NU) for x in (("sq", i), ("rt", i))] +
                       ["eG", "ekd", "egl"] + trs[1::2])
        dn2_dv = Steps(sem("dn2_dve"), ["neg", "ln1", "g", "Gc"] + [("unit", i) for i in range(NU)] + ["dec"] + trs[0::2])

        def pool_dn2(e, c):
            for n, m in MASK.items():
                e.dma_start(m, io["const"][:, CAT[n][0]:CAT[n][0] + P]).then_inc(s_dn2in, 16)
            e.dma_start(dtb, io["dn_dt"].unsqueeze(0).broadcast_to([P, 16])).then_inc(s_dn2in, 16)
            e.dma_start(ala, io["dn_alog"].unsqueeze(0).broadcast_to([P, 16])).then_inc(s_dn2in, 16)
            e.wait_ge(s_dn2in, 128)

        def act_dn2(e, c):
            e.wait_ge(s_dn2in, 128)
            dn2_ac.mark(nc.scalar.activation(beta, ba[:, :, 0:16], ACT.Sigmoid), "beta")
            dn2_ac.mark(nc.scalar.activation(ala, ala, ACT.Exp), "alog")
            dn2_dv.wait(e, "neg")
            dn2_ac.mark(nc.scalar.activation(scr[:, 1], scr[:, 1], ACT.Exp), "abs_e")
            dn2_dv.wait(e, "ln1")
            dn2_ac.mark(nc.scalar.activation(scr[:, 1], scr[:, 1], ACT.Ln), "ln")
            for i, (u, _) in enumerate(units):
                if i >= 2:
                    dn2_dv.wait(e, ("unit", i - 2))
                    dn2_pe.wait(e, ("ss", i - 2))
                shape = sq[:, i % 2, :].rearrange("p (a c) -> p a c", a=2) if i < 4 else sq[:, i % 2, :]
                dn2_ac.mark(nc.scalar.activation(shape, u, ACT.Square), ("sq", i))
                dn2_pe.wait(e, ("ss", i))
                dn2_ac.mark(nc.scalar.activation(rn[:, i % 2, :], PS[:, 1 + i % 3, :], ACT.Sqrt, bias=eps_col), ("rt", i))
            dn2_dv.wait(e, "Gc")
            dn2_ac.mark(nc.scalar.activation(eG, Gc, ACT.Exp), "eG")
            dn2_ac.mark(nc.scalar.activation(ekd, ekd, ACT.Exp), "ekd")
            dn2_ac.mark(nc.scalar.activation(egl, Gtot, ACT.Exp), "egl")
            for i, (w, t, b) in list(enumerate(trs))[1::2]:
                dn2_pe.wait(e, (w, t, b))
                dst = (Krow if w == "k" else Vrow)[:, t, 4 * b:4 * b + 4, :]
                dn2_ac.mark(nc.scalar.copy(dst, PS[:, 4 + i % 4, :].rearrange("p (h d) -> p h d", h=4)), (w, t, b))
            return dn2_ac

        def dve_dn2(e, c):
            e.wait_ge(s_dn2in, 128)
            c(nc.vector.tensor_tensor(scr[:, 0], ba[:, :, 16:32], bc(dtb, 1, NQ), ALU.add))
            c(nc.vector.tensor_scalar(scr[:, 2], scr[:, 0], -1.0, None, ALU.mult))
            dn2_dv.mark(nc.vector.tensor_tensor(scr[:, 1], scr[:, 0], scr[:, 2], ALU.min), "neg")
            dn2_ac.wait(e, "abs_e")
            dn2_dv.mark(nc.vector.tensor_scalar_add(scr[:, 1], scr[:, 1], 1.0), "ln1")
            dn2_ac.wait(e, "ln")
            c(nc.vector.scalar_tensor_tensor(scr[:, 1], scr[:, 0], 0.0, scr[:, 1], ALU.max, ALU.add))
            c(nc.vector.tensor_scalar(ala, ala, -1.0, None, ALU.mult))
            dn2_dv.mark(nc.vector.tensor_tensor(g16, scr[:, 1], bc(ala, 1, NQ), ALU.mult), "g")
            dn2_pe.wait(e, "G")
            c(nc.vector.tensor_copy(Gc, PS[:, 0, 0:64].rearrange("p (t c) -> p t c", t=NQ)))
            c(nc.vector.tensor_copy(Gtot, PS[:, 0, 64:128].rearrange("p (t c) -> p t c", t=NQ)))
            dn2_dv.mark(nc.vector.tensor_tensor(ekd, Gtot, Gc, ALU.subtract), "Gc")
            for i, (u, is_q) in enumerate(units):
                dn2_ac.wait(e, ("rt", i))
                c(nc.vector.reciprocal(rn[:, i % 2, :], rn[:, i % 2, :]))
                r = rn[:, i % 2, :]
                if i < 4:
                    r = r.rearrange("p (a c) -> p a c", a=2)
                ins = nc.vector.scalar_tensor_tensor(u, u, float(P) ** -0.5 if is_q else 1.0, r, ALU.mult, ALU.mult)
                dn2_dv.mark(ins, ("unit", i))
            dn2_ac.wait(e, "eG")
            dn2_dv.mark(nc.vector.scalar_tensor_tensor(nbeG, beta, -1.0, eG, ALU.mult, ALU.mult), "dec")
            for i, (w, t, b) in list(enumerate(trs))[0::2]:
                dn2_pe.wait(e, (w, t, b))
                dst = (Krow if w == "k" else Vrow)[:, t, 4 * b:4 * b + 4, :]
                dn2_dv.mark(nc.vector.tensor_copy(dst, PS[:, 4 + i % 4, :].rearrange("p (h d) -> p h d", h=4)), (w, t, b))
            return dn2_dv

        def pe_dn2(e, c):
            dn2_dv.wait(e, "g")
            e.wait_ge(s_dn2in, 128)
            for t in range(NQ):
                for d, m in enumerate(("inc_f", "inc_b")):
                    o = t * 16 + d * 8
                    nc.tensor.matmul(PS[:, 0, o:o + 8], MASK[m], g16[:, t, d * 8:d * 8 + 8], start=True, stop=True)
                ins = nc.tensor.matmul(PS[:, 0, 64 + t * 16:80 + t * 16], ones, g16[:, t, :], start=True, stop=True)
            dn2_pe.mark(ins, "G")
            for i in range(NU):
                dn2_ac.wait(e, ("sq", i))
                if i >= 3:
                    dn2_ac.wait(e, ("rt", i - 3))
                dn2_pe.mark(nc.tensor.matmul(PS[:, 1 + i % 3, :], ones, sq[:, i % 2, :], start=True, stop=True), ("ss", i))
            dn2_dv.wait(e, ("unit", NU - 1))
            for i, (w, t, b) in enumerate(trs):
                if i >= 4:
                    (dn2_dv if i % 2 == 0 else dn2_ac).wait(e, trs[i - 4])
                src = kT if w == "k" else vT
                for h in range(4):
                    ins = nc.tensor.transpose(PS[:, 4 + i % 4, h * P:(h + 1) * P],
                                              src[:, 4 * b + h, t * P:(t + 1) * P], ident)
                dn2_pe.mark(ins, (w, t, b))
            return dn2_pe

        stage("dn_unit", pool=pool_dn2, pe=pe_dn2, act=act_dn2, dve=dve_dn2)

        HG = 4
        NAMES = ("E", "DT", "A", "Aoff", "p0", "p1", "q0", "q1", "t0", "t1", "kb", "vb", "kd", "wT", "qg", "qa")

        def four(base, i):
            return ring[:, base + i * 512:base + (i + 1) * 512].rearrange("p (h c) -> p h c", h=HG)
        buf = [{n: four(SLOT, i) for i, n in enumerate(NAMES)}, {n: four(RB, i) for i, n in enumerate(NAMES)}]
        state = ring[:, 0:2 * DN_H * P].rearrange("p (d h c) -> p d h c", d=2, h=DN_H)
        O = hT.rearrange("p k t -> p (k t)").rearrange("p (t h d) -> p t h d", t=NT, h=DN_H)
        ORDER = [[2, 3, 0, 1], [3, 2, 1, 0]]
        groups = [(st, hg) for st in range(4) for hg in range(DN_H // HG)]
        ROUNDS = 5
        pe_names, ac_names, dv_names = [], [], []
        for gi, (st, hg) in enumerate(groups):
            xt = st >= 2
            pn = ["Gr", "KK"] + (["QK"] if xt else []) + ["A", "q0"]
            for r in range(ROUNDS):
                pn += [("p", r)] + ([("q", r)] if r < ROUNDS - 1 else []) + [("t", r)]
            pn += ["Tb", "Z", "R", "wT", "vn", "ds"] + (["o"] if xt else [])
            an = ["DT"] + (["eG"] if xt else []) + ["q0"] + [("p", r) for r in range(ROUNDS)] + ["Tb", "wT"]
            dn = ["R", "E", "Araw", "A", "p0", "t0"] + (["qx"] if xt else [])
            for r in range(ROUNDS):
                dn += ([("q", r)] if r < ROUNDS - 1 else []) + [("t", r)]
            dn += ["Z", "Tinv", "vn", "s"] + (["o"] if xt else [])
            pe_names += [(gi, n) for n in pn]
            ac_names += [(gi, n) for n in an]
            dv_names += [(gi, n) for n in dn]
        dl_pe = [Steps(sem(f"dl_pe{d}"), pe_names) for d in range(2)]
        dl_ac = [Steps(sem(f"dl_act{d}"), ac_names) for d in range(2)]
        dl_dv = [Steps(sem(f"dl_dve{d}"), dv_names) for d in range(2)]
        BANK = {"Gr": 0, "KK": 1, "QK": 2, "A": 3, "q0": 1, "Tb": 1, "Z": 2, "R": 3, "wT": 1, "vn": 2, "ds": 3, "o": 0}

        def bank(d, name):
            if isinstance(name, tuple):
                b = {"p": 2, "q": 3, "t": 0}[name[0]]
            else:
                b = BANK[name]
            return PS[:, 4 * d + b, :].rearrange("p (h c) -> p h c", h=HG)

        def dl_pe_prog(e, c):
            for gi, (st, hg) in enumerate(groups):
                xt = st >= 2
                heads = [hg * HG + h for h in range(HG)]
                tile = [ORDER[d][st] for d in range(2)]

                def each(name, f, before=()):
                    for d in range(2):
                        for s, n in before:
                            s[d].wait(e, (gi, n))
                        for h in range(HG):
                            ins = f(d, h, bank(d, name)[:, h, :])
                        dl_pe[d].mark(ins, (gi, name))

                def mm(d, o, a, b_):
                    return nc.tensor.matmul(o, a, b_, start=True, stop=True)

                if gi:
                    for d in range(2):
                        last = "o" if groups[gi - 1][0] >= 2 else "s"
                        dl_dv[d].wait(e, (gi - 1, last))
                for d in range(2):
                    dl_dv[d].wait(e, (gi, "R"))
                    dl_pe[d].mark(nc.tensor.matmul(PS[:, 4 * d, :], ones, buf[d]["E"].rearrange("p h c -> p (h c)"),
                                                   start=True, stop=True), (gi, "Gr"))
                tk = [slice(t * P, (t + 1) * P) for t in tile]
                each("KK", lambda d, h, o: mm(d, o, kT[:, heads[h], tk[d]], kT[:, heads[h], tk[d]]))
                if xt:
                    each("QK", lambda d, h, o: mm(d, o, kT[:, heads[h], tk[d]], qT[:, heads[h], tk[d]]))
                each("A", lambda d, h, o: nc.tensor.transpose(o, buf[d]["wT"][:, h, :], ident), [(dl_dv, "Araw")])
                each("q0", lambda d, h, o: nc.tensor.transpose(o, buf[d]["p0"][:, h, :], ident), [(dl_dv, "p0")])
                for r in range(ROUNDS):
                    cur, new = r % 2, 1 - r % 2
                    need = [(dl_ac, "q0"), (dl_dv, "p0")] if r == 0 else [(dl_ac, ("p", r - 1)), (dl_dv, ("q", r - 1))]
                    if r == 0 and xt:
                        need.append((dl_dv, "qx"))
                    each(("p", r), lambda d, h, o: mm(d, o, buf[d][f"q{cur}"][:, h, :], buf[d][f"p{cur}"][:, h, :]), need)
                    if r < ROUNDS - 1:
                        each(("q", r), lambda d, h, o: mm(d, o, buf[d][f"p{cur}"][:, h, :], buf[d][f"q{cur}"][:, h, :]),
                             [(dl_dv, "A")] if r == 0 else [])
                    each(("t", r), lambda d, h, o: mm(d, o, buf[d][f"p{new}"][:, h, :], buf[d][f"t{cur}"][:, h, :]),
                         [(dl_ac, ("p", r)), (dl_dv, "t0" if r == 0 else ("t", r - 1))])
                tl = f"t{ROUNDS % 2}"
                each("Tb", lambda d, h, o: nc.tensor.transpose(o, buf[d][tl][:, h, :], ident), [(dl_dv, ("t", ROUNDS - 1))])
                each("Z", lambda d, h, o: mm(d, o, buf[d]["Aoff"][:, h, :], buf[d][tl][:, h, :]))
                each("R", lambda d, h, o: mm(d, o, buf[d]["q0"][:, h, :], buf[d]["q1"][:, h, :]),
                     [(dl_ac, "Tb"), (dl_dv, "Z")])
                tf = "p0"
                each("wT", lambda d, h, o: mm(d, o, buf[d]["kb"][:, h, :], buf[d][tf][:, h, :]), [(dl_dv, "Tinv")])

                def vn(d, h, o):
                    nc.tensor.matmul(o, buf[d][tf][:, h, :], buf[d]["vb"][:, h, :], start=True, stop=False)
                    return nc.tensor.matmul(o, buf[d]["wT"][:, h, :], state[:, d, heads[h], :], start=False, stop=True)
                each("vn", vn, [(dl_ac, "wT")])
                each("ds", lambda d, h, o: mm(d, o, buf[d]["kd"][:, h, :], buf[d]["A"][:, h, :]), [(dl_dv, "vn")])
                if xt:
                    def out(d, h, o):
                        nc.tensor.matmul(o, buf[d]["qg"][:, h, :], buf[d]["t0"][:, h, :], start=True, stop=False)
                        return nc.tensor.matmul(o, buf[d]["qa"][:, h, :], buf[d]["A"][:, h, :], start=False, stop=True)
                    each("o", out)
            e.wait_ge(dl_pe[0].sem, dl_pe[0].n)
            return dl_pe[1]

        def dl_act_prog(e, c):
            for gi, (st, hg) in enumerate(groups):
                xt = st >= 2
                for d in range(2):
                    dl_dv[d].wait(e, (gi, "E"))
                    dl_ac[d].mark(nc.scalar.activation(buf[d]["DT"], buf[d]["DT"], ACT.Exp), (gi, "DT"))
                    if xt:
                        dl_ac[d].mark(nc.scalar.activation(buf[d]["qg"], bank(d, "Gr"), ACT.Exp), (gi, "eG"))
                for d in range(2):
                    dl_pe[d].wait(e, (gi, "q0"))
                    dl_ac[d].mark(nc.scalar.copy(buf[d]["q0"], bank(d, "q0")), (gi, "q0"))
                for r in range(ROUNDS):
                    new = 1 - r % 2
                    for d in range(2):
                        dl_pe[d].wait(e, (gi, ("p", r)))
                        if r:
                            dl_pe[d].wait(e, (gi, ("t", r - 1)))
                        dl_ac[d].mark(nc.scalar.copy(buf[d][f"p{new}"], bank(d, ("p", r))), (gi, ("p", r)))
                for d in range(2):
                    dl_pe[d].wait(e, (gi, "Tb"))
                    dl_ac[d].mark(nc.scalar.copy(buf[d]["q0"], bank(d, "Tb")), (gi, "Tb"))
                for d in range(2):
                    dl_pe[d].wait(e, (gi, "wT"))
                    dl_ac[d].mark(nc.scalar.copy(buf[d]["wT"], bank(d, "wT")), (gi, "wT"))
            e.wait_ge(dl_ac[0].sem, dl_ac[0].n)
            return dl_ac[1]

        def dl_dve_prog(e, c):
            c(nc.vector.memset(state, 0.0))
            V = nc.vector
            for gi, (st, hg) in enumerate(groups):
                xt = st >= 2
                hs = slice(hg * HG, hg * HG + HG)
                tile = [ORDER[d][st] for d in range(2)]
                col = [slice(d * DN_H + hg * HG, d * DN_H + hg * HG + HG) for d in range(2)]
                fb = "fb"
                for d in range(2):
                    if gi and groups[gi - 1][0] >= 2:
                        dl_pe[d].wait(e, (gi - 1, "o"))
                    dl_dv[d].mark(V.tensor_tensor(buf[d]["E"], bc(MASK["inc_" + fb[d]], 1, HG),
                                                  bc(g16[:, tile[d], col[d]], 2, P), ALU.mult), (gi, "R"))
                    B = buf[d]
                    dec = lambda a: bc(a[:, tile[d], col[d]], 2, P)
                    c(V.tensor_tensor(B["kb"], Krow[:, tile[d], hs, :], dec(nbeG), ALU.mult))
                    c(V.tensor_tensor(B["vb"], Vrow[:, tile[d], hs, :], dec(beta), ALU.mult))
                    c(V.tensor_tensor(B["kd"], Krow[:, tile[d], hs, :], dec(ekd), ALU.mult))
                for d in range(2):
                    dec = lambda a: bc(a[:, tile[d], col[d]], 2, P)
                    dl_pe[d].wait(e, (gi, "Gr"))
                    c(V.tensor_tensor(buf[d]["DT"], bank(d, "Gr"), dec(Gc), ALU.subtract))
                    dl_dv[d].mark(V.tensor_scalar_min(buf[d]["DT"], buf[d]["DT"], 0.0), (gi, "E"))
                for d in range(2):
                    B = buf[d]
                    dl_ac[d].wait(e, (gi, "DT"))
                    c(V.tensor_tensor(B["DT"], B["DT"], bc(MASK["inc_" + fb[d]], 1, HG), ALU.mult))
                    dl_pe[d].wait(e, (gi, "KK"))
                    c(V.tensor_tensor(B["wT"], bank(d, "KK"), B["DT"], ALU.mult))
                    dl_dv[d].mark(V.tensor_tensor(B["wT"], B["wT"], bc(MASK["strict_" + fb[d]], 1, HG), ALU.mult),
                                  (gi, "Araw"))
                for d in range(2):
                    B = buf[d]
                    dl_pe[d].wait(e, (gi, "A"))
                    dl_dv[d].mark(V.tensor_tensor(B["A"], bank(d, "A"), bc(beta[:, tile[d], col[d]], 2, P), ALU.mult),
                                  (gi, "A"))
                    dl_dv[d].wait(e, (gi, "A"))
                    dl_dv[d].mark(V.tensor_tensor(B["p0"], B["A"], bc(MASK["block"], 1, HG), ALU.mult), (gi, "p0"))
                    c(V.tensor_tensor(B["Aoff"], B["A"], bc(MASK["off"], 1, HG), ALU.mult))
                for d in range(2):
                    dl_ac[d].wait(e, (gi, "q0"))
                    dl_dv[d].mark(V.tensor_tensor(buf[d]["t0"], bc(ident, 1, HG), buf[d]["q0"], ALU.subtract),
                                  (gi, "t0"))
                    if xt:
                        dl_ac[d].wait(e, (gi, "eG"))
                        tk = slice(tile[d] * P, tile[d] * P + P)
                        c(V.tensor_tensor(buf[d]["qg"], buf[d]["qg"], qT[:, hs, tk], ALU.mult))
                        dl_dv[d].mark(V.tensor_tensor(buf[d]["qa"], bank(d, "QK"), buf[d]["DT"], ALU.mult), (gi, "qx"))
                for r in range(ROUNDS):
                    cur, new = r % 2, 1 - r % 2
                    for d in range(2):
                        if r < ROUNDS - 1:
                            dl_pe[d].wait(e, (gi, ("q", r)))
                            dl_dv[d].mark(V.tensor_copy(buf[d][f"q{new}"], bank(d, ("q", r))), (gi, ("q", r)))
                    for d in range(2):
                        dl_pe[d].wait(e, (gi, ("t", r)))
                        dl_dv[d].mark(V.tensor_tensor(buf[d][f"t{new}"], buf[d][f"t{cur}"], bank(d, ("t", r)), ALU.add),
                                      (gi, ("t", r)))
                tl = f"t{ROUNDS % 2}"
                for d in range(2):
                    dl_pe[d].wait(e, (gi, "Z"))
                    dl_dv[d].mark(V.tensor_copy(buf[d]["q1"], bank(d, "Z")), (gi, "Z"))
                for d in range(2):
                    dl_pe[d].wait(e, (gi, "R"))
                    dl_dv[d].mark(V.tensor_tensor(buf[d]["p0"], buf[d][tl], bank(d, "R"), ALU.subtract), (gi, "Tinv"))
                    if xt:
                        c(V.tensor_copy(buf[d]["t0"], state[:, d, hs, :]))
                for d in range(2):
                    dl_pe[d].wait(e, (gi, "vn"))
                    dl_dv[d].mark(V.tensor_copy(buf[d]["A"], bank(d, "vn")), (gi, "vn"))
                    c(V.tensor_tensor(state[:, d, hs, :], state[:, d, hs, :], bc(egl[:, tile[d], col[d]], 2, P),
                                      ALU.mult))
                for d in range(2):
                    dl_pe[d].wait(e, (gi, "ds"))
                    dl_dv[d].mark(V.tensor_tensor(state[:, d, hs, :], state[:, d, hs, :], bank(d, "ds"), ALU.add),
                                  (gi, "s"))
                if xt:
                    for d in range(2):
                        dl_pe[d].wait(e, (gi, "o"))
                        o = O[:, tile[d], hs, :]
                        if st == 2:
                            ins = V.tensor_copy(o, bank(d, "o"))
                        else:
                            ins = V.tensor_tensor(o, o, bank(d, "o"), ALU.add)
                        dl_dv[d].mark(ins, (gi, "o"))
            e.wait_ge(dl_dv[0].sem, dl_dv[0].n)
            return dl_dv[1]

        stage("dn_delta", pe=dl_pe_prog, act=dl_act_prog, dve=dl_dve_prog)

        first_wo = out_proj_loads("dn_delta", io["dn_wo"])
        ngb = arena(10240, P)
        osq = arena(10240 + P, 2, DN_H, P)
        s_ng = sem("s_ng")
        dno_dv = Steps(sem("dno_dve"), ["ss"] + ["y"])
        dno_ac = Steps(sem("dno_act"), ["rt"])

        def pool_dno(e, c):
            e.dma_start(ngb, io["dn_ng"].unsqueeze(0).broadcast_to([P, P])).then_inc(s_ng, 16)
            e.wait_ge(s_ng, 16)

        def dve_dno(e, c):
            V = nc.vector
            c(V.tensor_tensor(osq, O, O, ALU.mult))
            ss = sm[:, 128:144].rearrange("p (t h) -> p t h", t=NT)
            dno_dv.mark(V.tensor_reduce(ss, osq, AX, ALU.add), "ss")
            e.wait_ge(s_ng, 16)
            g4 = gate.rearrange("p t (h d) -> p (t h) d", h=DN_H)
            c(V.tensor_tensor(g4, g4, bc(ngb, 1, NT * DN_H), ALU.mult))
            dno_ac.wait(e, "rt")
            c(V.reciprocal(sm[:, 128:144], sm[:, 128:144]))
            o16 = O.rearrange("p t h d -> p (t h) d")
            c(V.tensor_tensor(o16, o16, bc(sm[:, 128:144], 2, P), ALU.mult))
            dno_dv.mark(V.tensor_tensor(g4, o16, g4, ALU.mult), "y")
            return dno_dv

        def act_dno(e, c):
            dno_dv.wait(e, "ss")
            dno_ac.mark(nc.scalar.activation(sm[:, 128:144], sm[:, 128:144], ACT.Sqrt, bias=eps_col, scale=1.0 / P), "rt")
            return dno_ac

        stage("dn_gate", pool=pool_dno, dve=dve_dno, act=act_dno)
        out_proj_stage("dn_out", gate, arena(16384, KC, T), first_wo, MOD[:, 2, :], arena(12800, CW))

        first_q = ring_loads(io["peer_wq"], 4)
        norm_T_stage("norm_b", [(X[:, t, :], MOD[:, 4, :], MOD[:, 3, :]) for t in range(NT)], io["norm_g1"], hT, 12288)
        NPH = 2 * PH
        QT = arena(0, NPH, T)
        keysT = arena(4096, NPH, NK)
        S = arena(6144, NT, NPH, NK)
        V1 = arena(10240, NT, NPH, TOPK)
        U1 = arena(10752, NT, NPH, TOPK)
        U1f = arena(11264, NT, NPH, TOPK)
        cand = arena(11776, PH, TOPK, TOPK)
        eqs = arena(13824, PH, TOPK, TOPK)
        TS = arena(15872, NT, PH, TOPK)
        pos = arena(16128, NT, PH, TOPK)
        part = arena(16384, 2, NT, PH, TOPK)
        partf = arena(16896, 2, NT, PH, TOPK)
        sel = arena(17408, 3, NT, PH * TOPK)
        s_pk = sem("s_pk")
        sq_names = [("q", n) for n in range(NPH)]
        ss_names = [("s", t, b) for t in range(NT) for b in range(4)]
        tr_names = [("tr", a) for a in range(3)]
        pq_pe = Steps(sem("pq_pe"), sq_names + ss_names + tr_names)
        pq_ac = Steps(sem("pq_act"), ["gt"] + sq_names + ss_names + ["exp"])
        pq_dv = Steps(sem("pq_dve"), ["max", "sel"] + tr_names)
        for s in range(4):
            free_at[first_q + s] = (pq_pe, ("q", 4 * s + 3))

        def pool_pq(e, c):
            e.dma_start(keysT, io["peer_kT"].rearrange("p (n k) -> p n k", n=NPH)).then_inc(s_pk, 16)
            e.wait_ge(s_pk, 16)

        def pe_pq(e, c):
            for n in range(NPH):
                ring_wait(e, first_q + n // 4)
                if n >= 4:
                    pq_ac.wait(e, ("q", n - 4))
                for k in range(KC):
                    ins = nc.tensor.matmul(PS[:, n % 4, 0:T], slot(first_q + n // 4)[:, k, (n % 4) * P:(n % 4 + 1) * P],
                                           hT[:, k, :], start=(k == 0), stop=(k == KC - 1))
                pq_pe.mark(ins, ("q", n))
            e.wait_ge(s_pk, 16)
            for i, (_, t, b) in enumerate(ss_names):
                pq_ac.wait(e, ("q", NPH - 1) if i < 4 else ss_names[i - 4])
                for n in range(4):
                    ins = nc.tensor.matmul(PS[:, 4 + i % 4, n * NK:(n + 1) * NK], QT[:, 4 * b + n, t * P:(t + 1) * P],
                                           keysT[:, 4 * b + n, :], start=True, stop=True)
                pq_pe.mark(ins, ss_names[i])
            pq_dv.wait(e, "sel")
            for a in range(3):
                for t in range(NT):
                    ins = nc.tensor.transpose(PS[:, a, t * P:(t + 1) * P], sel[:, a, t, :], ident)
                pq_pe.mark(ins, ("tr", a))
            return pq_pe

        def act_pq(e, c):
            pq_ac.mark(nc.scalar.copy(GT[:], MOD[:, 5, :]), "gt")
            for n in range(NPH):
                pq_pe.wait(e, ("q", n))
                pq_ac.mark(nc.scalar.copy(QT[:, n, :], PS[:, n % 4, 0:T]), ("q", n))
            for i, (_, t, b) in enumerate(ss_names):
                pq_pe.wait(e, ss_names[i])
                pq_ac.mark(nc.scalar.copy(S[:, t, 4 * b:4 * b + 4, :],
                                          PS[:, 4 + i % 4, :].rearrange("p (n k) -> p n k", n=4)), ss_names[i])
            pq_dv.wait(e, "max")
            pq_ac.mark(nc.scalar.activation(sel[:, 2], sel[:, 2], ACT.Exp), "exp")
            return pq_ac

        def dve_pq(e, c):
            V = nc.vector

            def top16(srcs, vals, ids):
                for lo in (0, 8):
                    for s, v in zip(srcs, vals):
                        ins = V.max(v[:, lo:lo + 8], s)
                    c(ins)
                    for s, v, u in zip(srcs, vals, ids):
                        ins = V.max_index(u[:, lo:lo + 8], v[:, lo:lo + 8], s)
                    c(ins)
                    if lo == 0:
                        for s, v in zip(srcs, vals):
                            ins = V.match_replace(s, v[:, 0:8], s, NEG)
                        c(ins)
            Uu = U1.bitcast(U32)
            for t in range(NT):
                pq_ac.wait(e, ("s", t, 3))
                top16([S[:, t, n, :] for n in range(NPH)], [V1[:, t, n, :] for n in range(NPH)],
                      [Uu[:, t, n, :] for n in range(NPH)])
            c(V.tensor_copy(U1f, Uu))
            posu, partu = pos.bitcast(U32), part.bitcast(U32)
            V1h = V1.rearrange("p t (h a) k -> p t h a k", a=2)
            U1h = U1f.rearrange("p t (h a) k -> p t h a k", a=2)
            for t in range(NT):
                c(V.tensor_tensor(cand, bc(V1h[:, t, :, 0, :], 3, TOPK), bc(V1h[:, t, :, 1, :], 2, TOPK), ALU.add))
                flat = cand.rearrange("p h a b -> p h (a b)")
                top16([flat[:, h, :] for h in range(PH)], [TS[:, t, h, :] for h in range(PH)],
                      [posu[:, t, h, :] for h in range(PH)])
            c(V.tensor_scalar(partu[:, 0], posu, 4, None, ALU.logical_shift_right))
            c(V.tensor_scalar(partu[:, 1], posu, TOPK - 1, None, ALU.bitwise_and))
            c(V.tensor_copy(partf, partu))
            g = sel[:, 2].rearrange("p t (h k) -> p t h k", h=PH)
            for t in range(NT):
                ins = V.tensor_tensor(g[:, t], TS[:, t], TS[:, t, :, 0:1].broadcast_to([P, PH, TOPK]), ALU.subtract)
            pq_dv.mark(ins, "max")
            for t in range(NT):
                for a in range(2):
                    c(V.tensor_tensor(eqs, bc(partf[:, a, t], 3, TOPK),
                                      iota[:, 0:TOPK].unsqueeze(1).unsqueeze(1).broadcast_to([P, PH, TOPK, TOPK]),
                                      ALU.is_equal))
                    c(V.tensor_tensor(eqs, eqs, bc(U1h[:, t, :, a, :], 2, TOPK), ALU.mult))
                    c(V.tensor_reduce(sel[:, a, t, :].rearrange("p (h k) -> p h k", h=PH), eqs, AX, ALU.add))
            pq_ac.wait(e, "exp")
            g16v = sel[:, 2].rearrange("p t (h k) -> p (t h) k", h=PH)
            c(V.tensor_reduce(sm[:, 144:160], g16v, AX, ALU.add))
            c(V.reciprocal(sm[:, 144:160], sm[:, 144:160]))
            pq_dv.mark(V.tensor_tensor(g16v, g16v, bc(sm[:, 144:160], 2, TOPK), ALU.mult), "sel")
            for a in range(3):
                pq_pe.wait(e, ("tr", a))
                pq_dv.mark(V.tensor_copy(idx[:, a, :], PS[:, a, 0:T]), ("tr", a))
            return pq_dv

        stage("peer_route", pool=pool_pq, pe=pe_pq, act=act_pq, dve=dve_pq)

        G = arena(0, NK, T)
        GQ = 4
        hotA = ring[:, 8192:8192 + 1024].rearrange("p (b q k) -> p b q k", b=2, q=GQ)
        hotB = ring[:, 9216:9216 + 1024].rearrange("p (b q k) -> p b q k", b=2, q=GQ)
        s_hot, s_gmm, s_gev = sem("s_hot"), sem("s_gmm"), sem("s_gev")
        NG2 = T // GQ // 2

        def groups_loop(e, body):
            for b in range(2):
                body(b, b, True)
            with e.Fori(1, NG2) as i:
                for b in range(2):
                    body(i * 2 + b, b, False)

        def dve_g(e, c):
            def body(n, b, first):
                if not first:
                    e.wait_ge(s_gmm, n - 1)
                nc.vector.tensor_tensor(hotA[:, b], bc(iota, 1, GQ), bc(idx[:, 0, bass.ds(n * GQ, GQ)], 2, P),
                                        ALU.is_equal)
                for q in range(GQ):
                    t = n * GQ + q
                    ins = nc.vector.tensor_scalar(hotB[:, b, q, :], iota, idx[:, 1, bass.ds(t, 1)],
                                                  idx[:, 2, bass.ds(t, 1)], ALU.is_equal, ALU.mult)
                ins.then_inc(s_hot, 1)
            groups_loop(e, body)
            e.wait_ge(s_hot, 2 * NG2)

        def pe_g(e, c):
            def body(n, b, first):
                e.wait_ge(s_hot, n + 1)
                if not first:
                    e.wait_ge(s_gev, n - 1)
                for q in range(GQ):
                    ins = nc.tensor.matmul(PS[:, b, q * NK:(q + 1) * NK], hotA[:, b, q, :], hotB[:, b, q, :],
                                           start=True, stop=True)
                ins.then_inc(s_gmm, 1)
            groups_loop(e, body)
            e.wait_ge(s_gmm, 2 * NG2)

        def act_g(e, c):
            def body(n, b, first):
                e.wait_ge(s_gmm, n + 1)
                nc.scalar.copy(G[:, :, bass.ds(n * GQ, GQ)].rearrange("p j q -> p q j"),
                               PS[:, b, :].rearrange("p (q j) -> p q j", q=GQ)).then_inc(s_gev, 1)
            groups_loop(e, body)
            e.wait_ge(s_gev, 2 * NG2)

        stage("peer_weights", dve=dve_g, pe=pe_g, act=act_g)

        NSL = 4
        pu = [ring[:, q * 2048:q * 2048 + 1024].rearrange("p (k e) -> p k e", k=KC) for q in range(NSL)]
        pv = [ring[:, q * 2048 + 1024:q * 2048 + 2048] for q in range(NSL)]
        act_h = ring[:, 8192:8192 + 512].rearrange("p (b t) -> p b t", b=2)
        coef = ring[:, 9216:9216 + 512].rearrange("p (b t) -> p b t", b=2)
        zero = ring[:, 10240:10240 + 512]
        p_ld = [sem(f"p_ld{q}") for q in range(NSL)]
        s_hid, s_gelu, s_coef, s_y = sem("s_hid"), sem("s_gelu"), sem("s_coef"), sem("s_y")
        s_zero = sem("s_zero")

        def load_peer(sp):
            for n in range(first_q + 1, first_q + 4):
                free_at[n][0].wait(sp, free_at[n][1])

            def body(j, q, first):
                if not first:
                    sp.wait_ge(s_y, j - NSL + 1)
                sp.dma_start(ring[:, q * 2048:q * 2048 + 1024], io["peer_u"][j]).then_inc(p_ld[q], 16)
                sp.dma_start(pv[q], io["peer_v"][:, j, :]).then_inc(p_ld[q], 16)
            for q in range(NSL):
                body(q, q, True)
            with sp.Fori(1, NK // NSL) as i:
                for q in range(NSL):
                    body(i * NSL + q, q, False)
        stream.append(load_peer)

        def pe_x(e, c):
            e.wait_ge(s_zero, 1)
            for b in range(4):
                nc.tensor.matmul(PS[:, 4 + b, :], zero[:, 0:P], zero, start=True, stop=False)

            def hid(j, q, turn, first=False):
                e.wait_ge(p_ld[q], turn * 32 + 32)
                if not first:
                    e.wait_ge(s_gelu, j - 1)
                for k in range(KC):
                    ins = nc.tensor.matmul(PS[:, q % 2, 0:T], pu[q][:, k, :], hT[:, k, :],
                                           start=(k == 0), stop=(k == KC - 1))
                ins.then_inc(s_hid, 1)

            def y(j, q, last=False):
                e.wait_ge(s_coef, j + 1)
                for t in range(NT):
                    for h in range(2):
                        ins = nc.tensor.matmul(PS[:, 4 + 2 * t + h, :], coef[:, q % 2, t * P:(t + 1) * P],
                                               pv[q][:, h * CW:(h + 1) * CW], start=False, stop=last)
                ins.then_inc(s_y, 1)
            hid(0, 0, 0, True)
            for q in range(NSL):
                hid(q + 1, (q + 1) % NSL, (q + 1) // NSL, q == 0)
                y(q, q)
            with e.Fori(1, NK // NSL - 1) as i:
                for q in range(NSL):
                    hid(i * NSL + q + 1, (q + 1) % NSL, i + (q + 1) // NSL)
                    y(i * NSL + q, q)
            for j in range(NK - NSL, NK):
                if j < NK - 1:
                    hid(j + 1, (j + 1) % NSL, (j + 1) // NSL)
                y(j, j % NSL, j == NK - 1)
            e.wait_ge(s_y, NK)

        def tiles_loop(e, body):
            for q in range(NSL):
                body(q, q, q < 2)
            with e.Fori(1, NK // NSL) as i:
                for q in range(NSL):
                    body(i * NSL + q, q, False)

        def act_x(e, c):
            def body(j, q, first):
                e.wait_ge(s_hid, j + 1)
                if not first:
                    e.wait_ge(s_coef, j - 1)
                nc.scalar.activation(act_h[:, q % 2, :], PS[:, q % 2, 0:T], ACT.Gelu).then_inc(s_gelu, 1)
            tiles_loop(e, body)
            e.wait_ge(s_gelu, NK)

        def dve_x(e, c):
            nc.vector.memset(zero, 0.0).then_inc(s_zero, 1)

            def body(j, q, first):
                e.wait_ge(s_gelu, j + 1)
                if not first:
                    e.wait_ge(s_y, j - 1)
                nc.vector.tensor_tensor(coef[:, q % 2, :], act_h[:, q % 2, :],
                                        G[:, bass.ds(j, 1), :].rearrange("p a t -> p (a t)"),
                                        ALU.mult).then_inc(s_coef, 1)
            tiles_loop(e, body)
            e.wait_ge(s_coef, NK)

        stage("peer_experts", pe=pe_x, act=act_x, dve=dve_x)

        def add_norm_stage(tag, gain, g_dram, off):
            tmp, gb, sq2 = arena(off, 2, CW), arena(off + D, D), arena(off + 2 * D, D)
            s_in = sem(f"{tag}_in")
            dv_s = Steps(sem(f"{tag}_dve"), [("add", t) for t in range(NT)] +
                         ([("n", t) for t in range(NT)] if g_dram is not None else []))
            ac_s = Steps(sem(f"{tag}_act"), [x for t in range(NT) for x in (("ss", t), ("rt", t))])

            def dve(e, c):
                for t in range(NT):
                    for h in range(2):
                        cols = slice(h * CW, (h + 1) * CW)
                        c(nc.vector.tensor_tensor(tmp[:, h, :], PS[:, 4 + 2 * t + h, :], gain[:, cols], ALU.mult))
                        ins = nc.vector.tensor_tensor(X[:, t, cols], X[:, t, cols], tmp[:, h, :], ALU.add)
                        if h == 0:
                            c(ins)
                    dv_s.mark(ins, ("add", t))
                if g_dram is None:
                    return dv_s
                e.wait_ge(s_in, 16)
                for t in range(NT):
                    ac_s.wait(e, ("rt", t))
                    c(nc.vector.reciprocal(sm[:, 16 + t:17 + t], sm[:, 8 + t:9 + t]))
                    dv_s.mark(nc.vector.scalar_tensor_tensor(X[:, t, :], X[:, t, :], sm[:, 16 + t:17 + t], gb,
                                                             ALU.mult, ALU.mult), ("n", t))
                return dv_s

            def act(e, c):
                for t in range(NT):
                    dv_s.wait(e, ("add", t))
                    if t:
                        ac_s.wait(e, ("ss", t - 1))
                    ac_s.mark(nc.scalar.activation(sq2, X[:, t, :], ACT.Square, accum_out=sm[:, t:t + 1]), ("ss", t))
                    ac_s.wait(e, ("ss", t))
                    ac_s.mark(nc.scalar.activation(sm[:, 8 + t:9 + t], sm[:, t:t + 1], ACT.Sqrt, bias=eps_col,
                                                   scale=1.0 / D), ("rt", t))
                return ac_s

            def pool(e, c):
                e.dma_start(gb, g_dram.unsqueeze(0).broadcast_to([P, D])).then_inc(s_in, 16)
                e.wait_ge(s_in, 16)
            if g_dram is None:
                stage(tag, dve=dve)
            else:
                stage(tag, dve=dve, act=act, pool=pool)

        add_norm_stage("peer_out", GT, io["final_g"], 0)

        NSEG = 3
        SEG = ((0, 0), (0, 1), (1, 1))

        def release_ring(after):
            k = [s[0] for s in stages].index(after) + 1
            stream.append(lambda sp: sp.wait_ge(s_bar, 4 * k))

        for layer in range(LAYERS):
            L = f"l{layer}_"
            release_ring("peer_experts" if layer == 0 else "l0_experts")
            ada_stage(L + "ada", io[f"ada_w{layer}"], io[f"ada_b{layer}"], io["c2"])
            first_in = ring_loads(io[f"w_in{layer}"], 8)
            norm_T_stage(L + "norm_mix", [(X[:, t, :], MOD[:, 1, :], MOD[:, 0, :]) for t in range(NT)],
                         io[f"ng_mix{layer}"], hT, 12288)

            mcn = ("lev_mask", "lev_sum", "cos", "sin", "ret_decay", "inc_f")
            mc_at, off = {}, 0
            for n in mcn:
                mc_at[n] = off
                off += CAT[n][1]
            lev_mask = arena(mc_at["lev_mask"], LEVELS + 1, P)
            lev_sum = arena(mc_at["lev_sum"], LEVELS + 2, P)
            cos, sin = arena(mc_at["cos"], T), arena(mc_at["sin"], T)
            ret_decay = arena(mc_at["ret_decay"], RE_H, NSEG, P)
            inc = arena(mc_at["inc_f"], P)
            XBCp, XBC = arena(4352, 6, TAPS2 - 1 + T), arena(5920, 6, T)
            hqT, kinT = arena(7456, 2, T), arena(7968, 2, T)
            RT, rot = arena(8480, 8, T), arena(10528, 4, T)
            zrow, logf, hi = arena(11552, NT, 512), arena(12576, NT, T), arena(13088, NT, T)
            hg, rv, rg = arena(13600, NT, T), arena(14112, NT, T), arena(14624, NT, T)
            dtr, g8, Gc8 = arena(15136, NT, 8), arena(15152, NT, 8), arena(15168, NT, 8)
            spar, sscr = arena(15200, 3, 8), arena(15224, 3, NT, 8)
            ngs, lb, oml, ngh = arena(15400, 512), arena(15912, T + 2), arena(16170, T + 2), arena(16432, T)
            cw2, wdt = arena(16690, 6, TAPS2 + 1), arena(16724, KC, 8)
            xs, xdt = arena(16820, NT, 512), arena(17844, NT, 512)
            WS = arena(18868, SSD_H, NSEG, P)
            EX = arena(21940, 4, LEVELS + 1, P)
            Rg = arena(21940, SSD_H, NSEG, P)
            mtmp = arena(26036, HG_H, P)
            WH, WR = arena(8480, HG_H, NSEG, P), arena(4352, RE_H, NSEG, P)
            lbr = arena(18868, 2, T + 2)
            lbs2 = arena(18868 + 2 * (T + 2), T + 2)
            MIX = hT.rearrange("p k t -> p (k t)").rearrange("p (t d) -> p t d", t=NT)

            def proj(L=L, layer=layer, first_in=first_in):
                s_in = sem(L + "proj_in")
                pairs = [("T", i) for i in range(9)]
                rows = [("r", j, t) for j in range(4) for t in range(NT)]
                pe_s = Steps(sem(L + "proj_pe"), pairs + rows + ["dt"])
                ac_s = Steps(sem(L + "proj_act"), ["lbe", "alog"] + pairs + rows + ["conv", "dte", "ln", "logf"])
                dv_s = Steps(sem(L + "proj_dve"), ["lb0", "lb", "conv", "dt0", "dt1", "logf0", "done"])
                for s in range(4):
                    free_at[first_in + s] = (pe_s, ("T", 2 * s + 1))
                for s in range(4):
                    free_at[first_in + 4 + s] = (pe_s, ("r", s, NT - 1))

                def pool(e, c):
                    n = 0

                    def load(dst, src):
                        e.dma_start(dst, src).then_inc(s_in, 16)
                        return 1

                    def row(a, k):
                        return a.unsqueeze(0).broadcast_to([P, k])
                    n += load(lbr[:, :, 0:T], io["lbs"].unsqueeze(0).broadcast_to([P, 2, T]))
                    n += load(lbr[:, :, T:T + 2], io["lbsT"].rearrange("p (a b) -> p a b", a=2))
                    n += load(cw2, io[f"conv{layer}"].rearrange("p (a b) -> p a b", a=6))
                    n += load(wdt, io[f"w_dt{layer}"].rearrange("p (a b) -> p a b", a=KC))
                    n += load(spar.rearrange("p a b -> p (a b)"), row(io[f"ssd{layer}"], 24))
                    n += load(ngs, row(io[f"ng_ssd{layer}"], 512))
                    n += load(ngh, row(io[f"ng_hgrn{layer}"], T))
                    for m in mcn:
                        n += load(arena(mc_at[m], CAT[m][1]), io["const"][:, CAT[m][0]:CAT[m][0] + CAT[m][1]])
                    assert n == 13
                    e.wait_ge(s_in, 16 * n)

                def pe(e, c):
                    for i in range(9):
                        s = i // 2
                        ring_wait(e, first_in + s)
                        if i >= 4:
                            ac_s.wait(e, ("T", i - 4))
                        for a in range(2):
                            ct = (2 * i + a) % 4
                            for k in range(KC):
                                ins = nc.tensor.matmul(PS[:, i % 4, a * T:(a + 1) * T],
                                                       slot(first_in + s)[:, k, ct * P:(ct + 1) * P], hT[:, k, :],
                                                       start=(k == 0), stop=(k == KC - 1))
                        pe_s.mark(ins, ("T", i))
                    for u, (_, j, t) in enumerate(rows):
                        ring_wait(e, first_in + 4 + j)
                        if u >= 4:
                            ac_s.wait(e, rows[u - 4])
                        lo = T if j == 0 else 0
                        for k in range(KC):
                            ins = nc.tensor.matmul(PS[:, 4 + u % 4, lo:CW], hT[:, k, t * P:(t + 1) * P],
                                                   slot(first_in + 4 + j)[:, k, lo:CW], start=(k == 0), stop=(k == KC - 1))
                        pe_s.mark(ins, rows[u])
                    e.wait_ge(s_in, 16 * 13)
                    ac_s.wait(e, ("T", 8))
                    for t in range(NT):
                        for k in range(KC):
                            ins = nc.tensor.matmul(PS[:, 0, t * 8:t * 8 + 8], hT[:, k, t * P:(t + 1) * P], wdt[:, k, :],
                                                   start=(k == 0), stop=(k == KC - 1))
                    pe_s.mark(ins, "dt")
                    return pe_s

                def act(e, c):
                    A = nc.scalar
                    dv_s.wait(e, "lb0")
                    ac_s.mark(A.activation(lbr, lbr, ACT.Exp), "lbe")
                    ac_s.mark(A.activation(spar[:, 1], spar[:, 1], ACT.Exp), "alog")
                    for i in range(9):
                        pe_s.wait(e, ("T", i))
                        src = PS[:, i % 4, :].rearrange("p (a t) -> p a t", a=2)
                        if i < 3:
                            ins = A.copy(XBCp[:, 2 * i:2 * i + 2, TAPS2 - 1:], src)
                        elif i == 3:
                            ins = A.copy(hqT, src)
                        elif i == 4:
                            ins = A.activation(kinT, src, ACT.Sigmoid)
                        else:
                            ins = A.copy(RT[:, 2 * i - 10:2 * i - 8, :], src)
                        ac_s.mark(ins, ("T", i))
                    for u, (_, j, t) in enumerate(rows):
                        pe_s.wait(e, rows[u])
                        b = PS[:, 4 + u % 4, :]
                        if j == 0:
                            ins = A.activation(logf[:, t, :], b[:, T:CW], ACT.Sigmoid)
                        elif j == 1:
                            ins = A.activation(zrow[:, t, :], b, ACT.Silu)
                        elif j == 2:
                            A.copy(hi[:, t, :], b[:, 0:T])
                            ins = A.activation(hg[:, t, :], b[:, T:CW], ACT.Sigmoid)
                        else:
                            A.copy(rv[:, t, :], b[:, 0:T])
                            ins = A.activation(rg[:, t, :], b[:, T:CW], ACT.Silu)
                        ac_s.mark(ins, rows[u])
                    dv_s.wait(e, "conv")
                    ac_s.mark(A.activation(XBC, XBC, ACT.Silu), "conv")
                    dv_s.wait(e, "dt0")
                    ac_s.mark(A.activation(sscr[:, 1], sscr[:, 1], ACT.Exp), "dte")
                    dv_s.wait(e, "dt1")
                    ac_s.mark(A.activation(sscr[:, 1], sscr[:, 1], ACT.Ln), "ln")
                    dv_s.wait(e, "logf0")
                    ac_s.mark(A.activation(logf, logf, ACT.Ln), "logf")
                    return ac_s

                def dve(e, c):
                    V = nc.vector
                    c(V.memset(XBCp[:, :, 0:TAPS2 - 1], 0.0))
                    e.wait_ge(s_in, 16 * 13)
                    c(V.tensor_tensor(lbs2, lbr[:, 0], lbr[:, 1], ALU.max))
                    dv_s.mark(V.tensor_tensor(lbr, lbr, bc(lbs2, 1, 2), ALU.subtract), "lb0")
                    ac_s.wait(e, "lbe")
                    c(V.tensor_tensor(lbs2, lbr[:, 0], lbr[:, 1], ALU.add))
                    c(V.reciprocal(lbs2, lbs2))
                    c(V.tensor_tensor(lbr, lbr, bc(lbs2, 1, 2), ALU.mult))
                    if layer == 0:
                        c(V.tensor_tensor(lb, lbr[:, 0], lbr[:, 0], ALU.subtract))
                    else:
                        c(V.tensor_tensor(lb, lbr[:, 0], lbr[:, 1], ALU.add))
                        c(V.tensor_tensor(lb, lb, lbr[:, 0], ALU.subtract))
                    dv_s.mark(V.tensor_scalar(oml, lb, -1.0, 1.0, ALU.mult, ALU.add), "lb")
                    dv_s.wait(e, "lb")
                    ac_s.wait(e, ("T", 2))
                    for n in range(6):
                        for j in range(TAPS2):
                            if j == 0:
                                ins = V.tensor_scalar(XBC[:, n, :], XBCp[:, n, 0:T], cw2[:, n, 0:1],
                                                      cw2[:, n, TAPS2:TAPS2 + 1], ALU.mult, ALU.add)
                            else:
                                ins = V.scalar_tensor_tensor(XBC[:, n, :], XBCp[:, n, j:j + T], cw2[:, n, j:j + 1],
                                                             XBC[:, n, :], ALU.mult, ALU.add)
                            if (n, j) == (5, TAPS2 - 1):
                                dv_s.mark(ins, "conv")
                            else:
                                c(ins)
                    ac_s.wait(e, ("T", 4))
                    for a in range(2):
                        c(V.tensor_scalar(kinT[:, a, :], kinT[:, a, :], oml[:, T + a:T + a + 1], lb[:, T + a:T + a + 1],
                                          ALU.mult, ALU.add))
                    c(V.tensor_scalar(kinT, kinT, -1.0, 1.0, ALU.mult, ALU.add))
                    ac_s.wait(e, ("T", 8))
                    c(V.tensor_tensor(rot, RT[:, 0:4, :], bc(cos, 1, 4), ALU.mult))
                    c(V.tensor_tensor(RT[:, 4:8, :], RT[:, 4:8, :], bc(sin, 1, 4), ALU.mult))
                    c(V.tensor_tensor(rot, rot, RT[:, 4:8, :], ALU.add))
                    c(V.tensor_scalar(rot[:, 2:4, :], rot[:, 2:4, :], float(HD) ** -0.5, None, ALU.mult))
                    pe_s.wait(e, "dt")
                    c(V.tensor_tensor(sscr[:, 0], PS[:, 0, 0:16].rearrange("p (t h) -> p t h", t=NT),
                                      bc(spar[:, 0], 1, NT), ALU.add))
                    c(V.tensor_scalar(sscr[:, 2], sscr[:, 0], -1.0, None, ALU.mult))
                    dv_s.mark(V.tensor_tensor(sscr[:, 1], sscr[:, 0], sscr[:, 2], ALU.min), "dt0")
                    ac_s.wait(e, "dte")
                    dv_s.mark(V.tensor_scalar_add(sscr[:, 1], sscr[:, 1], 1.0), "dt1")
                    ac_s.wait(e, ("r", 0, NT - 1))
                    c(V.tensor_tensor(logf, logf, bc(oml[:, 0:T], 1, NT), ALU.mult))
                    c(V.tensor_tensor(logf, logf, bc(lb[:, 0:T], 1, NT), ALU.add))
                    dv_s.mark(V.tensor_scalar_max(logf, logf, GATE_FLOOR), "logf0")
                    ac_s.wait(e, "ln")
                    c(V.scalar_tensor_tensor(dtr, sscr[:, 0], 0.0, sscr[:, 1], ALU.max, ALU.add))
                    c(V.tensor_scalar(spar[:, 1], spar[:, 1], -1.0, None, ALU.mult))
                    dv_s.mark(V.tensor_tensor(g8, dtr, bc(spar[:, 1], 1, NT), ALU.mult), "done")
                    return dv_s

                stage(L + "proj", pool=pool, pe=pe, act=act, dve=dve)
            proj()

            def value_products(W, val, bank, heads, width):
                for h in range(heads):
                    cols = slice(h * HD, (h + 1) * HD)
                    nc.tensor.matmul(PS[:, bank, cols], W[:, h, 0, :], val[:, 0, cols], start=True, stop=True)
                    nc.tensor.matmul(PS[:, bank + 1, cols], W[:, h, 1, :], val[:, 0, cols], start=True, stop=False)
                    ins = nc.tensor.matmul(PS[:, bank + 1, cols], W[:, h, 2, :], val[:, 1, cols], start=False, stop=True)
                return ins

            def score_products(bank, k, q):
                nc.tensor.matmul(PS[:, bank, 0:T], k[:, 0:P], q, start=True, stop=True)
                return nc.tensor.matmul(PS[:, bank, T:TRI], k[:, P:T], q[:, P:T], start=True, stop=True)

            def ssd(L=L):
                pe_s = Steps(sem(L + "ssd_pe"), ["xs", "Gc", "CB", "Gr", "o"])
                dv_s = Steps(sem(L + "ssd_dve"), ["xs", "R", "E", "W", "o"])
                ac_s = Steps(sem(L + "ssd_act"), ["exp"])
                GRB = (0, 1, 5, 6)

                def pe(e, c):
                    for t in range(NT):
                        for n in range(4):
                            ins = nc.tensor.transpose(PS[:, t, n * P:(n + 1) * P], XBC[:, n, t * P:(t + 1) * P], ident)
                    pe_s.mark(ins, "xs")
                    nc.tensor.matmul(PS[:, 2, 0:8], inc, g8[:, 0, :], start=True, stop=True)
                    nc.tensor.matmul(PS[:, 2, 8:16], ones, g8[:, 0, :], start=True, stop=False)
                    pe_s.mark(nc.tensor.matmul(PS[:, 2, 8:16], inc, g8[:, 1, :], start=False, stop=True), "Gc")
                    for g in range(2):
                        rows = slice(g * HD, (g + 1) * HD)
                        ins = score_products(3 + g, XBC[rows, 4, :], XBC[rows, 5, :])
                    pe_s.mark(ins, "CB")
                    dv_s.wait(e, "xs")
                    dv_s.wait(e, "R")
                    for h in range(SSD_H):
                        o = PS[:, GRB[h // 2], (h % 2) * T:(h % 2) * T + T]
                        nc.tensor.matmul(o[:, 0:P], ones, Rg[:, h, 0, :], start=True, stop=True)
                        nc.tensor.matmul(o[:, P:T], ones, Rg[:, h, 1, :], start=True, stop=False)
                        ins = nc.tensor.matmul(o[:, P:T], ones, Rg[:, h, 2, :], start=False, stop=True)
                    pe_s.mark(ins, "Gr")
                    dv_s.wait(e, "W")
                    pe_s.mark(value_products(WS, xdt, 0, SSD_H, 512), "o")
                    return pe_s

                def act(e, c):
                    dv_s.wait(e, "E")
                    ac_s.mark(nc.scalar.activation(WS, WS, ACT.Exp), "exp")
                    return ac_s

                def dve(e, c):
                    V = nc.vector
                    c(V.tensor_tensor(Rg[:, :, 0, :], bc(inc, 1, SSD_H), bc(g8[:, 0, :], 2, P), ALU.mult))
                    c(V.tensor_copy(Rg[:, :, 1, :], bc(g8[:, 0, :], 2, P)))
                    c(V.tensor_tensor(Rg[:, :, 2, :], bc(inc, 1, SSD_H), bc(g8[:, 1, :], 2, P), ALU.mult))
                    pe_s.wait(e, "xs")
                    for t in range(NT):
                        ins = V.tensor_copy(xs[:, t, :], PS[:, t, :])
                    dv_s.mark(ins, "xs")
                    dv_s.wait(e, "xs")
                    for t in range(NT):
                        c(V.tensor_tensor(xdt[:, t, :].rearrange("p (h d) -> p h d", h=SSD_H),
                                          xs[:, t, :].rearrange("p (h d) -> p h d", h=SSD_H),
                                          bc(dtr[:, t, :], 2, HD), ALU.mult))
                    pe_s.wait(e, "Gc")
                    dv_s.mark(V.tensor_copy(Gc8, PS[:, 2, 0:16].rearrange("p (t h) -> p t h", t=NT)), "R")
                    dv_s.wait(e, "R")
                    pe_s.wait(e, "Gr")
                    for h in range(SSD_H):
                        o = PS[:, GRB[h // 2], (h % 2) * T:(h % 2) * T + T]
                        V.tensor_scalar(WS[:, h, 0:2, :].rearrange("p a t -> p (a t)"), o, Gc8[:, 0, h:h + 1], 0.0,
                                        ALU.subtract, ALU.min)
                        ins = V.tensor_scalar(WS[:, h, 2, :], o[:, P:T], Gc8[:, 1, h:h + 1], 0.0, ALU.subtract, ALU.min)
                    dv_s.mark(ins, "E")
                    ac_s.wait(e, "exp")
                    for s in (0, 2):
                        c(V.tensor_tensor(WS[:, :, s, :], WS[:, :, s, :], bc(inc, 1, SSD_H), ALU.mult))
                    pe_s.wait(e, "CB")
                    for g in range(2):
                        w = WS[:, 4 * g:4 * g + 4].rearrange("p h a t -> p h (a t)")
                        ins = V.tensor_tensor(w, w, bc(PS[:, 3 + g, 0:TRI], 1, 4), ALU.mult)
                    dv_s.mark(ins, "W")
                    for t in range(NT):
                        m = MIX[:, t, 0:512].rearrange("p (h d) -> p h d", h=SSD_H)
                        c(V.tensor_tensor(m, xs[:, t, :].rearrange("p (h d) -> p h d", h=SSD_H), bc(spar[:, 2], 2, HD),
                                          ALU.mult))
                    pe_s.wait(e, "o")
                    for t in range(NT):
                        c(V.tensor_tensor(MIX[:, t, 0:512], MIX[:, t, 0:512], PS[:, t, :], ALU.add))
                        ins = V.tensor_tensor(MIX[:, t, 0:512], MIX[:, t, 0:512], zrow[:, t, :], ALU.mult)
                        if t == 0:
                            c(ins)
                    dv_s.mark(ins, "o")
                    return dv_s
                stage(L + "ssd", pe=pe, act=act, dve=dve)
            ssd()

            def ret(L=L):
                pe_s = Steps(sem(L + "ret_pe"), ["qk", "o"])
                dv_s = Steps(sem(L + "ret_dve"), ["W", "o"])

                def pe(e, c):
                    for h in range(RE_H):
                        rows = slice((h % 2) * HD, (h % 2) * HD + HD)
                        ins = score_products(h, rot[rows, 2 + h // 2, :], rot[rows, h // 2, :])
                    pe_s.mark(ins, "qk")
                    dv_s.wait(e, "W")
                    pe_s.mark(value_products(WR, rv, 4, RE_H, T), "o")
                    return pe_s

                def dve(e, c):
                    pe_s.wait(e, "qk")
                    for h in range(RE_H):
                        ins = nc.vector.tensor_tensor(WR[:, h].rearrange("p a t -> p (a t)"), PS[:, h, 0:TRI],
                                                      ret_decay[:, h].rearrange("p a t -> p (a t)"), ALU.mult)
                    dv_s.mark(ins, "W")
                    pe_s.wait(e, "o")
                    for t in range(NT):
                        ins = nc.vector.tensor_copy(MIX[:, t, 768:1024], PS[:, 4 + t, 0:T])
                    dv_s.mark(ins, "o")
                    return dv_s
                stage(L + "ret", pe=pe, dve=dve)
            ret()

            def hgrn(L=L):
                sums = [("sum", a, b) for a in range(4) for b in range(2)]
                scs = [("sc", t, m) for t in range(NT) for m in range(LEVELS + 1)] + [("sc", 2, 0)]
                pe_s = Steps(sem(L + "hg_pe"), sums + scs + ["o"])
                ac_s = Steps(sem(L + "hg_act"), sums)
                dv_s = Steps(sem(L + "hg_dve"), ["qk"] + scs + ["o"])

                def pe(e, c):
                    for _, a, b in sums:
                        hp, t = a // 2, a % 2
                        lf = logf[:, t, hp * P:(hp + 1) * P]
                        bank = PS[:, 2 * a + b, :]
                        if b == 0:
                            ins = nc.tensor.matmul(bank, lf, lev_sum[:, 0:4, :], start=True, stop=True)
                        else:
                            nc.tensor.matmul(bank[:, 0:3 * P], lf, lev_sum[:, 4:7, :], start=True, stop=True)
                            ins = nc.tensor.matmul(bank[:, 3 * P:], lf, lev_sum[:, 7 + t, :], start=True, stop=True)
                        pe_s.mark(ins, ("sum", a, b))
                    dv_s.wait(e, "qk")
                    for i, (_, t, m) in enumerate(scs):
                        if i >= 4:
                            dv_s.wait(e, scs[i - 4])
                        for h in range(HG_H):
                            rows, hp = slice((h % 2) * HD, (h % 2) * HD + HD), h // 2
                            tk = slice(t * P, (t + 1) * P)
                            if t == 2:
                                a, b = EX[rows, 2 * hp, LEVELS, :], EX[rows, 2 * hp + 1, LEVELS, :]
                            elif m == 0:
                                a, b = kinT[rows, hp, tk], hqT[rows, hp, tk]
                            else:
                                a = b = EX[rows, 2 * hp + t, m - 1, :]
                            ins = nc.tensor.matmul(PS[:, 2 * (i % 4) + h % 2, hp * P:(hp + 1) * P], a, b,
                                                   start=True, stop=True)
                        pe_s.mark(ins, scs[i])
                    dv_s.wait(e, scs[-1])
                    pe_s.mark(value_products(WH, hi, 2, HG_H, T), "o")
                    return pe_s

                def act(e, c):
                    for _, a, b in sums:
                        pe_s.wait(e, ("sum", a, b))
                        ac_s.mark(nc.scalar.activation(EX[:, a, 4 * b:4 * b + 4, :],
                                                       PS[:, 2 * a + b, :].rearrange("p (l t) -> p l t", l=4), ACT.Exp),
                                  ("sum", a, b))
                    return ac_s

                def dve(e, c):
                    V = nc.vector
                    ac_s.wait(e, sums[-1])
                    q4 = hqT.rearrange("p h (t c) -> p (h t) c", t=NT)
                    k4 = kinT.rearrange("p h (t c) -> p (h t) c", t=NT)
                    for lev in range(LEVELS):
                        half, size = 1 << lev, 2 << lev
                        for src, lo in ((k4, 0), (q4, half)):
                            ex = EX[:, :, lev, :].rearrange("p a (n s) -> p a n s", s=size)[:, :, :, lo:lo + half]
                            sv = src.rearrange("p a (n s) -> p a n s", s=size)[:, :, :, lo:lo + half]
                            V.tensor_tensor(ex, ex, sv, ALU.mult)
                    V.tensor_tensor(EX[:, 0:4:2, LEVELS, :], EX[:, 0:4:2, LEVELS, :], k4[:, 0:4:2, :], ALU.mult)
                    dv_s.mark(V.tensor_tensor(EX[:, 1:4:2, LEVELS, :], EX[:, 1:4:2, LEVELS, :], q4[:, 1:4:2, :], ALU.mult), "qk")
                    mt4 = mtmp.rearrange("p (h r) t -> p r h t", r=2)

                    def lmask(m):
                        return lev_mask[:, m, :].unsqueeze(1).unsqueeze(1).broadcast_to([P, 2, 2, P])
                    for i, (_, t, m) in enumerate(scs):
                        pe_s.wait(e, scs[i])
                        b2 = 2 * (i % 4)
                        bank = PS[:, b2:b2 + 2, 0:2 * P].rearrange("p r (h t) -> p r h t", h=2)
                        dst = WH[:, :, (0, 2, 1)[t], :].rearrange("p (h r) t -> p r h t", r=2)
                        if t == 2:
                            ins = V.tensor_copy(dst, bank)
                        elif m == 0:
                            ins = V.tensor_tensor(dst, bank, lmask(0), ALU.mult)
                        else:
                            c(V.tensor_tensor(mt4, bank, lmask(m), ALU.mult))
                            ins = V.tensor_tensor(dst, dst, mt4, ALU.add)
                        dv_s.mark(ins, scs[i])
                        dv_s.wait(e, scs[i])
                    pe_s.wait(e, "o")
                    for t in range(NT):
                        ins = V.tensor_copy(MIX[:, t, 512:768], PS[:, 2 + t, 0:T])
                    dv_s.mark(ins, "o")
                    return dv_s
                stage(L + "hgrn", pe=pe, act=act, dve=dve)
            hgrn()

            def mixnorm(L=L):
                dv_s = Steps(sem(L + "mn_dve"), ["ss", "y"])
                ac_s = Steps(sem(L + "mn_act"), ["rt"])
                sq2 = arena(18868, NT, D)
                ssg, ssh = sm[:, 160:164], sm[:, 164:180]
                big = MIX[:, :, 0:512].rearrange("p t (g d) -> p t g d", g=2)
                small = MIX[:, :, 512:1024].rearrange("p t (h d) -> p t h d", h=8)

                def dve(e, c):
                    V = nc.vector
                    c(V.tensor_tensor(sq2, MIX, MIX, ALU.mult))
                    c(V.tensor_reduce(ssg.rearrange("p (t g) -> p t g", t=NT),
                                      sq2[:, :, 0:512].rearrange("p t (g d) -> p t g d", g=2), AX, ALU.add))
                    dv_s.mark(V.tensor_reduce(ssh.rearrange("p (t g) -> p t g", t=NT),
                                              sq2[:, :, 512:1024].rearrange("p t (g d) -> p t g d", g=8), AX, ALU.add), "ss")
                    c(V.tensor_tensor(hg, hg, bc(ngh, 1, NT), ALU.mult))
                    ac_s.wait(e, "rt")
                    c(V.reciprocal(sm[:, 160:180], sm[:, 160:180]))
                    c(V.tensor_tensor(big, big, bc(ssg.rearrange("p (t g) -> p t g", t=NT), 3, 256), ALU.mult))
                    c(V.tensor_tensor(small, small, bc(ssh.rearrange("p (t g) -> p t g", t=NT), 3, HD), ALU.mult))
                    c(V.tensor_tensor(MIX[:, :, 0:512], MIX[:, :, 0:512], bc(ngs, 1, NT), ALU.mult))
                    c(V.tensor_tensor(MIX[:, :, 512:768], MIX[:, :, 512:768], hg, ALU.mult))
                    dv_s.mark(V.tensor_tensor(MIX[:, :, 768:1024], MIX[:, :, 768:1024], rg, ALU.mult), "y")
                    return dv_s

                def act(e, c):
                    dv_s.wait(e, "ss")
                    nc.scalar.activation(ssg, ssg, ACT.Sqrt, bias=eps_col, scale=1.0 / 256)
                    ac_s.mark(nc.scalar.activation(ssh, ssh, ACT.Sqrt, bias=eps_col, scale=1.0 / HD), "rt")
                    return ac_s
                stage(L + "mixnorm", dve=dve, act=act)
            mixnorm()
            first_wo2 = ring_loads(io[f"w_out{layer}"], 2)
            out_proj_stage(L + "out", MIX, arena(18868, KC, T), first_wo2, MOD[:, 2, :], arena(21940, CW))

            NES, ESL = 4, 2 * KC * FE + 2 * D
            ebase = [ring[:, q * ESL:(q + 1) * ESL] for q in range(NES)]
            wg = [b[:, 0:KC * FE].rearrange("p (k f) -> p k f", k=KC) for b in ebase]
            wu = [b[:, KC * FE:2 * KC * FE].rearrange("p (k f) -> p k f", k=KC) for b in ebase]
            wd = [b[:, 2 * KC * FE:].rearrange("p (k n) -> p k n", k=2) for b in ebase]
            e_ld = [sem(L + f"e_ld{q}") for q in range(NES)]
            s_gu, s_silu, s_hm0, s_hm, s_dn, s_ez = (sem(L + n) for n in ("gu", "silu", "hm0", "hm", "dn", "ez"))
            release_ring(L + "out")

            def load_experts(sp, layer=layer, e_ld=e_ld, s_dn=s_dn, ebase=ebase, wd=wd):
                def body(x, q, first):
                    if not first:
                        sp.wait_ge(s_dn, x - NES + 1)
                    sp.dma_start(ebase[q][:, 0:KC * FE], io[f"w_gate{layer}"][x]).then_inc(e_ld[q], 16)
                    sp.dma_start(ebase[q][:, KC * FE:2 * KC * FE], io[f"w_up{layer}"][x]).then_inc(e_ld[q], 16)
                    sp.dma_start(wd[q], io[f"w_down{layer}"][x].rearrange("(k p) n -> p k n", p=P)).then_inc(e_ld[q], 16)
                for q in range(NES):
                    body(q, q, True)
                with sp.Fori(1, NEXP // NES) as i:
                    for q in range(NES):
                        body(i * NES + q, q, False)

            norm_T_stage(L + "norm_ffn", [(X[:, t, :], MOD[:, 4, :], MOD[:, 3, :]) for t in range(NT)],
                         io[f"ng_ffn{layer}"], hT, 12288)
            CMB = arena(12288, NEXP, T)
            sg, hid = arena(20480, 2, 512), arena(21504, 2, 512)
            wrt, brt = arena(22528, KC, 36), arena(22816, 36)
            lgt, comb = arena(22860, NT, 36), arena(22940, NT, NEXP)
            r1, r2 = arena(23010, NT, 4, 8), arena(23080, NT, 8)
            cT = arena(23200, T)
            rr = arena(23500, 200)

            def router(L=L, layer=layer):
                s_in = sem(L + "rt_in")
                bcs = [("b", i) for i in range(16)]
                pe_s = Steps(sem(L + "rt_pe"), ["lg", "tr"] + bcs)
                ac_s = Steps(sem(L + "rt_act"), ["e0", "e1"] + bcs[1::2])
                dv_s = Steps(sem(L + "rt_dve"), ["x0", "x1", "comb", "tr"] + bcs[0::2])

                def pool(e, c):
                    e.dma_start(wrt, io[f"w_rt{layer}"].rearrange("p (k n) -> p k n", k=KC)).then_inc(s_in, 16)
                    e.dma_start(brt, io[f"b_rt{layer}"].unsqueeze(0).broadcast_to([P, 36])).then_inc(s_in, 16)
                    e.wait_ge(s_in, 32)

                def pe(e, c):
                    e.wait_ge(s_in, 32)
                    for t in range(NT):
                        for k in range(KC):
                            ins = nc.tensor.matmul(PS[:, 0, t * 36:(t + 1) * 36], hT[:, k, t * P:(t + 1) * P], wrt[:, k, :],
                                                   start=(k == 0), stop=(k == KC - 1))
                    pe_s.mark(ins, "lg")
                    dv_s.wait(e, "comb")
                    for t in range(NT):
                        ins = nc.tensor.transpose(PS[0:NEXP, 1, t * P:(t + 1) * P], comb[:, t, :], ident)
                    pe_s.mark(ins, "tr")
                    dv_s.wait(e, "tr")
                    for i in range(16):
                        if i >= 4:
                            (dv_s if i % 2 == 0 else ac_s).wait(e, ("b", i - 4))
                        for a in range(2):
                            x = 2 * i + a
                            ins = nc.tensor.matmul(PS[:, 2 + i % 4, a * T:(a + 1) * T],
                                                   ident[0:NEXP, x:x + 1].broadcast_to([NEXP, P]), cT[0:NEXP, :],
                                                   start=True, stop=True)
                        pe_s.mark(ins, ("b", i))
                    return pe_s

                def dst(i):
                    return CMB[:, 2 * i:2 * i + 2, :], PS[:, 2 + i % 4, :].rearrange("p (a t) -> p a t", a=2)

                def act(e, c):
                    dv_s.wait(e, "x0")
                    ac_s.mark(nc.scalar.activation(rr[:, 8:16], rr[:, 8:16], ACT.Exp), "e0")
                    dv_s.wait(e, "x1")
                    ac_s.mark(nc.scalar.activation(rr[:, 66:68], rr[:, 66:68], ACT.Exp), "e1")
                    for i in range(1, 16, 2):
                        pe_s.wait(e, ("b", i))
                        ac_s.mark(nc.scalar.copy(*dst(i)), ("b", i))
                    return ac_s

                def dve(e, c):
                    V = nc.vector

                    def v(lo, n):
                        return rr[:, lo:lo + n].rearrange("p (t k) -> p t k", t=NT)
                    e.wait_ge(s_in, 32)
                    pe_s.wait(e, "lg")
                    c(V.tensor_tensor(lgt, PS[:, 0, 0:72].rearrange("p (t k) -> p t k", t=NT), bc(brt, 1, NT), ALU.add))
                    grp = lgt[:, :, 0:NGRP]
                    c(V.tensor_reduce(rr[:, 0:2], grp, AX, ALU.max))
                    dv_s.mark(V.tensor_tensor(v(8, 8), grp, bc(rr[:, 0:2], 2, NGRP), ALU.subtract), "x0")
                    c(V.tensor_tensor(v(16, 8), grp, bc(rr[:, 0:2], 2, NGRP), ALU.is_equal))
                    c(V.scalar_tensor_tensor(v(16, 8), v(16, 8), -1000.0, bc(iota[:, 0:NGRP], 1, NT), ALU.mult, ALU.add))
                    c(V.tensor_reduce(rr[:, 2:4], v(16, 8), AX, ALU.min))
                    c(V.tensor_tensor(v(16, 8), v(16, 8), bc(rr[:, 2:4], 2, NGRP), ALU.is_equal))
                    ac_s.wait(e, "e0")
                    c(V.tensor_reduce(rr[:, 4:6], v(8, 8), AX, ALU.add))
                    c(V.reciprocal(rr[:, 4:6], rr[:, 4:6]))
                    ex = lgt[:, :, NGRP:].rearrange("p t (g x) -> p t g x", g=NGRP)
                    c(V.tensor_tensor(r1, ex, bc(v(16, 8), 3, EPG), ALU.mult))
                    c(V.tensor_reduce(r2, r1.rearrange("p t g x -> p t x g"), AX, ALU.add))
                    for t in range(NT):
                        ins = V.max(v(24, 16)[:, t, :], r2[:, t, :])
                    c(ins)
                    for t in range(NT):
                        ins = V.max_index(v(40, 16).bitcast(U32)[:, t, :], v(24, 16)[:, t, :], r2[:, t, :])
                    c(ins)
                    dv_s.mark(V.tensor_tensor(rr[:, 66:68], v(24, 16)[:, :, 1], v(24, 16)[:, :, 0], ALU.subtract), "x1")
                    c(V.tensor_copy(v(70, 16), v(40, 16).bitcast(U32)))
                    ac_s.wait(e, "e1")
                    c(V.tensor_scalar_add(rr[:, 68:70], rr[:, 66:68], 1.0))
                    c(V.reciprocal(rr[:, 68:70], rr[:, 68:70]))
                    c(V.tensor_tensor(rr[:, 68:70], rr[:, 68:70], rr[:, 4:6], ALU.mult))
                    c(V.tensor_tensor(rr[:, 66:68], rr[:, 66:68], rr[:, 68:70], ALU.mult))
                    io8 = bc(iota[:, 0:EPG], 1, NT)
                    for j, w in ((0, 68), (1, 66)):
                        o = v(90 + 16 * j, 16)
                        c(V.tensor_tensor(o, io8, bc(v(70, 16)[:, :, j], 2, EPG), ALU.is_equal))
                        c(V.tensor_tensor(o, o, bc(rr[:, w:w + 2], 2, EPG), ALU.mult))
                    c(V.tensor_tensor(v(90, 16), v(90, 16), v(106, 16), ALU.add))
                    dv_s.mark(V.tensor_tensor(comb.rearrange("p t (g x) -> p t g x", g=NGRP), bc(v(16, 8), 3, EPG),
                                              bc(v(90, 16), 2, NGRP), ALU.mult), "comb")
                    pe_s.wait(e, "tr")
                    dv_s.mark(V.tensor_copy(cT[0:NEXP, :], PS[0:NEXP, 1, 0:T]), "tr")
                    for i in range(0, 16, 2):
                        pe_s.wait(e, ("b", i))
                        dv_s.mark(V.tensor_copy(*dst(i)), ("b", i))
                    return dv_s
                stage(L + "router", pool=pool, pe=pe, act=act, dve=dve)
            router()

            def experts(L=L, wg=wg, wu=wu, wd=wd, e_ld=e_ld, s_gu=s_gu, s_silu=s_silu, s_hm0=s_hm0, s_hm=s_hm,
                        s_dn=s_dn, s_ez=s_ez):
                zero2 = arena(24000, CW)

                def pe(e, c):
                    e.wait_ge(s_ez, 1)
                    for b in range(4):
                        nc.tensor.matmul(PS[:, 4 + b, :], zero2[:, 0:P], zero2, start=True, stop=False)

                    def up(x, q, turn, first=False):
                        e.wait_ge(e_ld[q], turn * 48 + 48)
                        if not first:
                            e.wait_ge(s_hm, x - 1)
                        for g, w in enumerate((wg[q], wu[q])):
                            for f in range(2):
                                for k in range(KC):
                                    ins = nc.tensor.matmul(PS[:, 2 * (q % 2) + g, f * T:(f + 1) * T],
                                                           w[:, k, f * P:(f + 1) * P], hT[:, k, :],
                                                           start=(k == 0), stop=(k == KC - 1))
                        ins.then_inc(s_gu, 1)

                    def down(x, q, last=False):
                        e.wait_ge(s_hm, x + 1)
                        h = hid[:, q % 2, :].rearrange("p (f t) -> p f t", f=2)
                        for f in range(2):
                            for t in range(NT):
                                for n in range(2):
                                    ins = nc.tensor.matmul(PS[:, 4 + 2 * t + n, :], h[:, f, t * P:(t + 1) * P],
                                                           wd[q][:, f, n * CW:(n + 1) * CW], start=False,
                                                           stop=last and f == 1)
                        ins.then_inc(s_dn, 1)
                    up(0, 0, 0, True)
                    for q in range(NES):
                        up(q + 1, (q + 1) % NES, (q + 1) // NES, q == 0)
                        down(q, q)
                    with e.Fori(1, NEXP // NES - 1) as i:
                        for q in range(NES):
                            up(i * NES + q + 1, (q + 1) % NES, i + (q + 1) // NES)
                            down(i * NES + q, q)
                    for x in range(NEXP - NES, NEXP):
                        if x < NEXP - 1:
                            up(x + 1, (x + 1) % NES, (x + 1) // NES)
                        down(x, x % NES, x == NEXP - 1)
                    e.wait_ge(s_dn, NEXP)

                def loop(e, body):
                    for q in range(NES):
                        body(q, q, q < 2)
                    with e.Fori(1, NEXP // NES) as i:
                        for q in range(NES):
                            body(i * NES + q, q, False)

                def act(e, c):
                    def body(x, q, first):
                        e.wait_ge(s_gu, x + 1)
                        if not first:
                            e.wait_ge(s_hm, x - 1)
                        nc.scalar.activation(sg[:, q % 2, :], PS[:, 2 * (q % 2), :], ACT.Silu).then_inc(s_silu, 1)
                    loop(e, body)
                    e.wait_ge(s_silu, NEXP)

                def dve(e, c):
                    nc.vector.memset(zero2, 0.0).then_inc(s_ez, 1)

                    def body(x, q, first):
                        e.wait_ge(s_silu, x + 1)
                        s = sg[:, q % 2, :].rearrange("p (f t) -> p f t", f=2)
                        nc.vector.tensor_tensor(s, s, CMB[:, bass.ds(x, 1), :].broadcast_to([P, 2, T]),
                                                ALU.mult).then_inc(s_hm0, 1)
                        e.wait_ge(s_hm0, x + 1)
                        if not first:
                            e.wait_ge(s_dn, x - 1)
                        nc.vector.tensor_tensor(hid[:, q % 2, :], sg[:, q % 2, :], PS[:, 2 * (q % 2) + 1, :],
                                                ALU.mult).then_inc(s_hm, 1)
                    loop(e, body)
                    e.wait_ge(s_hm, NEXP)
                stage(L + "experts", pe=pe, act=act, dve=dve)
            stream.append(load_experts)
            experts()
            add_norm_stage(L + "moe_out", MOD[:, 5, :], io["final2"] if layer == LAYERS - 1 else None, 20480)

        s_store = sem("s_store")

        def pool_out(e, c):
            e.dma_start(io["out"].rearrange("o (t p) d -> p (o t) d", p=P), X[:]).then_inc(s_store, 16)
            e.wait_ge(s_store, 16)
        stage("store", pool=pool_out)

        block = ctx.enter_context(nc.Block())

        def run(eng, kind, chain):
            for k, (name, progs) in enumerate(stages):
                if kind in progs:
                    steps = progs[kind](eng, chain)
                    if steps is not None:
                        assert steps.n == len(steps.names), (name, kind, steps.n)
                        eng.wait_ge(steps.sem, steps.n)
                eng.sem_inc(s_bar, 1)
                eng.wait_ge(s_bar, 4 * (k + 1))

        @block.sync
        def _(sp):
            for load in stream:
                load(sp)

        @block.scalar
        def _(act):
            run(act, "act", Chain(act, s_a))

        @block.vector
        def _(dve):
            run(dve, "dve", Chain(dve, s_v))

        @block.tensor
        def _(pe):
            run(pe, "pe", None)

        @block.gpsimd
        def _(pool):
            run(pool, "pool", Chain(pool, s_g))


def slots(w):
    n = w.shape[1] // CW
    return np.ascontiguousarray(w.reshape(P, KC, n, CW).transpose(2, 0, 1, 3)).reshape(n, P, SLOT)


def layout(i):
    a = {"const": CONST, "x": i["x"], "ctx": i["ctx"]}
    a["c"] = i["c"].reshape(P, KC)
    a["c_ctx"] = i["c_ctx"].reshape(P, KC)
    a["ada_w"] = slots(i["ada_w"][0])
    a["ada_b"] = i["ada_b"][0]
    a["norm_g0"], a["norm_g1"] = i["norm_g"][0, 0], i["norm_g"][0, 1]
    w = i["dn_w_in"][0]
    a["dn_w"] = slots(w[:, :4 * D])
    a["dn_wba"] = np.ascontiguousarray(w[:, 4 * D:]).reshape(P, KC * 32)
    a["dn_cw"] = np.ascontiguousarray(i["dn_conv_w"][0].reshape(DN_TAPS, 24, P).transpose(2, 1, 0)).reshape(P, 24 * DN_TAPS)
    a["dn_alog"], a["dn_dt"] = i["dn_a_log"].reshape(16), i["dn_dt_bias"].reshape(16)
    a["dn_ng"] = i["dn_norm_g"][0]
    a["dn_wo"] = slots(i["dn_w_out"][0])
    a["peer_wq"] = slots(i["peer_w_q"][0])
    a["peer_kT"] = np.ascontiguousarray(i["peer_keys"][0].reshape(16, NK, P).transpose(2, 0, 1)).reshape(P, 16 * NK)
    a["peer_u"] = np.ascontiguousarray(i["peer_u"][0].reshape(NK, NK, P, KC).transpose(1, 2, 3, 0)).reshape(NK, P, KC * P)
    a["peer_v"] = i["peer_v"][0].reshape(NK, NK, D)
    a["final_g"] = i["final_g"]
    for l in range(LAYERS):
        w = i["w_in_2"][l]
        cut = np.cumsum([512, 768, 8, 256, 256, 256, 256, 256, 256, 256, 256])[:-1]
        z, xbc, dt, hq, hf, hi, hg, rq, rk, rv, rg = np.split(w, cut, axis=1)

        def swap(m):
            return m.reshape(D, RE_H, 2, HD // 2)[:, :, ::-1].reshape(D, RE_H * HD)
        a[f"w_in{l}"] = slots(np.concatenate([xbc, hq, hf, rq, rk, swap(rq), swap(rk), hf, z, hi, hg, rv, rg], 1))
        a[f"w_dt{l}"] = np.ascontiguousarray(dt).reshape(P, KC * 8)
        a[f"ada_w{l}"] = slots(i["w_ada_2"][l])
        a[f"ada_b{l}"] = i["b_ada_2"][l]
        a[f"ng_mix{l}"], a[f"ng_ffn{l}"] = i["norm_mix_g_2"][l], i["norm_ffn_g_2"][l]
        cw = np.concatenate([i["conv_w_2"][l], i["conv_b_2"][l][None]], 0)
        a[f"conv{l}"] = np.ascontiguousarray(cw.reshape(5, 6, P).transpose(2, 1, 0)).reshape(P, 30)
        a[f"ssd{l}"] = np.concatenate([i["ssd_dt_bias_2"][l], i["ssd_a_log_2"][l], i["ssd_d_2"][l]])
        a[f"ng_ssd{l}"], a[f"ng_hgrn{l}"] = i["ssd_norm_g_2"][l], i["hgrn_norm_g_2"][l]
        a[f"w_out{l}"] = slots(i["w_out_2"][l])
        a[f"w_rt{l}"] = np.concatenate([i["w_grp_2"][l], i["w_exp_2"][l]], 1).reshape(P, KC * 36)
        a[f"b_rt{l}"] = np.concatenate([i["b_grp_2"][l], i["b_exp_2"][l]])
        a[f"w_gate{l}"] = i["w_gate_2"][l].reshape(NEXP, P, KC * FE)
        a[f"w_up{l}"] = i["w_up_2"][l].reshape(NEXP, P, KC * FE)
        a[f"w_down{l}"] = i["w_down_2"][l]
    a["lbs"] = i["hgrn_lower_bounds_2"]
    a["lbsT"] = np.ascontiguousarray(i["hgrn_lower_bounds_2"].reshape(2, 2, P).transpose(2, 0, 1)).reshape(P, 4)
    a["c2"] = i["c_2"].reshape(P, KC)
    a["final2"] = i["final_norm_g_2"]
    return a


def kernel(**inputs):
    import concourse.bacc as bacc
    from concourse.bass_utils import run_bass_kernel_spmd as run

    arrays = layout({k: np.asarray(v) for k, v in inputs.items()})
    arrays = {f"in_{k}": np.ascontiguousarray(v) for k, v in arrays.items()}
    nc = bacc.Bacc("TRN2", target_bir_lowering=False, num_devices=1)
    io = {k[3:]: nc.dram_tensor(k, v.shape, mybir.dt.from_np(v.dtype), kind="ExternalInput").ap()
          for k, v in arrays.items()}
    io["out"] = nc.dram_tensor("out", (1, T, D), F32, kind="ExternalOutput").ap()
    build(nc, io)
    r = run(nc, [arrays], core_ids=[0])
    return r.results[0]["out"]
```

```python
from contextlib import ExitStack

import numpy as np

import concourse.bass as bass
from concourse import mybir

F32 = mybir.dt.float32
U32 = mybir.dt.uint32
F32R = mybir.dt.float32r
ALU = mybir.AluOpType
ACT = mybir.ActivationFunctionType
AX = mybir.AxisListType.X

P = 128
T = 256
NT = T // P
D = 1024
KC = D // P
EPS = 1e-6
CW = 512
SLOT = KC * CW
NRING = 3

DN_H = 8
DN_BLOCK = 64
ROWS, ROW_W = 4, 64
DN_TAPS = 5
DN_PAD = (DN_TAPS - 1) // 2
PH, NK, TOPK = 8, 128, 16
LAYERS = 2
SSD_H, HG_H, RE_H, HD = 8, 4, 4, 64
TAPS2 = 4
GATE_FLOOR = 1e-30
NGRP, EPG, NEXP, FE = 4, 8, 32, 256
LEVELS = 7
TRI = P * 3
NEG = -3.0e38



def shape_constants():
    i = np.arange(P)
    row, col = i[:, None], i[None, :]
    parts = {}
    parts["ident"] = row == col
    parts["ones"] = np.ones((P, P))
    parts["inc_f"] = row <= col
    parts["inc_b"] = row >= col
    parts["strict_f"] = row < col
    parts["strict_b"] = row > col
    same = row // DN_BLOCK == col // DN_BLOCK
    parts["block"] = same
    parts["off"] = ~same
    lm = [row == col]
    em = []
    for lev in range(LEVELS):
        half, size = 1 << lev, 2 << lev
        blk = row // size == col // size
        left_r, right_c = row % size < half, col % size >= half
        lm.append(blk & left_r & right_c)
        right = right_c & (row % size >= half) & (row <= col)
        left = ~right_c & left_r & (row > col)
        em.append(blk & (right | left))
    em.append(row > col)
    em.append(row <= col)
    parts["lev_mask"] = np.concatenate(lm, 1)
    parts["lev_sum"] = np.concatenate(em, 1)
    half = HD // 2
    inv = (np.float32(10000.0) ** (-np.arange(half, dtype=np.float32) / np.float32(half))).astype(np.float32)
    ang = (np.arange(T, dtype=np.float32)[:, None] * inv[None, :]).astype(np.float32)
    cos, sin = np.cos(ang.astype(np.float64)).T, np.sin(ang.astype(np.float64)).T
    parts["cos"] = np.tile(cos, (4, 1))
    parts["sin"] = np.tile(np.concatenate([-sin, sin], 0), (2, 1))
    lg = np.log1p(-np.exp2(-5.0 - np.arange(RE_H)))
    dd = []
    for h in range(RE_H):
        a = np.where(row <= col, np.exp(lg[h] * np.maximum(col - row, 0)), 0.0)
        b = np.exp(lg[h] * (col + P - row))
        dd += [a, b, a]
    parts["ret_decay"] = np.concatenate(dd, 1)
    parts["iota"] = np.broadcast_to(col, (P, P))
    out, at = [], {}
    n = 0
    for k, v in parts.items():
        at[k] = (n, v.shape[1])
        n += v.shape[1]
        out.append(v.astype(np.float32))
    return np.ascontiguousarray(np.concatenate(out, 1)), at


CONST, CAT = shape_constants()


class Steps:

    def __init__(self, sem, names, base=0, done=None):
        self.sem, self.names, self.at = sem, names, {n: base + i + 1 for i, n in enumerate(names)}
        assert len(self.at) == len(names)
        self.n, self.base, self.done = 0, base, done if done is not None else [base]

    def mark(self, ins, name):
        assert self.names[self.n] == name, (self.n, self.names[self.n], name)
        assert self.done[0] == self.base + self.n
        self.done[0] += 1
        self.n += 1
        ins.then_inc(self.sem, 1)

    def wait(self, eng, name):
        eng.wait_ge(self.sem, self.at[name])


class Chain:

    def __init__(self, eng, sem):
        self.eng, self.sem, self.n = eng, sem, 0

    def __call__(self, ins):
        self.n += 1
        ins.then_inc(self.sem, 1)
        self.eng.wait_ge(self.sem, self.n)


def bc(ap, axis, n):
    v = ap.unsqueeze(axis)
    shape = list(v.shape)
    shape[axis] = n
    return v.broadcast_to(shape)


def build(nc, io):
    ctx = ExitStack()
    with ctx:
        def sb(name, shape, dt=F32):
            return ctx.enter_context(nc.sbuf_tensor(name, shape, dt))

        def sem(name):
            return ctx.enter_context(nc.semaphore(name))

        WORDS = NRING * SLOT + 32768 + 3 * P + 2 * NT * D + D + 3 * T + 256 + 1536
        slab_at = (nc.sbuf_base + 31) // 32 * 32
        ring = sb("ring", [P, WORDS])
        RB = NRING * SLOT
        taken = [RB + 32768]

        def fixed(n):
            taken[0] += n
            assert taken[0] <= WORDS
            return ring[:, taken[0] - n:taken[0]]

        over = []

        def r32(word, *shape):
            over.append(nc.alloc_sbuf_tensor_at(f"over{len(over)}", [P, *shape], F32R, offset=slab_at + 4 * word))
            v = over[-1][tuple(slice(None) for _ in range(len(shape) + 1))]
            return v, v.bitcast(F32)
        cst = fixed(3 * P)
        ident, ones, iota = cst[:, 0:P], cst[:, P:2 * P], cst[:, 2 * P:3 * P]
        X_at = taken[0]
        X = fixed(NT * D).rearrange("p (t d) -> p t d", t=NT)
        hT_at = taken[0]
        hT = fixed(KC * T).rearrange("p (k t) -> p k t", k=KC)
        GT = fixed(D)
        idx = fixed(3 * T).rearrange("p (a t) -> p a t", a=3)
        sm = fixed(256)
        spare_at = taken[0]
        PS = ctx.enter_context(nc.psum_tensor("PS", [P, 8, 512], F32))

        def arena(off, *shape):
            n = int(np.prod(shape))
            v = ring[:, RB + off:RB + off + n]
            if len(shape) == 1:
                return v
            names = "abcd"[:len(shape)]
            return v.rearrange(f"p ({' '.join(names)}) -> p {' '.join(names)}",
                               **{names[i]: shape[i] for i in range(1, len(shape))})

        MOD = arena(26624, 6, D)

        s_bar = sem("s_bar")
        s_ring = [sem(f"s_ring{i}") for i in range(NRING)]
        s_v, s_a, s_g = sem("s_v"), sem("s_a"), sem("s_g")
        s_steps = {who: sem(f"s_{who}_steps") for who in ("pe", "act", "dve")}
        n_steps = {who: 0 for who in s_steps}
        steps_done = {who: [0] for who in s_steps}

        def steps(who, names):
            st = Steps(s_steps[who], names, n_steps[who], steps_done[who])
            n_steps[who] += len(names)
            return st

        s_out = sem("s_out")
        s_cst = sem("s_cst")
        stream = []
        free_at = []
        stages = []

        def stage(name, **progs):
            stages.append((name, progs))

        def ring_load(src):
            n = len(free_at)
            free_at.append(None)

            def load(sp):
                if n >= NRING:
                    steps, name = free_at[n - NRING]
                    steps.wait(sp, name)
                sp.dma_start(ring[:, (n % NRING) * SLOT:(n % NRING + 1) * SLOT], src).then_inc(s_ring[n % NRING], 16)
            stream.append(load)
            return n

        def ring_loads(src, count):
            first = len(free_at)
            for j in range(count):
                ring_load(src[j])
            return first

        def slot(n):
            return ring[:, (n % NRING) * SLOT:(n % NRING) * SLOT + SLOT].rearrange("p (k c) -> p k c", k=KC)

        def ring_wait(eng, n):
            eng.wait_ge(s_ring[n % NRING], 16 * (n // NRING + 1))

        def exact3(out, lhs, rhs, start, stop):
            nc.tensor.matmul(out, lhs[0], rhs[0], start=start, stop=False)
            nc.tensor.matmul(out, lhs[0], rhs[1], start=False, stop=False)
            return nc.tensor.matmul(out, lhs[1], rhs[0], start=False, stop=stop)

        def ada_stage(tag, w_slots, b_dram, c_cols, c2_cols=None, modc=None):
            first = ring_loads(w_slots, 12)
            s_in = sem(f"{tag}_in")
            rep = arena(0, 2, KC, P)
            cc = sm[:, 0:2 * KC].rearrange("p (a k) -> p a k", a=2)
            n2 = 1 if c2_cols is None else 2
            mm_names = [(who, n) for n in range(12) for who in ("c", "ctx")[:n2 if n < 4 else 1]]
            pe_s = steps("pe", mm_names)
            dv_s = steps("dve", ["rep"] + mm_names)
            ac_s = steps("act", ["silu"])
            for n in range(12):
                free_at[first + n] = (pe_s, (("c", "ctx")[n2 - 1 if n < 4 else 0], n))

            def pool(e, c):
                e.dma_start(MOD.rearrange("p a b -> p (a b)"), b_dram.unsqueeze(0).broadcast_to([P, 6 * D])).then_inc(s_in, 16)
                e.dma_start(cc[:, 0, :], c_cols).then_inc(s_in, 16)
                if n2 == 2:
                    e.dma_start(modc.rearrange("p a b -> p (a b)"), b_dram[0:2 * D].unsqueeze(0).broadcast_to([P, 2 * D])).then_inc(s_in, 16)
                    e.dma_start(cc[:, 1, :], c2_cols).then_inc(s_in, 16)
                e.wait_ge(s_in, 32 * n2)

            def act(e, c):
                e.wait_ge(s_in, 32 * n2)
                ac_s.mark(nc.scalar.activation(cc[:, 0:n2, :], cc[:, 0:n2, :], ACT.Silu), "silu")
                return ac_s

            def dve(e, c):
                ac_s.wait(e, "silu")
                dv_s.mark(nc.vector.tensor_copy(rep[:, 0:n2], bc(cc[:, 0:n2, :], 3, P)), "rep")
                for i, (who, n) in enumerate(mm_names):
                    pe_s.wait(e, (who, n))
                    dst = (MOD if who == "c" else modc)[:, n // 2, (n % 2) * CW:(n % 2) * CW + CW]
                    dv_s.mark(nc.vector.tensor_tensor(dst, dst, PS[:, i % 4, :], ALU.add), (who, n))
                dv_s.wait(e, mm_names[-1])
                for m in (1, 4):
                    c(nc.vector.tensor_scalar_add(MOD[:, m, :], MOD[:, m, :], 1.0))
                if n2 == 2:
                    c(nc.vector.tensor_scalar_add(modc[:, 1, :], modc[:, 1, :], 1.0))

            def pe(e, c):
                dv_s.wait(e, "rep")
                for i, (who, n) in enumerate(mm_names):
                    ring_wait(e, first + n)
                    if i >= 4:
                        dv_s.wait(e, mm_names[i - 4])
                    for k in range(KC):
                        ins = nc.tensor.matmul(PS[:, i % 4, :], rep[:, int(who == "ctx"), k, :],
                                               slot(first + n)[:, k, :], start=(k == 0), stop=(k == KC - 1))
                    pe_s.mark(ins, (who, n))
                return pe_s

            stage(tag, pool=pool, act=act, dve=dve, pe=pe)

        def norm_T_stage(tag, srcs, g_dram, dest, off):
            n = len(srcs)
            gb = arena(off, D)
            A = arena(off + D, 2, D)
            sq = arena(off + 3 * D, D)
            HN = arena(off + 4 * D, n, D)
            s_in = sem(f"{tag}_in")
            ac_s = steps("act", [x for t in range(n) for x in (("ss", t), ("rt", t))] +
                         [("ev", t, 1) for t in range(n)])
            dv_s = steps("dve", [("hn", t) for t in range(n)] + [("ev", t, 0) for t in range(n)])
            pe_s = steps("pe", [("tr", t, b) for t in range(n) for b in range(2)])

            def pool(e, c):
                e.dma_start(gb, g_dram.unsqueeze(0).broadcast_to([P, D])).then_inc(s_in, 16)
                e.wait_ge(s_in, 16)

            def act(e, c):
                for t in range(n):
                    if t:
                        ac_s.wait(e, ("ss", t - 1))
                    ac_s.mark(nc.scalar.activation(sq, srcs[t][0], ACT.Square, accum_out=sm[:, t:t + 1]), ("ss", t))
                    ac_s.wait(e, ("ss", t))
                    ac_s.mark(nc.scalar.activation(sm[:, 8 + t:9 + t], sm[:, t:t + 1], ACT.Sqrt,
                                                   bias=eps_col, scale=1.0 / D), ("rt", t))
                for t in range(n):
                    pe_s.wait(e, ("tr", t, 1))
                    ac_s.mark(nc.scalar.copy(dest[:, 4:8, t * P:(t + 1) * P],
                                             PS[:, (2 * t + 1) % 8, :].rearrange("p (k t) -> p k t", k=4)),
                              ("ev", t, 1))
                return ac_s

            def dve(e, c):
                e.wait_ge(s_in, 16)
                for a in range(n // NT):
                    c(nc.vector.tensor_tensor(A[:, a, :], gb, srcs[a * NT][1], ALU.mult))
                for t, (rows, sc, sh) in enumerate(srcs):
                    ac_s.wait(e, ("rt", t))
                    c(nc.vector.reciprocal(sm[:, 16 + t:17 + t], sm[:, 8 + t:9 + t]))
                    c(nc.vector.scalar_tensor_tensor(HN[:, t, :], rows, sm[:, 16 + t:17 + t],
                                                     A[:, t // NT, :], ALU.mult, ALU.mult))
                    dv_s.mark(nc.vector.tensor_tensor(HN[:, t, :], HN[:, t, :], sh, ALU.add), ("hn", t))
                for t in range(n):
                    pe_s.wait(e, ("tr", t, 0))
                    dv_s.mark(nc.vector.tensor_copy(dest[:, 0:4, t * P:(t + 1) * P],
                                                    PS[:, (2 * t) % 8, :].rearrange("p (k t) -> p k t", k=4)),
                              ("ev", t, 0))
                return dv_s

            def pe(e, c):
                for t in range(n):
                    dv_s.wait(e, ("hn", t))
                    v = HN[:, t, :].rearrange("p (c k) -> p k c", k=KC)
                    for b in range(2):
                        for k in range(4):
                            ins = nc.tensor.transpose(PS[:, (2 * t + b) % 8, k * P:(k + 1) * P], v[:, 4 * b + k, :],
                                                      ident)
                        pe_s.mark(ins, ("tr", t, b))
                return pe_s

            stage(tag, pool=pool, act=act, dve=dve, pe=pe)

        eps_col = sm[:, 255:256]

        ctxr = arena(24576 - 2 * D, NT, D)
        modc = arena(24576 - 4 * D, 2, D)
        s_x = sem("s_x")

        def pool0(sp, c):
            for n, name in enumerate(("ident", "ones", "iota")):
                sp.dma_start(cst[:, n * P:(n + 1) * P], io["const"][:, CAT[name][0]:CAT[name][0] + P]).then_inc(s_cst, 16)
            sp.dma_start(X, io["x"].rearrange("o (t p) d -> p (o t) d", p=P)).then_inc(s_x, 16)
            sp.dma_start(ctxr, io["ctx"].rearrange("o (t p) d -> p (o t) d", p=P)).then_inc(s_x, 16)

            sp.wait_ge(s_x, 32)
            sp.wait_ge(s_cst, 48)

        def dve0(e, c):
            c(nc.vector.memset(eps_col, EPS))
            e.wait_ge(s_x, 32)

        def wait_cst(e, c):
            e.wait_ge(s_cst, 48)

        def act0(e, c):
            e.wait_ge(s_x, 32)

        stage("start", pool=pool0, dve=dve0, pe=wait_cst, act=act0)

        ada_stage("ada_a", io["ada_w"], io["ada_b"], io["c"], io["c_ctx"], modc)
        hnT = arena(0, KC, 2 * T)
        sc_x, sh_x, sc_c, sh_c = MOD[:, 1, :], MOD[:, 0, :], modc[:, 1, :], modc[:, 0, :]
        norm_T_stage("norm_a", [(X[:, 0, :], sc_x, sh_x), (X[:, 1, :], sc_x, sh_x),
                                (ctxr[:, 0, :], sc_c, sh_c), (ctxr[:, 1, :], sc_c, sh_c)],
                     io["norm_g0"], hnT, 4096)


        def out_proj_loads(after, src):
            k = [s[0] for s in stages].index(after) + 1
            stream.append(lambda sp: sp.wait_ge(s_bar, 4 * k))
            return ring_loads(src, 2)

        def out_proj_stage(tag, rows, rT, first, gain, tmp):
            tr = [("tr", t, b) for t in range(NT) for b in range(2)]
            mmn = [("mm", s, t) for s in range(2) for t in range(NT)]
            pe_s = steps("pe", tr + mmn)
            dv_s = steps("dve", tr[0::2] + mmn)
            ac_s = steps("act", tr[1::2])
            for s in range(2):
                free_at[first + s] = (pe_s, ("mm", s, NT - 1))

            def pe(e, c):
                for i, (_, t, b) in enumerate(tr):
                    v = rows[:, t, :].rearrange("p (c k) -> p k c", k=KC)
                    for k in range(4):
                        ins = nc.tensor.transpose(PS[:, i, k * P:(k + 1) * P], v[:, 4 * b + k, :], ident)
                    pe_s.mark(ins, tr[i])
                dv_s.wait(e, tr[2])
                ac_s.wait(e, tr[3])
                for i, (_, s, t) in enumerate(mmn):
                    ring_wait(e, first + s)
                    for k in range(KC):
                        ins = nc.tensor.matmul(PS[:, 4 + i, :], rT[:, k, t * P:(t + 1) * P], slot(first + s)[:, k, :],
                                               start=(k == 0), stop=(k == KC - 1))
                    pe_s.mark(ins, mmn[i])
                return pe_s

            def evac(op, i):
                _, t, b = tr[i]
                return op(rT[:, 4 * b:4 * b + 4, t * P:(t + 1) * P], PS[:, i, :].rearrange("p (k t) -> p k t", k=4))

            def act(e, c):
                for i in (1, 3):
                    pe_s.wait(e, tr[i])
                    ac_s.mark(evac(nc.scalar.copy, i), tr[i])
                return ac_s

            def dve(e, c):
                for i in (0, 2):
                    pe_s.wait(e, tr[i])
                    dv_s.mark(evac(nc.vector.tensor_copy, i), tr[i])
                for i, (_, s, t) in enumerate(mmn):
                    pe_s.wait(e, mmn[i])
                    cols = slice(s * CW, (s + 1) * CW)
                    c(nc.vector.tensor_tensor(tmp, PS[:, 4 + i, :], gain[:, cols], ALU.mult))
                    dv_s.mark(nc.vector.tensor_tensor(X[:, t, cols], X[:, t, cols], tmp, ALU.add), mmn[i])
                    dv_s.wait(e, mmn[i])
                return dv_s

            stage(tag, pe=pe, act=act, dve=dve)

        NQ = 4
        kT = arena(10240, DN_H, 2 * T)
        qT = arena(14336, DN_H, T)
        Krow = arena(16384, NQ, DN_H, P)
        Vrow = arena(20480, NQ, DN_H, P)
        gate = arena(24576, NT, D)
        vT = arena(4096, DN_H, 2 * T)
        XPAD = ROWS * (ROW_W + 2 * DN_PAD)
        CPAD = T + 2 * DN_PAD
        zpad = arena(16384, 2, XPAD + CPAD)
        conv = arena(16384 + 2 * (XPAD + CPAD), 2, 2 * T)
        cw = arena(19000, 24, DN_TAPS)
        wba = arena(19200, KC, 32)
        first_w = ring_loads(io["dn_w"], 8)
        s_dnin = sem("s_dnin")
        ba = sm[:, 0:NQ * 32].rearrange("p (t c) -> p t c", t=NQ)
        rows_ev = [("row", s, t) for s in range(2) for t in range(NT)]
        dn1_pe = steps("pe", [("z", n) for n in range(24)] + rows_ev + ["ba"])
        dn1_ac = steps("act", [x for n in range(24) for x in ([("pad", n)] + ([("silu", n - 1)] if n else []))] +
                       [("silu", 23)] + rows_ev)
        dn1_dv = steps("dve", ["zero"] + [("conv", n) for n in range(24)] + ["ba"])
        for s in range(6):
            free_at[first_w + s] = (dn1_pe, ("z", 4 * s + 3))
        for s in range(2):
            free_at[first_w + 6 + s] = (dn1_pe, ("row", s, NT - 1))

        def pool_dn1(e, c):
            e.dma_start(cw, io["dn_cw"].rearrange("p (n t) -> p n t", n=24)).then_inc(s_dnin, 16)
            e.dma_start(wba, io["dn_wba"].rearrange("p (k n) -> p k n", k=KC)).then_inc(s_dnin, 16)
            e.wait_ge(s_dnin, 32)

        def pe_dn1(e, c):
            for n in range(24):
                s = n // 4
                ring_wait(e, first_w + s)
                if n >= 4:
                    dn1_ac.wait(e, ("pad", n - 4))
                w = slot(first_w + s)
                toks = T if n < DN_H else 2 * T
                for k in range(KC):
                    ins = nc.tensor.matmul(PS[:, n % 4, 0:toks], w[:, k, (n % 4) * P:(n % 4 + 1) * P],
                                           hnT[:, k, 0:toks], start=(k == 0), stop=(k == KC - 1))
                dn1_pe.mark(ins, ("z", n))
            for s in range(2):
                ring_wait(e, first_w + 6 + s)
                for t in range(NT):
                    for k in range(KC):
                        ins = nc.tensor.matmul(PS[:, 4 + 2 * s + t, :], hnT[:, k, t * P:(t + 1) * P],
                                               slot(first_w + 6 + s)[:, k, :], start=(k == 0), stop=(k == KC - 1))
                    dn1_pe.mark(ins, ("row", s, t))
            e.wait_ge(s_dnin, 32)
            dn1_ac.wait(e, ("pad", 20))
            for t in range(NQ):
                for k in range(KC):
                    ins = nc.tensor.matmul(PS[:, 0, t * 32:(t + 1) * 32], hnT[:, k, t * P:(t + 1) * P], wba[:, k, :],
                                           start=(k == 0), stop=(k == KC - 1))
            dn1_pe.mark(ins, "ba")
            return dn1_pe

        def pad_views(buf):
            return (buf[:, 0:XPAD].rearrange("p (r w) -> p r w", r=ROWS), buf[:, XPAD:XPAD + CPAD])

        def act_dn1(e, c):
            dn1_dv.wait(e, "zero")

            def silu(n):
                dn1_dv.wait(e, ("conv", n))
                toks = T if n < DN_H else 2 * T
                dest = (qT, kT, vT)[n // DN_H]
                dn1_ac.mark(nc.scalar.activation(dest[:, n % DN_H, :], conv[:, n % 2, 0:toks], ACT.Silu), ("silu", n))
            for n in range(24):
                dn1_pe.wait(e, ("z", n))
                if n >= 2:
                    dn1_dv.wait(e, ("conv", n - 2))
                xv, cv = pad_views(zpad[:, n % 2])
                ins = nc.scalar.copy(xv[:, :, DN_PAD:DN_PAD + ROW_W],
                                     PS[:, n % 4, 0:T].rearrange("p (r w) -> p r w", r=ROWS))
                if n >= DN_H:
                    ins = nc.scalar.copy(cv[:, DN_PAD:DN_PAD + T], PS[:, n % 4, T:2 * T])
                dn1_ac.mark(ins, ("pad", n))
                if n:
                    silu(n - 1)
            silu(23)
            for s in range(2):
                for t in range(NT):
                    dn1_pe.wait(e, ("row", s, t))
                    dn1_ac.mark(nc.scalar.activation(gate[:, t, s * CW:(s + 1) * CW], PS[:, 4 + 2 * s + t, :], ACT.Silu),
                                ("row", s, t))
            return dn1_ac

        def dve_dn1(e, c):
            dn1_dv.mark(nc.vector.memset(zpad, 0.0), "zero")
            e.wait_ge(s_dnin, 32)
            for n in range(24):
                dn1_ac.wait(e, ("pad", n))
                if n >= 2:
                    dn1_ac.wait(e, ("silu", n - 2))
                xv, cv = pad_views(zpad[:, n % 2])
                xo = conv[:, n % 2, 0:T].rearrange("p (r w) -> p r w", r=ROWS)
                co = conv[:, n % 2, T:2 * T]
                pairs = [(xo, xv)] + ([(co, cv)] if n >= DN_H else [])
                for j in range(DN_TAPS):
                    for o, v in pairs:
                        src = v[:, :, j:j + ROW_W] if o is xo else v[:, j:j + T]
                        tap = cw[:, n, j:j + 1]
                        if j == 0:
                            ins = nc.vector.tensor_scalar(o, src, tap, None, ALU.mult)
                        else:
                            ins = nc.vector.scalar_tensor_tensor(o, src, tap, o, ALU.mult, ALU.add)
                        if j == DN_TAPS - 1 and o is pairs[-1][0]:
                            dn1_dv.mark(ins, ("conv", n))
                        else:
                            c(ins)
            dn1_pe.wait(e, "ba")
            dn1_dv.mark(nc.vector.tensor_copy(ba, PS[:, 0, 0:NQ * 32].rearrange("p (t c) -> p t c", t=NQ)), "ba")
            return dn1_dv

        stage("dn_proj", pool=pool_dn1, pe=pe_dn1, act=act_dn1, dve=dve_dn1)

        masks = idx.rearrange("p a t -> p (a t)")
        MASK = {n: masks[:, i * P:(i + 1) * P]
                for i, n in enumerate(("inc_f", "inc_b", "strict_f", "strict_b", "block", "off"))}
        sq = hT.rearrange("p k t -> p (k t)")[:, 0:1024].rearrange("p (a c) -> p a c", a=2)
        rn = hT.rearrange("p k t -> p (k t)")[:, 1024:2048].rearrange("p (a c) -> p a c", a=2)
        units = [(qT[:, 2 * b:2 * b + 2, :], True) for b in range(4)] + [(kT[:, h, :], False) for h in range(DN_H)]
        NU = len(units)
        dec = arena(8192, 8, NQ, 16)
        beta, g16, Gc, Gtot, eG, ekd, egl, nbeG = [dec[:, j] for j in range(8)]
        scr = arena(8192 + 512, 4, NQ, 16)
        dtb, ala = arena(8192 + 768, 16), arena(8192 + 784, 16)
        s_dn2in = sem("s_dn2in")
        trs = [(w, t, b) for w in ("k", "v") for t in range(NQ) for b in range(2)]
        dn2_pe = steps("pe", ["G"] + [("ss", i) for i in range(NU)] + trs)
        dn2_ac = steps("act", ["beta", "alog", "abs_e", "ln"] + [x for i in range(NU) for x in (("sq", i), ("rt", i))] +
                       ["eG", "ekd", "egl"] + trs[1::2])
        dn2_dv = steps("dve", ["neg", "ln1", "g", "Gc"] + [("unit", i) for i in range(NU)] + ["dec"] + trs[0::2])

        def pool_dn2(e, c):
            for n, m in MASK.items():
                e.dma_start(m, io["const"][:, CAT[n][0]:CAT[n][0] + P]).then_inc(s_dn2in, 16)
            e.dma_start(dtb, io["dn_dt"].unsqueeze(0).broadcast_to([P, 16])).then_inc(s_dn2in, 16)
            e.dma_start(ala, io["dn_alog"].unsqueeze(0).broadcast_to([P, 16])).then_inc(s_dn2in, 16)
            e.wait_ge(s_dn2in, 128)

        def act_dn2(e, c):
            e.wait_ge(s_dn2in, 128)
            dn2_ac.mark(nc.scalar.activation(beta, ba[:, :, 0:16], ACT.Sigmoid), "beta")
            dn2_ac.mark(nc.scalar.activation(ala, ala, ACT.Exp), "alog")
            dn2_dv.wait(e, "neg")
            dn2_ac.mark(nc.scalar.activation(scr[:, 1], scr[:, 1], ACT.Exp), "abs_e")
            dn2_dv.wait(e, "ln1")
            dn2_ac.mark(nc.scalar.activation(scr[:, 1], scr[:, 1], ACT.Ln), "ln")
            for i, (u, _) in enumerate(units):
                if i >= 2:
                    dn2_dv.wait(e, ("unit", i - 2))
                    dn2_pe.wait(e, ("ss", i - 2))
                shape = sq[:, i % 2, :].rearrange("p (a c) -> p a c", a=2) if i < 4 else sq[:, i % 2, :]
                dn2_ac.mark(nc.scalar.activation(shape, u, ACT.Square), ("sq", i))
                dn2_pe.wait(e, ("ss", i))
                dn2_ac.mark(nc.scalar.activation(rn[:, i % 2, :], PS[:, 1 + i % 3, :], ACT.Sqrt, bias=eps_col), ("rt", i))
            dn2_dv.wait(e, "Gc")
            dn2_ac.mark(nc.scalar.activation(eG, Gc, ACT.Exp), "eG")
            dn2_ac.mark(nc.scalar.activation(ekd, ekd, ACT.Exp), "ekd")
            dn2_ac.mark(nc.scalar.activation(egl, Gtot, ACT.Exp), "egl")
            for i, (w, t, b) in list(enumerate(trs))[1::2]:
                dn2_pe.wait(e, (w, t, b))
                dst = (Krow if w == "k" else Vrow)[:, t, 4 * b:4 * b + 4, :]
                dn2_ac.mark(nc.scalar.copy(dst, PS[:, 4 + i % 4, :].rearrange("p (h d) -> p h d", h=4)), (w, t, b))
            return dn2_ac

        def dve_dn2(e, c):
            e.wait_ge(s_dn2in, 128)
            c(nc.vector.tensor_tensor(scr[:, 0], ba[:, :, 16:32], bc(dtb, 1, NQ), ALU.add))
            c(nc.vector.tensor_scalar(scr[:, 2], scr[:, 0], -1.0, None, ALU.mult))
            dn2_dv.mark(nc.vector.tensor_tensor(scr[:, 1], scr[:, 0], scr[:, 2], ALU.min), "neg")
            dn2_ac.wait(e, "abs_e")
            dn2_dv.mark(nc.vector.tensor_scalar_add(scr[:, 1], scr[:, 1], 1.0), "ln1")
            dn2_ac.wait(e, "ln")
            c(nc.vector.scalar_tensor_tensor(scr[:, 1], scr[:, 0], 0.0, scr[:, 1], ALU.max, ALU.add))
            c(nc.vector.tensor_scalar(ala, ala, -1.0, None, ALU.mult))
            dn2_dv.mark(nc.vector.tensor_tensor(g16, scr[:, 1], bc(ala, 1, NQ), ALU.mult), "g")
            dn2_pe.wait(e, "G")
            c(nc.vector.tensor_copy(Gc, PS[:, 0, 0:64].rearrange("p (t c) -> p t c", t=NQ)))
            c(nc.vector.tensor_copy(Gtot, PS[:, 0, 64:128].rearrange("p (t c) -> p t c", t=NQ)))
            dn2_dv.mark(nc.vector.tensor_tensor(ekd, Gtot, Gc, ALU.subtract), "Gc")
            for i, (u, is_q) in enumerate(units):
                dn2_ac.wait(e, ("rt", i))
                c(nc.vector.reciprocal(rn[:, i % 2, :], rn[:, i % 2, :]))
                r = rn[:, i % 2, :]
                if i < 4:
                    r = r.rearrange("p (a c) -> p a c", a=2)
                ins = nc.vector.scalar_tensor_tensor(u, u, float(P) ** -0.5 if is_q else 1.0, r, ALU.mult, ALU.mult)
                dn2_dv.mark(ins, ("unit", i))
            dn2_ac.wait(e, "eG")
            dn2_dv.mark(nc.vector.scalar_tensor_tensor(nbeG, beta, -1.0, eG, ALU.mult, ALU.mult), "dec")
            for i, (w, t, b) in list(enumerate(trs))[0::2]:
                dn2_pe.wait(e, (w, t, b))
                dst = (Krow if w == "k" else Vrow)[:, t, 4 * b:4 * b + 4, :]
                dn2_dv.mark(nc.vector.tensor_copy(dst, PS[:, 4 + i % 4, :].rearrange("p (h d) -> p h d", h=4)), (w, t, b))
            return dn2_dv

        def pe_dn2(e, c):
            dn2_dv.wait(e, "g")
            e.wait_ge(s_dn2in, 128)
            for t in range(NQ):
                for d, m in enumerate(("inc_f", "inc_b")):
                    o = t * 16 + d * 8
                    nc.tensor.matmul(PS[:, 0, o:o + 8], MASK[m], g16[:, t, d * 8:d * 8 + 8], start=True, stop=True)
                ins = nc.tensor.matmul(PS[:, 0, 64 + t * 16:80 + t * 16], ones, g16[:, t, :], start=True, stop=True)
            dn2_pe.mark(ins, "G")
            for i in range(NU):
                dn2_ac.wait(e, ("sq", i))
                if i >= 3:
                    dn2_ac.wait(e, ("rt", i - 3))
                dn2_pe.mark(nc.tensor.matmul(PS[:, 1 + i % 3, :], ones, sq[:, i % 2, :], start=True, stop=True), ("ss", i))
            dn2_dv.wait(e, ("unit", NU - 1))
            for i, (w, t, b) in enumerate(trs):
                if i >= 4:
                    (dn2_dv if i % 2 == 0 else dn2_ac).wait(e, trs[i - 4])
                src = kT if w == "k" else vT
                for h in range(4):
                    ins = nc.tensor.transpose(PS[:, 4 + i % 4, h * P:(h + 1) * P],
                                              src[:, 4 * b + h, t * P:(t + 1) * P], ident)
                dn2_pe.mark(ins, (w, t, b))
            return dn2_pe

        stage("dn_unit", pool=pool_dn2, pe=pe_dn2, act=act_dn2, dve=dve_dn2)

        HG = 4
        NAMES = ("E", "DT", "A", "Aoff", "p0", "p1", "q0", "q1", "t0", "t1", "kb", "vb", "kd", "wT", "qg", "qa")

        def four(base, i):
            return ring[:, base + i * 512:base + (i + 1) * 512].rearrange("p (h c) -> p h c", h=HG)
        buf = [{n: four(SLOT, i) for i, n in enumerate(NAMES)}, {n: four(RB, i) for i, n in enumerate(NAMES)}]
        state = ring[:, 0:2 * DN_H * P].rearrange("p (d h c) -> p d h c", d=2, h=DN_H)
        O = hT.rearrange("p k t -> p (k t)").rearrange("p (t h d) -> p t h d", t=NT, h=DN_H)
        ORDER = [[2, 3, 0, 1], [3, 2, 1, 0]]
        groups = [(st, hg) for st in range(4) for hg in range(DN_H // HG)]
        ROUNDS = 5
        pe_names, ac_names, dv_names = [], [], []
        for gi, (st, hg) in enumerate(groups):
            xt = st >= 2
            pn = ["Gr", "KK"] + (["QK"] if xt else []) + ["A", "q0"]
            for r in range(ROUNDS):
                pn += [("p", r)] + ([("q", r)] if r < ROUNDS - 1 else []) + [("t", r)]
            pn += ["Tb", "Z", "R", "wT", "vn", "ds"] + (["o"] if xt else [])
            an = ["DT"] + (["eG"] if xt else []) + ["q0"] + [("p", r) for r in range(ROUNDS)] + ["Tb", "wT"]
            dn = ["R", "E", "Araw", "A", "p0", "t0"] + (["qx"] if xt else [])
            for r in range(ROUNDS):
                dn += ([("q", r)] if r < ROUNDS - 1 else []) + [("t", r)]
            dn += ["Z", "Tinv", "vn", "s"] + (["o"] if xt else [])
            pe_names += [(gi, n) for n in pn]
            ac_names += [(gi, n) for n in an]
            dv_names += [(gi, n) for n in dn]
        dl_pe = [Steps(sem(f"dl_pe{d}"), pe_names) for d in range(2)]
        dl_ac = [Steps(sem(f"dl_act{d}"), ac_names) for d in range(2)]
        dl_dv = [Steps(sem(f"dl_dve{d}"), dv_names) for d in range(2)]
        BANK = {"Gr": 0, "KK": 1, "QK": 2, "A": 3, "q0": 1, "Tb": 1, "Z": 2, "R": 3, "wT": 1, "vn": 2, "ds": 3, "o": 0}

        def bank(d, name):
            if isinstance(name, tuple):
                b = {"p": 2, "q": 3, "t": 0}[name[0]]
            else:
                b = BANK[name]
            return PS[:, 4 * d + b, :].rearrange("p (h c) -> p h c", h=HG)

        def dl_pe_prog(e, c):
            for gi, (st, hg) in enumerate(groups):
                xt = st >= 2
                heads = [hg * HG + h for h in range(HG)]
                tile = [ORDER[d][st] for d in range(2)]

                def each(name, f, before=()):
                    for d in range(2):
                        for s, n in before:
                            s[d].wait(e, (gi, n))
                        for h in range(HG):
                            ins = f(d, h, bank(d, name)[:, h, :])
                        dl_pe[d].mark(ins, (gi, name))

                def mm(d, o, a, b_):
                    return nc.tensor.matmul(o, a, b_, start=True, stop=True)

                if gi:
                    for d in range(2):
                        last = "o" if groups[gi - 1][0] >= 2 else "s"
                        dl_dv[d].wait(e, (gi - 1, last))
                for d in range(2):
                    dl_dv[d].wait(e, (gi, "R"))
                    dl_pe[d].mark(nc.tensor.matmul(PS[:, 4 * d, :], ones, buf[d]["E"].rearrange("p h c -> p (h c)"),
                                                   start=True, stop=True), (gi, "Gr"))
                tk = [slice(t * P, (t + 1) * P) for t in tile]
                each("KK", lambda d, h, o: mm(d, o, kT[:, heads[h], tk[d]], kT[:, heads[h], tk[d]]))
                if xt:
                    each("QK", lambda d, h, o: mm(d, o, kT[:, heads[h], tk[d]], qT[:, heads[h], tk[d]]))
                each("A", lambda d, h, o: nc.tensor.transpose(o, buf[d]["wT"][:, h, :], ident), [(dl_dv, "Araw")])
                each("q0", lambda d, h, o: nc.tensor.transpose(o, buf[d]["p0"][:, h, :], ident), [(dl_dv, "p0")])
                for r in range(ROUNDS):
                    cur, new = r % 2, 1 - r % 2
                    need = [(dl_ac, "q0"), (dl_dv, "p0")] if r == 0 else [(dl_ac, ("p", r - 1)), (dl_dv, ("q", r - 1))]
                    if r == 0 and xt:
                        need.append((dl_dv, "qx"))
                    each(("p", r), lambda d, h, o: mm(d, o, buf[d][f"q{cur}"][:, h, :], buf[d][f"p{cur}"][:, h, :]), need)
                    if r < ROUNDS - 1:
                        each(("q", r), lambda d, h, o: mm(d, o, buf[d][f"p{cur}"][:, h, :], buf[d][f"q{cur}"][:, h, :]),
                             [(dl_dv, "A")] if r == 0 else [])
                    each(("t", r), lambda d, h, o: mm(d, o, buf[d][f"p{new}"][:, h, :], buf[d][f"t{cur}"][:, h, :]),
                         [(dl_ac, ("p", r)), (dl_dv, "t0" if r == 0 else ("t", r - 1))])
                tl = f"t{ROUNDS % 2}"
                each("Tb", lambda d, h, o: nc.tensor.transpose(o, buf[d][tl][:, h, :], ident), [(dl_dv, ("t", ROUNDS - 1))])
                each("Z", lambda d, h, o: mm(d, o, buf[d]["Aoff"][:, h, :], buf[d][tl][:, h, :]))
                each("R", lambda d, h, o: mm(d, o, buf[d]["q0"][:, h, :], buf[d]["q1"][:, h, :]),
                     [(dl_ac, "Tb"), (dl_dv, "Z")])
                tf = "p0"
                each("wT", lambda d, h, o: mm(d, o, buf[d]["kb"][:, h, :], buf[d][tf][:, h, :]), [(dl_dv, "Tinv")])

                def vn(d, h, o):
                    nc.tensor.matmul(o, buf[d][tf][:, h, :], buf[d]["vb"][:, h, :], start=True, stop=False)
                    return nc.tensor.matmul(o, buf[d]["wT"][:, h, :], state[:, d, heads[h], :], start=False, stop=True)
                each("vn", vn, [(dl_ac, "wT")])
                each("ds", lambda d, h, o: mm(d, o, buf[d]["kd"][:, h, :], buf[d]["A"][:, h, :]), [(dl_dv, "vn")])
                if xt:
                    def out(d, h, o):
                        nc.tensor.matmul(o, buf[d]["qg"][:, h, :], buf[d]["t0"][:, h, :], start=True, stop=False)
                        return nc.tensor.matmul(o, buf[d]["qa"][:, h, :], buf[d]["A"][:, h, :], start=False, stop=True)
                    each("o", out)
            e.wait_ge(dl_pe[0].sem, dl_pe[0].n)
            return dl_pe[1]

        def dl_act_prog(e, c):
            for gi, (st, hg) in enumerate(groups):
                xt = st >= 2
                for d in range(2):
                    dl_dv[d].wait(e, (gi, "E"))
                    dl_ac[d].mark(nc.scalar.activation(buf[d]["DT"], buf[d]["DT"], ACT.Exp), (gi, "DT"))
                    if xt:
                        dl_ac[d].mark(nc.scalar.activation(buf[d]["qg"], bank(d, "Gr"), ACT.Exp), (gi, "eG"))
                for d in range(2):
                    dl_pe[d].wait(e, (gi, "q0"))
                    dl_ac[d].mark(nc.scalar.copy(buf[d]["q0"], bank(d, "q0")), (gi, "q0"))
                for r in range(ROUNDS):
                    new = 1 - r % 2
                    for d in range(2):
                        dl_pe[d].wait(e, (gi, ("p", r)))
                        if r:
                            dl_pe[d].wait(e, (gi, ("t", r - 1)))
                        dl_ac[d].mark(nc.scalar.copy(buf[d][f"p{new}"], bank(d, ("p", r))), (gi, ("p", r)))
                for d in range(2):
                    dl_pe[d].wait(e, (gi, "Tb"))
                    dl_ac[d].mark(nc.scalar.copy(buf[d]["q0"], bank(d, "Tb")), (gi, "Tb"))
                for d in range(2):
                    dl_pe[d].wait(e, (gi, "wT"))
                    dl_ac[d].mark(nc.scalar.copy(buf[d]["wT"], bank(d, "wT")), (gi, "wT"))
            e.wait_ge(dl_ac[0].sem, dl_ac[0].n)
            return dl_ac[1]

        def dl_dve_prog(e, c):
            c(nc.vector.memset(state, 0.0))
            V = nc.vector
            for gi, (st, hg) in enumerate(groups):
                xt = st >= 2
                hs = slice(hg * HG, hg * HG + HG)
                tile = [ORDER[d][st] for d in range(2)]
                col = [slice(d * DN_H + hg * HG, d * DN_H + hg * HG + HG) for d in range(2)]
                fb = "fb"
                for d in range(2):
                    if gi and groups[gi - 1][0] >= 2:
                        dl_pe[d].wait(e, (gi - 1, "o"))
                    dl_dv[d].mark(V.tensor_tensor(buf[d]["E"], bc(MASK["inc_" + fb[d]], 1, HG),
                                                  bc(g16[:, tile[d], col[d]], 2, P), ALU.mult), (gi, "R"))
                    B = buf[d]
                    dec = lambda a: bc(a[:, tile[d], col[d]], 2, P)
                    c(V.tensor_tensor(B["kb"], Krow[:, tile[d], hs, :], dec(nbeG), ALU.mult))
                    c(V.tensor_tensor(B["vb"], Vrow[:, tile[d], hs, :], dec(beta), ALU.mult))
                    c(V.tensor_tensor(B["kd"], Krow[:, tile[d], hs, :], dec(ekd), ALU.mult))
                for d in range(2):
                    dec = lambda a: bc(a[:, tile[d], col[d]], 2, P)
                    dl_pe[d].wait(e, (gi, "Gr"))
                    c(V.tensor_tensor(buf[d]["DT"], bank(d, "Gr"), dec(Gc), ALU.subtract))
                    dl_dv[d].mark(V.tensor_scalar_min(buf[d]["DT"], buf[d]["DT"], 0.0), (gi, "E"))
                for d in range(2):
                    B = buf[d]
                    dl_ac[d].wait(e, (gi, "DT"))
                    c(V.tensor_tensor(B["DT"], B["DT"], bc(MASK["inc_" + fb[d]], 1, HG), ALU.mult))
                    dl_pe[d].wait(e, (gi, "KK"))
                    c(V.tensor_tensor(B["wT"], bank(d, "KK"), B["DT"], ALU.mult))
                    dl_dv[d].mark(V.tensor_tensor(B["wT"], B["wT"], bc(MASK["strict_" + fb[d]], 1, HG), ALU.mult),
                                  (gi, "Araw"))
                for d in range(2):
                    B = buf[d]
                    dl_pe[d].wait(e, (gi, "A"))
                    dl_dv[d].mark(V.tensor_tensor(B["A"], bank(d, "A"), bc(beta[:, tile[d], col[d]], 2, P), ALU.mult),
                                  (gi, "A"))
                    dl_dv[d].wait(e, (gi, "A"))
                    dl_dv[d].mark(V.tensor_tensor(B["p0"], B["A"], bc(MASK["block"], 1, HG), ALU.mult), (gi, "p0"))
                    c(V.tensor_tensor(B["Aoff"], B["A"], bc(MASK["off"], 1, HG), ALU.mult))
                for d in range(2):
                    dl_ac[d].wait(e, (gi, "q0"))
                    dl_dv[d].mark(V.tensor_tensor(buf[d]["t0"], bc(ident, 1, HG), buf[d]["q0"], ALU.subtract),
                                  (gi, "t0"))
                    if xt:
                        dl_ac[d].wait(e, (gi, "eG"))
                        tk = slice(tile[d] * P, tile[d] * P + P)
                        c(V.tensor_tensor(buf[d]["qg"], buf[d]["qg"], qT[:, hs, tk], ALU.mult))
                        dl_dv[d].mark(V.tensor_tensor(buf[d]["qa"], bank(d, "QK"), buf[d]["DT"], ALU.mult), (gi, "qx"))
                for r in range(ROUNDS):
                    cur, new = r % 2, 1 - r % 2
                    for d in range(2):
                        if r < ROUNDS - 1:
                            dl_pe[d].wait(e, (gi, ("q", r)))
                            dl_dv[d].mark(V.tensor_copy(buf[d][f"q{new}"], bank(d, ("q", r))), (gi, ("q", r)))
                    for d in range(2):
                        dl_pe[d].wait(e, (gi, ("t", r)))
                        dl_dv[d].mark(V.tensor_tensor(buf[d][f"t{new}"], buf[d][f"t{cur}"], bank(d, ("t", r)), ALU.add),
                                      (gi, ("t", r)))
                tl = f"t{ROUNDS % 2}"
                for d in range(2):
                    dl_pe[d].wait(e, (gi, "Z"))
                    dl_dv[d].mark(V.tensor_copy(buf[d]["q1"], bank(d, "Z")), (gi, "Z"))
                for d in range(2):
                    dl_pe[d].wait(e, (gi, "R"))
                    dl_dv[d].mark(V.tensor_tensor(buf[d]["p0"], buf[d][tl], bank(d, "R"), ALU.subtract), (gi, "Tinv"))
                    if xt:
                        c(V.tensor_copy(buf[d]["t0"], state[:, d, hs, :]))
                for d in range(2):
                    dl_pe[d].wait(e, (gi, "vn"))
                    dl_dv[d].mark(V.tensor_copy(buf[d]["A"], bank(d, "vn")), (gi, "vn"))
                    c(V.tensor_tensor(state[:, d, hs, :], state[:, d, hs, :], bc(egl[:, tile[d], col[d]], 2, P),
                                      ALU.mult))
                for d in range(2):
                    dl_pe[d].wait(e, (gi, "ds"))
                    dl_dv[d].mark(V.tensor_tensor(state[:, d, hs, :], state[:, d, hs, :], bank(d, "ds"), ALU.add),
                                  (gi, "s"))
                if xt:
                    for d in range(2):
                        dl_pe[d].wait(e, (gi, "o"))
                        o = O[:, tile[d], hs, :]
                        if st == 2:
                            ins = V.tensor_copy(o, bank(d, "o"))
                        else:
                            ins = V.tensor_tensor(o, o, bank(d, "o"), ALU.add)
                        dl_dv[d].mark(ins, (gi, "o"))
            e.wait_ge(dl_dv[0].sem, dl_dv[0].n)
            return dl_dv[1]

        stage("dn_delta", pe=dl_pe_prog, act=dl_act_prog, dve=dl_dve_prog)

        first_wo = out_proj_loads("dn_delta", io["dn_wo"])
        ngb = arena(10240, P)
        osq = arena(10240 + P, 2, DN_H, P)
        s_ng = sem("s_ng")
        dno_dv = steps("dve", ["ss"] + ["y"])
        dno_ac = steps("act", ["rt"])

        def pool_dno(e, c):
            e.dma_start(ngb, io["dn_ng"].unsqueeze(0).broadcast_to([P, P])).then_inc(s_ng, 16)
            e.wait_ge(s_ng, 16)

        def dve_dno(e, c):
            V = nc.vector
            c(V.tensor_tensor(osq, O, O, ALU.mult))
            ss = sm[:, 128:144].rearrange("p (t h) -> p t h", t=NT)
            dno_dv.mark(V.tensor_reduce(ss, osq, AX, ALU.add), "ss")
            e.wait_ge(s_ng, 16)
            g4 = gate.rearrange("p t (h d) -> p (t h) d", h=DN_H)
            c(V.tensor_tensor(g4, g4, bc(ngb, 1, NT * DN_H), ALU.mult))
            dno_ac.wait(e, "rt")
            c(V.reciprocal(sm[:, 128:144], sm[:, 128:144]))
            o16 = O.rearrange("p t h d -> p (t h) d")
            c(V.tensor_tensor(o16, o16, bc(sm[:, 128:144], 2, P), ALU.mult))
            dno_dv.mark(V.tensor_tensor(g4, o16, g4, ALU.mult), "y")
            return dno_dv

        def act_dno(e, c):
            dno_dv.wait(e, "ss")
            dno_ac.mark(nc.scalar.activation(sm[:, 128:144], sm[:, 128:144], ACT.Sqrt, bias=eps_col, scale=1.0 / P), "rt")
            return dno_ac

        stage("dn_gate", pool=pool_dno, dve=dve_dno, act=act_dno)
        out_proj_stage("dn_out", gate, arena(16384, KC, T), first_wo, MOD[:, 2, :], arena(12800, CW))

        first_q = ring_loads(io["peer_wq"], 4)
        norm_T_stage("norm_b", [(X[:, t, :], MOD[:, 4, :], MOD[:, 3, :]) for t in range(NT)], io["norm_g1"], hT, 12288)
        NPH = 2 * PH
        QT = arena(0, NPH, T)
        keysT = arena(4096, NPH, NK)
        S = arena(6144, NT, NPH, NK)
        V1 = arena(10240, NT, NPH, TOPK)
        U1 = arena(10752, NT, NPH, TOPK)
        U1f = arena(11264, NT, NPH, TOPK)
        cand = arena(11776, PH, TOPK, TOPK)
        eqs = arena(13824, PH, TOPK, TOPK)
        TS = arena(15872, NT, PH, TOPK)
        pos = arena(16128, NT, PH, TOPK)
        part = arena(16384, 2, NT, PH, TOPK)
        partf = arena(16896, 2, NT, PH, TOPK)
        sel = arena(17408, 3, NT, PH * TOPK)
        s_pk = sem("s_pk")
        sq_names = [("q", n) for n in range(NPH)]
        ss_names = [("s", t, b) for t in range(NT) for b in range(4)]
        tr_names = [("tr", a) for a in range(3)]
        pq_pe = steps("pe", sq_names + ss_names + tr_names)
        pq_ac = steps("act", ["gt"] + sq_names + ss_names + ["exp"])
        pq_dv = steps("dve", ["max", "sel"] + tr_names)
        for s in range(4):
            free_at[first_q + s] = (pq_pe, ("q", 4 * s + 3))

        def pool_pq(e, c):
            e.dma_start(keysT, io["peer_kT"].rearrange("p (n k) -> p n k", n=NPH)).then_inc(s_pk, 16)
            e.wait_ge(s_pk, 16)

        def pe_pq(e, c):
            for n in range(NPH):
                ring_wait(e, first_q + n // 4)
                if n >= 4:
                    pq_ac.wait(e, ("q", n - 4))
                for k in range(KC):
                    ins = nc.tensor.matmul(PS[:, n % 4, 0:T], slot(first_q + n // 4)[:, k, (n % 4) * P:(n % 4 + 1) * P],
                                           hT[:, k, :], start=(k == 0), stop=(k == KC - 1))
                pq_pe.mark(ins, ("q", n))
            e.wait_ge(s_pk, 16)
            for i, (_, t, b) in enumerate(ss_names):
                pq_ac.wait(e, ("q", NPH - 1) if i < 4 else ss_names[i - 4])
                for n in range(4):
                    ins = nc.tensor.matmul(PS[:, 4 + i % 4, n * NK:(n + 1) * NK], QT[:, 4 * b + n, t * P:(t + 1) * P],
                                           keysT[:, 4 * b + n, :], start=True, stop=True)
                pq_pe.mark(ins, ss_names[i])
            pq_dv.wait(e, "sel")
            for a in range(3):
                for t in range(NT):
                    ins = nc.tensor.transpose(PS[:, a, t * P:(t + 1) * P], sel[:, a, t, :], ident)
                pq_pe.mark(ins, ("tr", a))
            return pq_pe

        def act_pq(e, c):
            pq_ac.mark(nc.scalar.copy(GT, MOD[:, 5, :]), "gt")
            for n in range(NPH):
                pq_pe.wait(e, ("q", n))
                pq_ac.mark(nc.scalar.copy(QT[:, n, :], PS[:, n % 4, 0:T]), ("q", n))
            for i, (_, t, b) in enumerate(ss_names):
                pq_pe.wait(e, ss_names[i])
                pq_ac.mark(nc.scalar.copy(S[:, t, 4 * b:4 * b + 4, :],
                                          PS[:, 4 + i % 4, :].rearrange("p (n k) -> p n k", n=4)), ss_names[i])
            pq_dv.wait(e, "max")
            pq_ac.mark(nc.scalar.activation(sel[:, 2], sel[:, 2], ACT.Exp), "exp")
            return pq_ac

        def dve_pq(e, c):
            V = nc.vector

            def top16(srcs, vals, ids):
                for lo in (0, 8):
                    for s, v in zip(srcs, vals):
                        ins = V.max(v[:, lo:lo + 8], s)
                    c(ins)
                    for s, v, u in zip(srcs, vals, ids):
                        ins = V.max_index(u[:, lo:lo + 8], v[:, lo:lo + 8], s)
                    c(ins)
                    if lo == 0:
                        for s, v in zip(srcs, vals):
                            ins = V.match_replace(s, v[:, 0:8], s, NEG)
                        c(ins)
            Uu = U1.bitcast(U32)
            for t in range(NT):
                pq_ac.wait(e, ("s", t, 3))
                top16([S[:, t, n, :] for n in range(NPH)], [V1[:, t, n, :] for n in range(NPH)],
                      [Uu[:, t, n, :] for n in range(NPH)])
            c(V.tensor_copy(U1f, Uu))
            posu, partu = pos.bitcast(U32), part.bitcast(U32)
            V1h = V1.rearrange("p t (h a) k -> p t h a k", a=2)
            U1h = U1f.rearrange("p t (h a) k -> p t h a k", a=2)
            for t in range(NT):
                c(V.tensor_tensor(cand, bc(V1h[:, t, :, 0, :], 3, TOPK), bc(V1h[:, t, :, 1, :], 2, TOPK), ALU.add))
                flat = cand.rearrange("p h a b -> p h (a b)")
                top16([flat[:, h, :] for h in range(PH)], [TS[:, t, h, :] for h in range(PH)],
                      [posu[:, t, h, :] for h in range(PH)])
            c(V.tensor_scalar(partu[:, 0], posu, 4, None, ALU.logical_shift_right))
            c(V.tensor_scalar(partu[:, 1], posu, TOPK - 1, None, ALU.bitwise_and))
            c(V.tensor_copy(partf, partu))
            g = sel[:, 2].rearrange("p t (h k) -> p t h k", h=PH)
            for t in range(NT):
                ins = V.tensor_tensor(g[:, t], TS[:, t], TS[:, t, :, 0:1].broadcast_to([P, PH, TOPK]), ALU.subtract)
            pq_dv.mark(ins, "max")
            for t in range(NT):
                for a in range(2):
                    c(V.tensor_tensor(eqs, bc(partf[:, a, t], 3, TOPK),
                                      iota[:, 0:TOPK].unsqueeze(1).unsqueeze(1).broadcast_to([P, PH, TOPK, TOPK]),
                                      ALU.is_equal))
                    c(V.tensor_tensor(eqs, eqs, bc(U1h[:, t, :, a, :], 2, TOPK), ALU.mult))
                    c(V.tensor_reduce(sel[:, a, t, :].rearrange("p (h k) -> p h k", h=PH), eqs, AX, ALU.add))
            pq_ac.wait(e, "exp")
            g16v = sel[:, 2].rearrange("p t (h k) -> p (t h) k", h=PH)
            c(V.tensor_reduce(sm[:, 144:160], g16v, AX, ALU.add))
            c(V.reciprocal(sm[:, 144:160], sm[:, 144:160]))
            pq_dv.mark(V.tensor_tensor(g16v, g16v, bc(sm[:, 144:160], 2, TOPK), ALU.mult), "sel")
            for a in range(3):
                pq_pe.wait(e, ("tr", a))
                pq_dv.mark(V.tensor_copy(idx[:, a, :], PS[:, a, 0:T]), ("tr", a))
            return pq_dv

        stage("peer_route", pool=pool_pq, pe=pe_pq, act=act_pq, dve=dve_pq)

        G = arena(0, NK, T)
        GQ = 4
        hotA = ring[:, 8192:8192 + 1024].rearrange("p (b q k) -> p b q k", b=2, q=GQ)
        hotB = ring[:, 9216:9216 + 1024].rearrange("p (b q k) -> p b q k", b=2, q=GQ)
        s_hot, s_gmm, s_gev = sem("s_hot"), sem("s_gmm"), sem("s_gev")
        NG2 = T // GQ // 2

        def groups_loop(e, body):
            for b in range(2):
                body(b, b, True)
            with e.Fori(1, NG2) as i:
                for b in range(2):
                    body(i * 2 + b, b, False)

        def dve_g(e, c):
            def body(n, b, first):
                if not first:
                    e.wait_ge(s_gmm, n - 1)
                nc.vector.tensor_tensor(hotA[:, b], bc(iota, 1, GQ), bc(idx[:, 0, bass.ds(n * GQ, GQ)], 2, P),
                                        ALU.is_equal)
                for q in range(GQ):
                    t = n * GQ + q
                    ins = nc.vector.tensor_scalar(hotB[:, b, q, :], iota, idx[:, 1, bass.ds(t, 1)],
                                                  idx[:, 2, bass.ds(t, 1)], ALU.is_equal, ALU.mult)
                ins.then_inc(s_hot, 1)
            groups_loop(e, body)
            e.wait_ge(s_hot, 2 * NG2)

        def pe_g(e, c):
            def body(n, b, first):
                e.wait_ge(s_hot, n + 1)
                if not first:
                    e.wait_ge(s_gev, n - 1)
                for q in range(GQ):
                    ins = nc.tensor.matmul(PS[:, b, q * NK:(q + 1) * NK], hotA[:, b, q, :], hotB[:, b, q, :],
                                           start=True, stop=True)
                ins.then_inc(s_gmm, 1)
            groups_loop(e, body)
            e.wait_ge(s_gmm, 2 * NG2)

        def act_g(e, c):
            def body(n, b, first):
                e.wait_ge(s_gmm, n + 1)
                nc.scalar.copy(G[:, :, bass.ds(n * GQ, GQ)].rearrange("p j q -> p q j"),
                               PS[:, b, :].rearrange("p (q j) -> p q j", q=GQ)).then_inc(s_gev, 1)
            groups_loop(e, body)
            e.wait_ge(s_gev, 2 * NG2)

        stage("peer_weights", dve=dve_g, pe=pe_g, act=act_g)

        NPART = 2 * NK
        PW = KC * P
        PRAW = [ring[:, q * PW:(q + 1) * PW] for q in range(4)]
        PSPL = [r32(4 * PW + q * 2 * PW, 2, PW) for q in range(4)]
        xs_hi, xs_hi32 = r32(X_at, KC, T)
        xs_lo, _ = r32(hT_at, KC, T)
        act_h = ring[:, spare_at:spare_at + 2 * T].rearrange("p (b t) -> p b t", b=2)
        coef, coef32 = r32(spare_at + 2 * T, 2, 2, T)
        x_home = nc.dram_tensor("x_home", (P, NT * D), F32).ap()
        p_ld = [sem(f"p_ld{q}") for q in range(4)]
        s_px, s_hi, s_lo, s_use = sem("p_x"), sem("p_hi"), sem("p_lo"), sem("p_use")
        s_gelu, s_coef, s_chi, s_xhi, s_xlo = sem("p_gelu"), sem("p_coef"), sem("p_chi"), sem("p_xhi"), sem("p_xlo")
        s_cs = sem("p_cs")
        PEEL = 3

        def pairs(e, body):
            for m in range(PEEL):
                body(m, 2 * m + 1, m)
            with e.Fori(0, (NK - 1 - PEEL) // 4) as i:
                for q in range(4):
                    body(i * 4 + (PEEL + q), i * 8 + (2 * (PEEL + q) + 1), 4 + PEEL + q)

        def load_peer(sp):
            for n in range(first_q + 1, first_q + 4):
                free_at[n][0].wait(sp, free_at[n][1])

            def part(src, n, s, turn):
                if s >= 4:
                    sp.wait_ge(s_lo, n - 3)
                sp.dma_start(PRAW[s % 4], src).then_inc(p_ld[s % 4], 16)
            part(io["peer_u"][0], 0, 0, 0)

            def body(m, n, mm):
                s = 2 * mm + 1
                part(io["peer_u"][m + 1], n, s, 0)
                part(io["peer_v"][:, m, :], n + 1, s + 1, 0)
            pairs(sp, body)
            part(io["peer_v"][:, NK - 1, :], NPART - 1, NPART - 1, 0)
        stream.append(load_peer)

        def ld_wait(e, n, s):
            if isinstance(n, int):
                e.wait_ge(p_ld[n % 4], 16 * (n // 4 + 1))
            else:
                e.wait_ge(p_ld[s % 4], n * 4 + (16 - 4 * (s % 4)))

        def pool_x(e, c):
            e.dma_start(x_home, X.rearrange("p t d -> p (t d)")).then_inc(s_px, 16)
            e.wait_ge(s_px, 16)

        def act_x(e, c):
            def hi(n, s):
                ld_wait(e, n, s)
                if s >= 4:
                    e.wait_ge(s_use, n - 3)
                nc.scalar.copy(PSPL[s % 4][0][:, 0, :], PRAW[s % 4]).then_inc(s_hi, 1)

            def gelu(m, mm):
                e.wait_ge(s_use, 1 if mm == 0 else m * 2)
                if mm >= 2:
                    e.wait_ge(s_coef, m - 1)
                nc.scalar.activation(act_h[:, mm % 2, :], PS[:, mm % 2, 0:T], ACT.Gelu).then_inc(s_gelu, 1)
            e.wait_ge(s_px, 16)
            nc.scalar.copy(xs_hi, hT).then_inc(s_xhi, 1)
            hi(0, 0)

            def body(m, n, mm):
                s = 2 * mm + 1
                hi(n, s)
                hi(n + 1, s + 1)
                gelu(m, mm)
            pairs(e, body)
            hi(NPART - 1, NPART - 1)
            gelu(NK - 1, NK - 1)
            e.wait_ge(s_gelu, NK)

        def dve_x(e, c):
            V = nc.vector

            def lo(n, s):
                e.wait_ge(s_hi, n + 1)
                V.tensor_tensor(PSPL[s % 4][0][:, 1, :], PRAW[s % 4], PSPL[s % 4][1][:, 0, :],
                                ALU.subtract).then_inc(s_lo, 1)

            def coefs(m, mm):
                b = mm % 2
                e.wait_ge(s_gelu, m + 1)
                V.tensor_tensor(act_h[:, b, :], act_h[:, b, :], G[:, bass.ds(m, 1), :].rearrange("p a t -> p (a t)"),
                                ALU.mult).then_inc(s_cs, 1)
                e.wait_ge(s_cs, m + 1)
                if mm >= 2:
                    e.wait_ge(s_use, m * 2 - 1)
                V.tensor_copy(coef[:, b, 0, :], act_h[:, b, :]).then_inc(s_chi, 1)
                e.wait_ge(s_chi, m + 1)
                V.tensor_tensor(coef[:, b, 1, :], act_h[:, b, :], coef32[:, b, 0, :], ALU.subtract).then_inc(s_coef, 1)
            e.wait_ge(s_xhi, 1)
            V.tensor_tensor(xs_lo, hT, xs_hi32, ALU.subtract).then_inc(s_xlo, 1)
            lo(0, 0)

            def body(m, n, mm):
                s = 2 * mm + 1
                lo(n, s)
                lo(n + 1, s + 1)
                coefs(m, mm)
            pairs(e, body)
            lo(NPART - 1, NPART - 1)
            coefs(NK - 1, NK - 1)
            e.wait_ge(s_coef, NK)

        def pe_x(e, c):
            def hid(j, n, s, jj):
                e.wait_ge(s_lo, n + 1)
                if jj >= 2:
                    e.wait_ge(s_gelu, j - 1)
                w = PSPL[s % 4][0].rearrange("p h (k e) -> p h k e", k=KC)
                for k in range(KC):
                    ins = exact3(PS[:, jj % 2, 0:T], (w[:, 0, k, :], w[:, 1, k, :]), (xs_hi[:, k, :], xs_lo[:, k, :]),
                                 k == 0, k == KC - 1)
                ins.then_inc(s_use, 1)

            def y(m, n, s, mm, start=False, stop=False):
                e.wait_ge(s_lo, n + 1)
                e.wait_ge(s_coef, m + 1)
                v, cf = PSPL[s % 4][0], coef[:, mm % 2]
                for t in range(NT):
                    for h in range(2):
                        cols, tk = slice(h * CW, (h + 1) * CW), slice(t * P, (t + 1) * P)
                        ins = exact3(PS[:, 4 + 2 * t + h, :], (cf[:, 0, tk], cf[:, 1, tk]), (v[:, 0, cols], v[:, 1, cols]),
                                     start, stop)
                ins.then_inc(s_use, 1)
            e.wait_ge(s_xlo, 1)
            hid(0, 0, 0, 0)

            def body(m, n, mm):
                hid(m + 1, n, 2 * mm + 1, mm + 1)
                y(m, n + 1, 2 * mm + 2, mm, start=mm == 0)
            pairs(e, body)
            y(NK - 1, NPART - 1, NPART - 1, NK - 1, stop=True)
            e.wait_ge(s_use, NPART)

        stage("peer_experts", pool=pool_x, pe=pe_x, act=act_x, dve=dve_x)

        def pool_back(e, c):
            e.dma_start(X.rearrange("p t d -> p (t d)"), x_home).then_inc(s_px, 16)
            e.wait_ge(s_px, 32)
        stage("x_back", pool=pool_back)

        def add_norm_stage(tag, gain, g_dram, off):
            tmp, gb, sq2 = arena(off, 2, CW), arena(off + D, D), arena(off + 2 * D, D)
            s_in = sem(f"{tag}_in")
            dv_s = steps("dve", [("add", t) for t in range(NT)] +
                         ([("n", t) for t in range(NT)] if g_dram is not None else []))
            ac_s = steps("act", [x for t in range(NT) for x in (("ss", t), ("rt", t))] if g_dram is not None else [])

            def dve(e, c):
                for t in range(NT):
                    for h in range(2):
                        cols = slice(h * CW, (h + 1) * CW)
                        c(nc.vector.tensor_tensor(tmp[:, h, :], PS[:, 4 + 2 * t + h, :], gain[:, cols], ALU.mult))
                        ins = nc.vector.tensor_tensor(X[:, t, cols], X[:, t, cols], tmp[:, h, :], ALU.add)
                        if h == 0:
                            c(ins)
                    dv_s.mark(ins, ("add", t))
                if g_dram is None:
                    return dv_s
                e.wait_ge(s_in, 16)
                for t in range(NT):
                    ac_s.wait(e, ("rt", t))
                    c(nc.vector.reciprocal(sm[:, 16 + t:17 + t], sm[:, 8 + t:9 + t]))
                    dv_s.mark(nc.vector.scalar_tensor_tensor(X[:, t, :], X[:, t, :], sm[:, 16 + t:17 + t], gb,
                                                             ALU.mult, ALU.mult), ("n", t))
                return dv_s

            def act(e, c):
                for t in range(NT):
                    dv_s.wait(e, ("add", t))
                    if t:
                        ac_s.wait(e, ("ss", t - 1))
                    ac_s.mark(nc.scalar.activation(sq2, X[:, t, :], ACT.Square, accum_out=sm[:, t:t + 1]), ("ss", t))
                    ac_s.wait(e, ("ss", t))
                    ac_s.mark(nc.scalar.activation(sm[:, 8 + t:9 + t], sm[:, t:t + 1], ACT.Sqrt, bias=eps_col,
                                                   scale=1.0 / D), ("rt", t))
                return ac_s

            def pool(e, c):
                e.dma_start(gb, g_dram.unsqueeze(0).broadcast_to([P, D])).then_inc(s_in, 16)
                e.wait_ge(s_in, 16)
            if g_dram is None:
                stage(tag, dve=dve)
            else:
                stage(tag, dve=dve, act=act, pool=pool)

        add_norm_stage("peer_out", GT, io["final_g"], 0)

        NSEG = 3
        SEG = ((0, 0), (0, 1), (1, 1))

        def release_ring(after):
            k = [s[0] for s in stages].index(after) + 1
            stream.append(lambda sp: sp.wait_ge(s_bar, 4 * k))

        for layer in range(LAYERS):
            L = f"l{layer}_"
            release_ring("peer_experts" if layer == 0 else "l0_experts")
            ada_stage(L + "ada", io[f"ada_w{layer}"], io[f"ada_b{layer}"], io["c2"])
            first_in = ring_loads(io[f"w_in{layer}"], 8)
            norm_T_stage(L + "norm_mix", [(X[:, t, :], MOD[:, 1, :], MOD[:, 0, :]) for t in range(NT)],
                         io[f"ng_mix{layer}"], hT, 12288)

            mcn = ("lev_mask", "lev_sum", "cos", "sin", "ret_decay", "inc_f")
            mc_at, off = {}, 0
            for n in mcn:
                mc_at[n] = off
                off += CAT[n][1]
            lev_mask = arena(mc_at["lev_mask"], LEVELS + 1, P)
            lev_sum = arena(mc_at["lev_sum"], LEVELS + 2, P)
            cos, sin = arena(mc_at["cos"], T), arena(mc_at["sin"], T)
            ret_decay = arena(mc_at["ret_decay"], RE_H, NSEG, P)
            inc = arena(mc_at["inc_f"], P)
            XBCp, XBC = arena(4352, 6, TAPS2 - 1 + T), arena(5920, 6, T)
            hqT, kinT = arena(7456, 2, T), arena(7968, 2, T)
            RT, rot = arena(8480, 8, T), arena(10528, 4, T)
            zrow, logf, hi = arena(11552, NT, 512), arena(12576, NT, T), arena(13088, NT, T)
            hg, rv, rg = arena(13600, NT, T), arena(14112, NT, T), arena(14624, NT, T)
            dtr, g8, Gc8 = arena(15136, NT, 8), arena(15152, NT, 8), arena(15168, NT, 8)
            spar, sscr = arena(15200, 3, 8), arena(15224, 3, NT, 8)
            ngs, lb, oml, ngh = arena(15400, 512), arena(15912, T + 2), arena(16170, T + 2), arena(16432, T)
            cw2, wdt = arena(16690, 6, TAPS2 + 1), arena(16724, KC, 8)
            xs, xdt = arena(16820, NT, 512), arena(17844, NT, 512)
            WS = arena(18868, SSD_H, NSEG, P)
            EX = arena(21940, 4, LEVELS + 1, P)
            Rg = arena(21940, SSD_H, NSEG, P)
            mtmp = arena(26036, HG_H, P)
            WH, WR = arena(8480, HG_H, NSEG, P), arena(4352, RE_H, NSEG, P)
            lbr = arena(18868, 2, T + 2)
            lbs2 = arena(18868 + 2 * (T + 2), T + 2)
            MIX = hT.rearrange("p k t -> p (k t)").rearrange("p (t d) -> p t d", t=NT)

            def proj(L=L, layer=layer, first_in=first_in):
                s_in = sem(L + "proj_in")
                pairs = [("T", i) for i in range(9)]
                rows = [("r", j, t) for j in range(4) for t in range(NT)]
                pe_s = steps("pe", pairs + rows + ["dt"])
                ac_s = steps("act", ["lbe", "alog"] + pairs + rows + ["conv", "dte", "ln", "logf"])
                dv_s = steps("dve", ["lb0", "lb", "conv", "dt0", "dt1", "logf0", "done"])
                for s in range(4):
                    free_at[first_in + s] = (pe_s, ("T", 2 * s + 1))
                for s in range(4):
                    free_at[first_in + 4 + s] = (pe_s, ("r", s, NT - 1))

                def pool(e, c):
                    n = 0

                    def load(dst, src):
                        e.dma_start(dst, src).then_inc(s_in, 16)
                        return 1

                    def row(a, k):
                        return a.unsqueeze(0).broadcast_to([P, k])
                    n += load(lbr[:, :, 0:T], io["lbs"].unsqueeze(0).broadcast_to([P, 2, T]))
                    n += load(lbr[:, :, T:T + 2], io["lbsT"].rearrange("p (a b) -> p a b", a=2))
                    n += load(cw2, io[f"conv{layer}"].rearrange("p (a b) -> p a b", a=6))
                    n += load(wdt, io[f"w_dt{layer}"].rearrange("p (a b) -> p a b", a=KC))
                    n += load(spar.rearrange("p a b -> p (a b)"), row(io[f"ssd{layer}"], 24))
                    n += load(ngs, row(io[f"ng_ssd{layer}"], 512))
                    n += load(ngh, row(io[f"ng_hgrn{layer}"], T))
                    for m in mcn:
                        n += load(arena(mc_at[m], CAT[m][1]), io["const"][:, CAT[m][0]:CAT[m][0] + CAT[m][1]])
                    assert n == 13
                    e.wait_ge(s_in, 16 * n)

                def pe(e, c):
                    for i in range(9):
                        s = i // 2
                        ring_wait(e, first_in + s)
                        if i >= 4:
                            ac_s.wait(e, ("T", i - 4))
                        for a in range(2):
                            ct = (2 * i + a) % 4
                            for k in range(KC):
                                ins = nc.tensor.matmul(PS[:, i % 4, a * T:(a + 1) * T],
                                                       slot(first_in + s)[:, k, ct * P:(ct + 1) * P], hT[:, k, :],
                                                       start=(k == 0), stop=(k == KC - 1))
                        pe_s.mark(ins, ("T", i))
                    for u, (_, j, t) in enumerate(rows):
                        ring_wait(e, first_in + 4 + j)
                        if u >= 4:
                            ac_s.wait(e, rows[u - 4])
                        lo = T if j == 0 else 0
                        for k in range(KC):
                            ins = nc.tensor.matmul(PS[:, 4 + u % 4, lo:CW], hT[:, k, t * P:(t + 1) * P],
                                                   slot(first_in + 4 + j)[:, k, lo:CW], start=(k == 0), stop=(k == KC - 1))
                        pe_s.mark(ins, rows[u])
                    e.wait_ge(s_in, 16 * 13)
                    ac_s.wait(e, ("T", 8))
                    for t in range(NT):
                        for k in range(KC):
                            ins = nc.tensor.matmul(PS[:, 0, t * 8:t * 8 + 8], hT[:, k, t * P:(t + 1) * P], wdt[:, k, :],
                                                   start=(k == 0), stop=(k == KC - 1))
                    pe_s.mark(ins, "dt")
                    return pe_s

                def act(e, c):
                    A = nc.scalar
                    dv_s.wait(e, "lb0")
                    ac_s.mark(A.activation(lbr, lbr, ACT.Exp), "lbe")
                    ac_s.mark(A.activation(spar[:, 1], spar[:, 1], ACT.Exp), "alog")
                    for i in range(9):
                        pe_s.wait(e, ("T", i))
                        src = PS[:, i % 4, :].rearrange("p (a t) -> p a t", a=2)
                        if i < 3:
                            ins = A.copy(XBCp[:, 2 * i:2 * i + 2, TAPS2 - 1:], src)
                        elif i == 3:
                            ins = A.copy(hqT, src)
                        elif i == 4:
                            ins = A.activation(kinT, src, ACT.Sigmoid)
                        else:
                            ins = A.copy(RT[:, 2 * i - 10:2 * i - 8, :], src)
                        ac_s.mark(ins, ("T", i))
                    for u, (_, j, t) in enumerate(rows):
                        pe_s.wait(e, rows[u])
                        b = PS[:, 4 + u % 4, :]
                        if j == 0:
                            ins = A.activation(logf[:, t, :], b[:, T:CW], ACT.Sigmoid)
                        elif j == 1:
                            ins = A.activation(zrow[:, t, :], b, ACT.Silu)
                        elif j == 2:
                            A.copy(hi[:, t, :], b[:, 0:T])
                            ins = A.activation(hg[:, t, :], b[:, T:CW], ACT.Sigmoid)
                        else:
                            A.copy(rv[:, t, :], b[:, 0:T])
                            ins = A.activation(rg[:, t, :], b[:, T:CW], ACT.Silu)
                        ac_s.mark(ins, rows[u])
                    dv_s.wait(e, "conv")
                    ac_s.mark(A.activation(XBC, XBC, ACT.Silu), "conv")
                    dv_s.wait(e, "dt0")
                    ac_s.mark(A.activation(sscr[:, 1], sscr[:, 1], ACT.Exp), "dte")
                    dv_s.wait(e, "dt1")
                    ac_s.mark(A.activation(sscr[:, 1], sscr[:, 1], ACT.Ln), "ln")
                    dv_s.wait(e, "logf0")
                    ac_s.mark(A.activation(logf, logf, ACT.Ln), "logf")
                    return ac_s

                def dve(e, c):
                    V = nc.vector
                    c(V.memset(XBCp[:, :, 0:TAPS2 - 1], 0.0))
                    e.wait_ge(s_in, 16 * 13)
                    c(V.tensor_tensor(lbs2, lbr[:, 0], lbr[:, 1], ALU.max))
                    dv_s.mark(V.tensor_tensor(lbr, lbr, bc(lbs2, 1, 2), ALU.subtract), "lb0")
                    ac_s.wait(e, "lbe")
                    c(V.tensor_tensor(lbs2, lbr[:, 0], lbr[:, 1], ALU.add))
                    c(V.reciprocal(lbs2, lbs2))
                    c(V.tensor_tensor(lbr, lbr, bc(lbs2, 1, 2), ALU.mult))
                    if layer == 0:
                        c(V.tensor_tensor(lb, lbr[:, 0], lbr[:, 0], ALU.subtract))
                    else:
                        c(V.tensor_tensor(lb, lbr[:, 0], lbr[:, 1], ALU.add))
                        c(V.tensor_tensor(lb, lb, lbr[:, 0], ALU.subtract))
                    dv_s.mark(V.tensor_scalar(oml, lb, -1.0, 1.0, ALU.mult, ALU.add), "lb")
                    dv_s.wait(e, "lb")
                    ac_s.wait(e, ("T", 2))
                    for n in range(6):
                        for j in range(TAPS2):
                            if j == 0:
                                ins = V.tensor_scalar(XBC[:, n, :], XBCp[:, n, 0:T], cw2[:, n, 0:1],
                                                      cw2[:, n, TAPS2:TAPS2 + 1], ALU.mult, ALU.add)
                            else:
                                ins = V.scalar_tensor_tensor(XBC[:, n, :], XBCp[:, n, j:j + T], cw2[:, n, j:j + 1],
                                                             XBC[:, n, :], ALU.mult, ALU.add)
                            if (n, j) == (5, TAPS2 - 1):
                                dv_s.mark(ins, "conv")
                            else:
                                c(ins)
                    ac_s.wait(e, ("T", 4))
                    for a in range(2):
                        c(V.tensor_scalar(kinT[:, a, :], kinT[:, a, :], oml[:, T + a:T + a + 1], lb[:, T + a:T + a + 1],
                                          ALU.mult, ALU.add))
                    c(V.tensor_scalar(kinT, kinT, -1.0, 1.0, ALU.mult, ALU.add))
                    ac_s.wait(e, ("T", 8))
                    c(V.tensor_tensor(rot, RT[:, 0:4, :], bc(cos, 1, 4), ALU.mult))
                    c(V.tensor_tensor(RT[:, 4:8, :], RT[:, 4:8, :], bc(sin, 1, 4), ALU.mult))
                    c(V.tensor_tensor(rot, rot, RT[:, 4:8, :], ALU.add))
                    c(V.tensor_scalar(rot[:, 2:4, :], rot[:, 2:4, :], float(HD) ** -0.5, None, ALU.mult))
                    pe_s.wait(e, "dt")
                    c(V.tensor_tensor(sscr[:, 0], PS[:, 0, 0:16].rearrange("p (t h) -> p t h", t=NT),
                                      bc(spar[:, 0], 1, NT), ALU.add))
                    c(V.tensor_scalar(sscr[:, 2], sscr[:, 0], -1.0, None, ALU.mult))
                    dv_s.mark(V.tensor_tensor(sscr[:, 1], sscr[:, 0], sscr[:, 2], ALU.min), "dt0")
                    ac_s.wait(e, "dte")
                    dv_s.mark(V.tensor_scalar_add(sscr[:, 1], sscr[:, 1], 1.0), "dt1")
                    ac_s.wait(e, ("r", 0, NT - 1))
                    c(V.tensor_tensor(logf, logf, bc(oml[:, 0:T], 1, NT), ALU.mult))
                    c(V.tensor_tensor(logf, logf, bc(lb[:, 0:T], 1, NT), ALU.add))
                    dv_s.mark(V.tensor_scalar_max(logf, logf, GATE_FLOOR), "logf0")
                    ac_s.wait(e, "ln")
                    c(V.scalar_tensor_tensor(dtr, sscr[:, 0], 0.0, sscr[:, 1], ALU.max, ALU.add))
                    c(V.tensor_scalar(spar[:, 1], spar[:, 1], -1.0, None, ALU.mult))
                    dv_s.mark(V.tensor_tensor(g8, dtr, bc(spar[:, 1], 1, NT), ALU.mult), "done")
                    return dv_s

                stage(L + "proj", pool=pool, pe=pe, act=act, dve=dve)
            proj()

            def value_products(W, val, bank, heads, width):
                for h in range(heads):
                    cols = slice(h * HD, (h + 1) * HD)
                    nc.tensor.matmul(PS[:, bank, cols], W[:, h, 0, :], val[:, 0, cols], start=True, stop=True)
                    nc.tensor.matmul(PS[:, bank + 1, cols], W[:, h, 1, :], val[:, 0, cols], start=True, stop=False)
                    ins = nc.tensor.matmul(PS[:, bank + 1, cols], W[:, h, 2, :], val[:, 1, cols], start=False, stop=True)
                return ins

            def score_products(bank, k, q):
                nc.tensor.matmul(PS[:, bank, 0:T], k[:, 0:P], q, start=True, stop=True)
                return nc.tensor.matmul(PS[:, bank, T:TRI], k[:, P:T], q[:, P:T], start=True, stop=True)

            def ssd(L=L):
                pe_s = steps("pe", ["xs", "Gc", "CB", "Gr", "o"])
                dv_s = steps("dve", ["xs", "R", "E", "W", "o"])
                ac_s = steps("act", ["exp"])
                GRB = (0, 1, 5, 6)

                def pe(e, c):
                    for t in range(NT):
                        for n in range(4):
                            ins = nc.tensor.transpose(PS[:, t, n * P:(n + 1) * P], XBC[:, n, t * P:(t + 1) * P], ident)
                    pe_s.mark(ins, "xs")
                    nc.tensor.matmul(PS[:, 2, 0:8], inc, g8[:, 0, :], start=True, stop=True)
                    nc.tensor.matmul(PS[:, 2, 8:16], ones, g8[:, 0, :], start=True, stop=False)
                    pe_s.mark(nc.tensor.matmul(PS[:, 2, 8:16], inc, g8[:, 1, :], start=False, stop=True), "Gc")
                    for g in range(2):
                        rows = slice(g * HD, (g + 1) * HD)
                        ins = score_products(3 + g, XBC[rows, 4, :], XBC[rows, 5, :])
                    pe_s.mark(ins, "CB")
                    dv_s.wait(e, "xs")
                    dv_s.wait(e, "R")
                    for h in range(SSD_H):
                        o = PS[:, GRB[h // 2], (h % 2) * T:(h % 2) * T + T]
                        nc.tensor.matmul(o[:, 0:P], ones, Rg[:, h, 0, :], start=True, stop=True)
                        nc.tensor.matmul(o[:, P:T], ones, Rg[:, h, 1, :], start=True, stop=False)
                        ins = nc.tensor.matmul(o[:, P:T], ones, Rg[:, h, 2, :], start=False, stop=True)
                    pe_s.mark(ins, "Gr")
                    dv_s.wait(e, "W")
                    pe_s.mark(value_products(WS, xdt, 0, SSD_H, 512), "o")
                    return pe_s

                def act(e, c):
                    dv_s.wait(e, "E")
                    ac_s.mark(nc.scalar.activation(WS, WS, ACT.Exp), "exp")
                    return ac_s

                def dve(e, c):
                    V = nc.vector
                    c(V.tensor_tensor(Rg[:, :, 0, :], bc(inc, 1, SSD_H), bc(g8[:, 0, :], 2, P), ALU.mult))
                    c(V.tensor_copy(Rg[:, :, 1, :], bc(g8[:, 0, :], 2, P)))
                    c(V.tensor_tensor(Rg[:, :, 2, :], bc(inc, 1, SSD_H), bc(g8[:, 1, :], 2, P), ALU.mult))
                    pe_s.wait(e, "xs")
                    for t in range(NT):
                        ins = V.tensor_copy(xs[:, t, :], PS[:, t, :])
                    dv_s.mark(ins, "xs")
                    dv_s.wait(e, "xs")
                    for t in range(NT):
                        c(V.tensor_tensor(xdt[:, t, :].rearrange("p (h d) -> p h d", h=SSD_H),
                                          xs[:, t, :].rearrange("p (h d) -> p h d", h=SSD_H),
                                          bc(dtr[:, t, :], 2, HD), ALU.mult))
                    pe_s.wait(e, "Gc")
                    dv_s.mark(V.tensor_copy(Gc8, PS[:, 2, 0:16].rearrange("p (t h) -> p t h", t=NT)), "R")
                    dv_s.wait(e, "R")
                    pe_s.wait(e, "Gr")
                    for h in range(SSD_H):
                        o = PS[:, GRB[h // 2], (h % 2) * T:(h % 2) * T + T]
                        V.tensor_scalar(WS[:, h, 0:2, :].rearrange("p a t -> p (a t)"), o, Gc8[:, 0, h:h + 1], 0.0,
                                        ALU.subtract, ALU.min)
                        ins = V.tensor_scalar(WS[:, h, 2, :], o[:, P:T], Gc8[:, 1, h:h + 1], 0.0, ALU.subtract, ALU.min)
                    dv_s.mark(ins, "E")
                    ac_s.wait(e, "exp")
                    for s in (0, 2):
                        c(V.tensor_tensor(WS[:, :, s, :], WS[:, :, s, :], bc(inc, 1, SSD_H), ALU.mult))
                    pe_s.wait(e, "CB")
                    for g in range(2):
                        w = WS[:, 4 * g:4 * g + 4].rearrange("p h a t -> p h (a t)")
                        ins = V.tensor_tensor(w, w, bc(PS[:, 3 + g, 0:TRI], 1, 4), ALU.mult)
                    dv_s.mark(ins, "W")
                    for t in range(NT):
                        m = MIX[:, t, 0:512].rearrange("p (h d) -> p h d", h=SSD_H)
                        c(V.tensor_tensor(m, xs[:, t, :].rearrange("p (h d) -> p h d", h=SSD_H), bc(spar[:, 2], 2, HD),
                                          ALU.mult))
                    pe_s.wait(e, "o")
                    for t in range(NT):
                        c(V.tensor_tensor(MIX[:, t, 0:512], MIX[:, t, 0:512], PS[:, t, :], ALU.add))
                        ins = V.tensor_tensor(MIX[:, t, 0:512], MIX[:, t, 0:512], zrow[:, t, :], ALU.mult)
                        if t == 0:
                            c(ins)
                    dv_s.mark(ins, "o")
                    return dv_s
                stage(L + "ssd", pe=pe, act=act, dve=dve)
            ssd()

            def ret(L=L):
                pe_s = steps("pe", ["qk", "o"])
                dv_s = steps("dve", ["W", "o"])

                def pe(e, c):
                    for h in range(RE_H):
                        rows = slice((h % 2) * HD, (h % 2) * HD + HD)
                        ins = score_products(h, rot[rows, 2 + h // 2, :], rot[rows, h // 2, :])
                    pe_s.mark(ins, "qk")
                    dv_s.wait(e, "W")
                    pe_s.mark(value_products(WR, rv, 4, RE_H, T), "o")
                    return pe_s

                def dve(e, c):
                    pe_s.wait(e, "qk")
                    for h in range(RE_H):
                        ins = nc.vector.tensor_tensor(WR[:, h].rearrange("p a t -> p (a t)"), PS[:, h, 0:TRI],
                                                      ret_decay[:, h].rearrange("p a t -> p (a t)"), ALU.mult)
                    dv_s.mark(ins, "W")
                    pe_s.wait(e, "o")
                    for t in range(NT):
                        ins = nc.vector.tensor_copy(MIX[:, t, 768:1024], PS[:, 4 + t, 0:T])
                    dv_s.mark(ins, "o")
                    return dv_s
                stage(L + "ret", pe=pe, dve=dve)
            ret()

            def hgrn(L=L):
                sums = [("sum", a, b) for a in range(4) for b in range(2)]
                scs = [("sc", t, m) for t in range(NT) for m in range(LEVELS + 1)] + [("sc", 2, 0)]
                pe_s = steps("pe", sums + scs + ["o"])
                ac_s = steps("act", sums)
                dv_s = steps("dve", ["qk"] + scs + ["o"])

                def pe(e, c):
                    for _, a, b in sums:
                        hp, t = a // 2, a % 2
                        lf = logf[:, t, hp * P:(hp + 1) * P]
                        bank = PS[:, 2 * a + b, :]
                        if b == 0:
                            ins = nc.tensor.matmul(bank, lf, lev_sum[:, 0:4, :], start=True, stop=True)
                        else:
                            nc.tensor.matmul(bank[:, 0:3 * P], lf, lev_sum[:, 4:7, :], start=True, stop=True)
                            ins = nc.tensor.matmul(bank[:, 3 * P:], lf, lev_sum[:, 7 + t, :], start=True, stop=True)
                        pe_s.mark(ins, ("sum", a, b))
                    dv_s.wait(e, "qk")
                    for i, (_, t, m) in enumerate(scs):
                        if i >= 4:
                            dv_s.wait(e, scs[i - 4])
                        for h in range(HG_H):
                            rows, hp = slice((h % 2) * HD, (h % 2) * HD + HD), h // 2
                            tk = slice(t * P, (t + 1) * P)
                            if t == 2:
                                a, b = EX[rows, 2 * hp, LEVELS, :], EX[rows, 2 * hp + 1, LEVELS, :]
                            elif m == 0:
                                a, b = kinT[rows, hp, tk], hqT[rows, hp, tk]
                            else:
                                a = b = EX[rows, 2 * hp + t, m - 1, :]
                            ins = nc.tensor.matmul(PS[:, 2 * (i % 4) + h % 2, hp * P:(hp + 1) * P], a, b,
                                                   start=True, stop=True)
                        pe_s.mark(ins, scs[i])
                    dv_s.wait(e, scs[-1])
                    pe_s.mark(value_products(WH, hi, 2, HG_H, T), "o")
                    return pe_s

                def act(e, c):
                    for _, a, b in sums:
                        pe_s.wait(e, ("sum", a, b))
                        ac_s.mark(nc.scalar.activation(EX[:, a, 4 * b:4 * b + 4, :],
                                                       PS[:, 2 * a + b, :].rearrange("p (l t) -> p l t", l=4), ACT.Exp),
                                  ("sum", a, b))
                    return ac_s

                def dve(e, c):
                    V = nc.vector
                    ac_s.wait(e, sums[-1])
                    q4 = hqT.rearrange("p h (t c) -> p (h t) c", t=NT)
                    k4 = kinT.rearrange("p h (t c) -> p (h t) c", t=NT)
                    for lev in range(LEVELS):
                        half, size = 1 << lev, 2 << lev
                        for src, lo in ((k4, 0), (q4, half)):
                            ex = EX[:, :, lev, :].rearrange("p a (n s) -> p a n s", s=size)[:, :, :, lo:lo + half]
                            sv = src.rearrange("p a (n s) -> p a n s", s=size)[:, :, :, lo:lo + half]
                            V.tensor_tensor(ex, ex, sv, ALU.mult)
                    V.tensor_tensor(EX[:, 0:4:2, LEVELS, :], EX[:, 0:4:2, LEVELS, :], k4[:, 0:4:2, :], ALU.mult)
                    dv_s.mark(V.tensor_tensor(EX[:, 1:4:2, LEVELS, :], EX[:, 1:4:2, LEVELS, :], q4[:, 1:4:2, :], ALU.mult), "qk")
                    mt4 = mtmp.rearrange("p (h r) t -> p r h t", r=2)

                    def lmask(m):
                        return lev_mask[:, m, :].unsqueeze(1).unsqueeze(1).broadcast_to([P, 2, 2, P])
                    for i, (_, t, m) in enumerate(scs):
                        pe_s.wait(e, scs[i])
                        b2 = 2 * (i % 4)
                        bank = PS[:, b2:b2 + 2, 0:2 * P].rearrange("p r (h t) -> p r h t", h=2)
                        dst = WH[:, :, (0, 2, 1)[t], :].rearrange("p (h r) t -> p r h t", r=2)
                        if t == 2:
                            ins = V.tensor_copy(dst, bank)
                        elif m == 0:
                            ins = V.tensor_tensor(dst, bank, lmask(0), ALU.mult)
                        else:
                            c(V.tensor_tensor(mt4, bank, lmask(m), ALU.mult))
                            ins = V.tensor_tensor(dst, dst, mt4, ALU.add)
                        dv_s.mark(ins, scs[i])
                        dv_s.wait(e, scs[i])
                    pe_s.wait(e, "o")
                    for t in range(NT):
                        ins = V.tensor_copy(MIX[:, t, 512:768], PS[:, 2 + t, 0:T])
                    dv_s.mark(ins, "o")
                    return dv_s
                stage(L + "hgrn", pe=pe, act=act, dve=dve)
            hgrn()

            def mixnorm(L=L):
                dv_s = steps("dve", ["ss", "y"])
                ac_s = steps("act", ["rt"])
                sq2 = arena(18868, NT, D)
                ssg, ssh = sm[:, 160:164], sm[:, 164:180]
                big = MIX[:, :, 0:512].rearrange("p t (g d) -> p t g d", g=2)
                small = MIX[:, :, 512:1024].rearrange("p t (h d) -> p t h d", h=8)

                def dve(e, c):
                    V = nc.vector
                    c(V.tensor_tensor(sq2, MIX, MIX, ALU.mult))
                    c(V.tensor_reduce(ssg.rearrange("p (t g) -> p t g", t=NT),
                                      sq2[:, :, 0:512].rearrange("p t (g d) -> p t g d", g=2), AX, ALU.add))
                    dv_s.mark(V.tensor_reduce(ssh.rearrange("p (t g) -> p t g", t=NT),
                                              sq2[:, :, 512:1024].rearrange("p t (g d) -> p t g d", g=8), AX, ALU.add), "ss")
                    c(V.tensor_tensor(hg, hg, bc(ngh, 1, NT), ALU.mult))
                    ac_s.wait(e, "rt")
                    c(V.reciprocal(sm[:, 160:180], sm[:, 160:180]))
                    c(V.tensor_tensor(big, big, bc(ssg.rearrange("p (t g) -> p t g", t=NT), 3, 256), ALU.mult))
                    c(V.tensor_tensor(small, small, bc(ssh.rearrange("p (t g) -> p t g", t=NT), 3, HD), ALU.mult))
                    c(V.tensor_tensor(MIX[:, :, 0:512], MIX[:, :, 0:512], bc(ngs, 1, NT), ALU.mult))
                    c(V.tensor_tensor(MIX[:, :, 512:768], MIX[:, :, 512:768], hg, ALU.mult))
                    dv_s.mark(V.tensor_tensor(MIX[:, :, 768:1024], MIX[:, :, 768:1024], rg, ALU.mult), "y")
                    return dv_s

                def act(e, c):
                    dv_s.wait(e, "ss")
                    nc.scalar.activation(ssg, ssg, ACT.Sqrt, bias=eps_col, scale=1.0 / 256)
                    ac_s.mark(nc.scalar.activation(ssh, ssh, ACT.Sqrt, bias=eps_col, scale=1.0 / HD), "rt")
                    return ac_s
                stage(L + "mixnorm", dve=dve, act=act)
            mixnorm()
            first_wo2 = ring_loads(io[f"w_out{layer}"], 2)
            out_proj_stage(L + "out", MIX, arena(18868, KC, T), first_wo2, MOD[:, 2, :], arena(21940, CW))

            EW = KC * FE
            ERAW = [ring[:, q * EW:(q + 1) * EW] for q in range(3)]
            ESPL = [r32(3 * EW + q * 2 * EW, 2, EW) for q in range(4)]
            hs, hs32 = r32(11 * EW, 2, KC, T)
            hidr, hidr32 = r32(RB + 23552, 2, 2, 2 * T)
            e_ld = [sem(L + f"e_ld{q}") for q in range(3)]
            s_ehi, s_elo, s_euse, s_silu, s_t, s_hm, s_hh, s_hs, s_xs, s_xl = (
                sem(L + n) for n in ("ehi", "elo", "euse", "silu", "t", "hm", "hh", "hs", "xs", "xl"))
            release_ring(L + "out")

            def triples(e, body):
                for m in range(PEEL):
                    body(m, 3 * m + 2, m)
                with e.Fori(0, (NEXP - 1 - PEEL) // 4) as i:
                    for q in range(4):
                        body(i * 4 + (PEEL + q), i * 12 + (3 * (PEEL + q) + 2), PEEL + q)

            def load_experts(sp, layer=layer, e_ld=e_ld, s_elo=s_elo, ERAW=ERAW, triples=triples):
                def part(kind, x, n, s):
                    if s >= 3:
                        sp.wait_ge(s_elo, n - 2)
                    src = io[f"w_{kind}{layer}"][x]
                    dst = ERAW[s % 3]
                    if kind == "down":
                        src = src.rearrange("(k p) n -> p k n", p=P)
                        dst = dst.rearrange("p (k n) -> p k n", k=2)
                    sp.dma_start(dst, src).then_inc(e_ld[s % 3], 16)
                part("gate", 0, 0, 0)
                part("up", 0, 1, 1)

                def body(m, n, mm):
                    s = 3 * mm + 2
                    part("gate", m + 1, n, s)
                    part("up", m + 1, n + 1, s + 1)
                    part("down", m, n + 2, s + 2)
                triples(sp, body)
                part("down", NEXP - 1, 3 * NEXP - 1, 3 * NEXP - 1)

            norm_T_stage(L + "norm_ffn", [(X[:, t, :], MOD[:, 4, :], MOD[:, 3, :]) for t in range(NT)],
                         io[f"ng_ffn{layer}"], hT, 14336)
            CMB = arena(14336, NEXP, T)
            sg = arena(22528, 2, 512)
            wrt, brt = arena(22528, KC, 36), arena(22816, 36)
            lgt, comb = arena(22860, NT, 36), arena(22940, NT, NEXP)
            r1, r2 = arena(23010, NT, 4, 8), arena(23080, NT, 8)
            cT = arena(23200, T)
            rr = arena(23500, 200)

            def router(L=L, layer=layer):
                s_in = sem(L + "rt_in")
                bcs = [("b", i) for i in range(16)]
                pe_s = steps("pe", ["lg", "tr"] + bcs)
                ac_s = steps("act", ["e0", "e1"] + bcs[1::2])
                dv_s = steps("dve", ["x0", "x1", "comb", "tr"] + bcs[0::2])

                def pool(e, c):
                    e.dma_start(wrt, io[f"w_rt{layer}"].rearrange("p (k n) -> p k n", k=KC)).then_inc(s_in, 16)
                    e.dma_start(brt, io[f"b_rt{layer}"].unsqueeze(0).broadcast_to([P, 36])).then_inc(s_in, 16)
                    e.wait_ge(s_in, 32)

                def pe(e, c):
                    e.wait_ge(s_in, 32)
                    for t in range(NT):
                        for k in range(KC):
                            ins = nc.tensor.matmul(PS[:, 0, t * 36:(t + 1) * 36], hT[:, k, t * P:(t + 1) * P], wrt[:, k, :],
                                                   start=(k == 0), stop=(k == KC - 1))
                    pe_s.mark(ins, "lg")
                    dv_s.wait(e, "comb")
                    for t in range(NT):
                        ins = nc.tensor.transpose(PS[0:NEXP, 1, t * P:(t + 1) * P], comb[:, t, :], ident)
                    pe_s.mark(ins, "tr")
                    dv_s.wait(e, "tr")
                    for i in range(16):
                        if i >= 4:
                            (dv_s if i % 2 == 0 else ac_s).wait(e, ("b", i - 4))
                        for a in range(2):
                            x = 2 * i + a
                            ins = nc.tensor.matmul(PS[:, 2 + i % 4, a * T:(a + 1) * T],
                                                   ident[0:NEXP, x:x + 1].broadcast_to([NEXP, P]), cT[0:NEXP, :],
                                                   start=True, stop=True)
                        pe_s.mark(ins, ("b", i))
                    return pe_s

                def dst(i):
                    return CMB[:, 2 * i:2 * i + 2, :], PS[:, 2 + i % 4, :].rearrange("p (a t) -> p a t", a=2)

                def act(e, c):
                    dv_s.wait(e, "x0")
                    ac_s.mark(nc.scalar.activation(rr[:, 8:16], rr[:, 8:16], ACT.Exp), "e0")
                    dv_s.wait(e, "x1")
                    ac_s.mark(nc.scalar.activation(rr[:, 66:68], rr[:, 66:68], ACT.Exp), "e1")
                    for i in range(1, 16, 2):
                        pe_s.wait(e, ("b", i))
                        ac_s.mark(nc.scalar.copy(*dst(i)), ("b", i))
                    return ac_s

                def dve(e, c):
                    V = nc.vector

                    def v(lo, n):
                        return rr[:, lo:lo + n].rearrange("p (t k) -> p t k", t=NT)
                    e.wait_ge(s_in, 32)
                    pe_s.wait(e, "lg")
                    c(V.tensor_tensor(lgt, PS[:, 0, 0:72].rearrange("p (t k) -> p t k", t=NT), bc(brt, 1, NT), ALU.add))
                    grp = lgt[:, :, 0:NGRP]
                    c(V.tensor_reduce(rr[:, 0:2], grp, AX, ALU.max))
                    dv_s.mark(V.tensor_tensor(v(8, 8), grp, bc(rr[:, 0:2], 2, NGRP), ALU.subtract), "x0")
                    c(V.tensor_tensor(v(16, 8), grp, bc(rr[:, 0:2], 2, NGRP), ALU.is_equal))
                    c(V.scalar_tensor_tensor(v(16, 8), v(16, 8), -1000.0, bc(iota[:, 0:NGRP], 1, NT), ALU.mult, ALU.add))
                    c(V.tensor_reduce(rr[:, 2:4], v(16, 8), AX, ALU.min))
                    c(V.tensor_tensor(v(16, 8), v(16, 8), bc(rr[:, 2:4], 2, NGRP), ALU.is_equal))
                    ac_s.wait(e, "e0")
                    c(V.tensor_reduce(rr[:, 4:6], v(8, 8), AX, ALU.add))
                    c(V.reciprocal(rr[:, 4:6], rr[:, 4:6]))
                    ex = lgt[:, :, NGRP:].rearrange("p t (g x) -> p t g x", g=NGRP)
                    c(V.tensor_tensor(r1, ex, bc(v(16, 8), 3, EPG), ALU.mult))
                    c(V.tensor_reduce(r2, r1.rearrange("p t g x -> p t x g"), AX, ALU.add))
                    for t in range(NT):
                        ins = V.max(v(24, 16)[:, t, :], r2[:, t, :])
                    c(ins)
                    for t in range(NT):
                        ins = V.max_index(v(40, 16).bitcast(U32)[:, t, :], v(24, 16)[:, t, :], r2[:, t, :])
                    c(ins)
                    dv_s.mark(V.tensor_tensor(rr[:, 66:68], v(24, 16)[:, :, 1], v(24, 16)[:, :, 0], ALU.subtract), "x1")
                    c(V.tensor_copy(v(70, 16), v(40, 16).bitcast(U32)))
                    ac_s.wait(e, "e1")
                    c(V.tensor_scalar_add(rr[:, 68:70], rr[:, 66:68], 1.0))
                    c(V.reciprocal(rr[:, 68:70], rr[:, 68:70]))
                    c(V.tensor_tensor(rr[:, 68:70], rr[:, 68:70], rr[:, 4:6], ALU.mult))
                    c(V.tensor_tensor(rr[:, 66:68], rr[:, 66:68], rr[:, 68:70], ALU.mult))
                    io8 = bc(iota[:, 0:EPG], 1, NT)
                    for j, w in ((0, 68), (1, 66)):
                        o = v(90 + 16 * j, 16)
                        c(V.tensor_tensor(o, io8, bc(v(70, 16)[:, :, j], 2, EPG), ALU.is_equal))
                        c(V.tensor_tensor(o, o, bc(rr[:, w:w + 2], 2, EPG), ALU.mult))
                    c(V.tensor_tensor(v(90, 16), v(90, 16), v(106, 16), ALU.add))
                    dv_s.mark(V.tensor_tensor(comb.rearrange("p t (g x) -> p t g x", g=NGRP), bc(v(16, 8), 3, EPG),
                                              bc(v(90, 16), 2, NGRP), ALU.mult), "comb")
                    pe_s.wait(e, "tr")
                    dv_s.mark(V.tensor_copy(cT[0:NEXP, :], PS[0:NEXP, 1, 0:T]), "tr")
                    for i in range(0, 16, 2):
                        pe_s.wait(e, ("b", i))
                        dv_s.mark(V.tensor_copy(*dst(i)), ("b", i))
                    return dv_s
                stage(L + "router", pool=pool, pe=pe, act=act, dve=dve)
            router()

            def experts(L=L, e_ld=e_ld, ESPL=ESPL, hs=hs, hs32=hs32, hidr=hidr, hidr32=hidr32, s_ehi=s_ehi, s_elo=s_elo,
                        s_euse=s_euse, s_silu=s_silu, s_t=s_t, s_hm=s_hm, s_hh=s_hh, s_hs=s_hs, s_xs=s_xs, s_xl=s_xl,
                        triples=triples, ERAW=ERAW):
                def act(e, c):
                    def hi(n, s):
                        if isinstance(n, int):
                            e.wait_ge(e_ld[n % 3], 16 * (n // 3 + 1))
                        else:
                            e.wait_ge(e_ld[s[0] % 3], s[1] * 16)
                            s = s[0]
                        if s >= 4:
                            e.wait_ge(s_euse, n - 3)
                        nc.scalar.copy(ESPL[s % 4][0][:, 0, :], ERAW[s % 3]).then_inc(s_ehi, 1)

                    def silu(x, xx):
                        e.wait_ge(s_euse, 1 if xx == 0 else x * 3)
                        if xx >= 2:
                            e.wait_ge(s_hs, x - 1)
                        nc.scalar.activation(sg[:, xx % 2, :], PS[:, 2 * (xx % 2), :], ACT.Silu).then_inc(s_silu, 1)
                    nc.scalar.copy(hs[:, 0], hT).then_inc(s_xs, 1)
                    hi(0, 0)
                    hi(1, 1)

                    def body(m, n, mm):
                        s = 3 * mm + 2
                        for j in range(3):
                            hi(n + j, s + j if isinstance(n, int) else (s + j, m + (1 + (2 + j) // 3)))
                        silu(m, mm)
                    triples(e, body)
                    hi(3 * NEXP - 1, 3 * NEXP - 1)
                    silu(NEXP - 1, NEXP - 1)
                    e.wait_ge(s_silu, NEXP)

                def dve(e, c):
                    V = nc.vector

                    def lo(n, s):
                        e.wait_ge(s_ehi, n + 1)
                        V.tensor_tensor(ESPL[s % 4][0][:, 1, :], ERAW[s % 3], ESPL[s % 4][1][:, 0, :],
                                        ALU.subtract).then_inc(s_elo, 1)

                    def hidden(x, xx):
                        b = xx % 2
                        s2 = sg[:, b, :].rearrange("p (f t) -> p f t", f=2)
                        e.wait_ge(s_silu, x + 1)
                        V.tensor_tensor(s2, s2, CMB[:, bass.ds(x, 1), :].broadcast_to([P, 2, T]), ALU.mult).then_inc(s_t, 1)
                        e.wait_ge(s_t, x + 1)
                        e.wait_ge(s_euse, 2 if xx == 0 else x * 3 + 1)
                        V.tensor_tensor(sg[:, b, :], sg[:, b, :], PS[:, 2 * b + 1, :], ALU.mult).then_inc(s_hm, 1)
                        e.wait_ge(s_hm, x + 1)
                        if xx >= 2:
                            e.wait_ge(s_euse, x * 3 - 1)
                        V.tensor_copy(hidr[:, b, 0, :], sg[:, b, :]).then_inc(s_hh, 1)
                        e.wait_ge(s_hh, x + 1)
                        V.tensor_tensor(hidr[:, b, 1, :], sg[:, b, :], hidr32[:, b, 0, :], ALU.subtract).then_inc(s_hs, 1)
                    e.wait_ge(s_xs, 1)
                    V.tensor_tensor(hs[:, 1], hT, hs32[:, 0], ALU.subtract).then_inc(s_xl, 1)
                    lo(0, 0)
                    lo(1, 1)

                    def body(m, n, mm):
                        s = 3 * mm + 2
                        for j in range(3):
                            lo(n + j, s + j)
                        hidden(m, mm)
                    triples(e, body)
                    lo(3 * NEXP - 1, 3 * NEXP - 1)
                    hidden(NEXP - 1, NEXP - 1)
                    e.wait_ge(s_hs, NEXP)

                def pe(e, c):
                    def up(x, n, s, bank):
                        e.wait_ge(s_elo, n + 1)
                        w = ESPL[s % 4][0].rearrange("p h (k f) -> p h k f", k=KC)
                        for f in range(2):
                            fs = slice(f * P, (f + 1) * P)
                            for k in range(KC):
                                ins = exact3(PS[:, bank, f * T:(f + 1) * T], (w[:, 0, k, fs], w[:, 1, k, fs]),
                                             (hs[:, 0, k, :], hs[:, 1, k, :]), k == 0, k == KC - 1)
                        ins.then_inc(s_euse, 1)

                    def gate_up(x, n, s, xx):
                        if xx >= 2:
                            e.wait_ge(s_hm, x - 1)
                        up(x, n, s, 2 * (xx % 2))
                        up(x, n + 1, s + 1, 2 * (xx % 2) + 1)

                    def down(x, n, s, xx, start=False, stop=False):
                        e.wait_ge(s_elo, n + 1)
                        e.wait_ge(s_hs, x + 1)
                        w = ESPL[s % 4][0].rearrange("p h (k n) -> p h k n", k=2)
                        h = hidr[:, xx % 2].rearrange("p s (f t) -> p s f t", f=2)
                        for f in range(2):
                            for t in range(NT):
                                for n2 in range(2):
                                    tk, cols = slice(t * P, (t + 1) * P), slice(n2 * CW, (n2 + 1) * CW)
                                    ins = exact3(PS[:, 4 + 2 * t + n2, :], (h[:, 0, f, tk], h[:, 1, f, tk]),
                                                 (w[:, 0, f, cols], w[:, 1, f, cols]), start and f == 0, stop and f == 1)
                        ins.then_inc(s_euse, 1)
                    e.wait_ge(s_xl, 1)
                    gate_up(0, 0, 0, 0)

                    def body(m, n, mm):
                        s = 3 * mm + 2
                        gate_up(m + 1, n, s, mm + 1)
                        down(m, n + 2, s + 2, mm, start=mm == 0)
                    triples(e, body)
                    down(NEXP - 1, 3 * NEXP - 1, 3 * NEXP - 1, NEXP - 1, stop=True)
                    e.wait_ge(s_euse, 3 * NEXP)
                stage(L + "experts", pe=pe, act=act, dve=dve)
            stream.append(load_experts)
            experts()
            add_norm_stage(L + "moe_out", MOD[:, 5, :], io["final2"] if layer == LAYERS - 1 else None, 20480)

        s_store = sem("s_store")

        def pool_out(e, c):
            e.dma_start(io["out"].rearrange("o (t p) d -> p (o t) d", p=P), X[:]).then_inc(s_store, 16)
            e.wait_ge(s_store, 16)
        stage("store", pool=pool_out)

        block = ctx.enter_context(nc.Block())

        def run(eng, kind, chain):
            for k, (name, progs) in enumerate(stages):
                if kind in progs:
                    steps = progs[kind](eng, chain)
                    if steps is not None:
                        assert steps.n == len(steps.names), (name, kind, steps.n)
                        eng.wait_ge(steps.sem, steps.base + steps.n)
                eng.sem_inc(s_bar, 1)
                eng.wait_ge(s_bar, 4 * (k + 1))

        @block.sync
        def _(sp):
            for load in stream:
                load(sp)

        @block.scalar
        def _(act):
            run(act, "act", Chain(act, s_a))

        @block.vector
        def _(dve):
            run(dve, "dve", Chain(dve, s_v))

        @block.tensor
        def _(pe):
            run(pe, "pe", None)

        @block.gpsimd
        def _(pool):
            run(pool, "pool", Chain(pool, s_g))


def slots(w):
    n = w.shape[1] // CW
    return np.ascontiguousarray(w.reshape(P, KC, n, CW).transpose(2, 0, 1, 3)).reshape(n, P, SLOT)


def layout(i):
    a = {"const": CONST, "x": i["x"], "ctx": i["ctx"]}
    a["c"] = i["c"].reshape(P, KC)
    a["c_ctx"] = i["c_ctx"].reshape(P, KC)
    a["ada_w"] = slots(i["ada_w"][0])
    a["ada_b"] = i["ada_b"][0]
    a["norm_g0"], a["norm_g1"] = i["norm_g"][0, 0], i["norm_g"][0, 1]
    w = i["dn_w_in"][0]
    a["dn_w"] = slots(w[:, :4 * D])
    a["dn_wba"] = np.ascontiguousarray(w[:, 4 * D:]).reshape(P, KC * 32)
    a["dn_cw"] = np.ascontiguousarray(i["dn_conv_w"][0].reshape(DN_TAPS, 24, P).transpose(2, 1, 0)).reshape(P, 24 * DN_TAPS)
    a["dn_alog"], a["dn_dt"] = i["dn_a_log"].reshape(16), i["dn_dt_bias"].reshape(16)
    a["dn_ng"] = i["dn_norm_g"][0]
    a["dn_wo"] = slots(i["dn_w_out"][0])
    a["peer_wq"] = slots(i["peer_w_q"][0])
    a["peer_kT"] = np.ascontiguousarray(i["peer_keys"][0].reshape(16, NK, P).transpose(2, 0, 1)).reshape(P, 16 * NK)
    a["peer_u"] = np.ascontiguousarray(i["peer_u"][0].reshape(NK, NK, P, KC).transpose(1, 2, 3, 0)).reshape(NK, P, KC * P)
    a["peer_v"] = i["peer_v"][0].reshape(NK, NK, D)
    a["final_g"] = i["final_g"]
    for l in range(LAYERS):
        w = i["w_in_2"][l]
        cut = np.cumsum([512, 768, 8, 256, 256, 256, 256, 256, 256, 256, 256])[:-1]
        z, xbc, dt, hq, hf, hi, hg, rq, rk, rv, rg = np.split(w, cut, axis=1)

        def swap(m):
            return m.reshape(D, RE_H, 2, HD // 2)[:, :, ::-1].reshape(D, RE_H * HD)
        a[f"w_in{l}"] = slots(np.concatenate([xbc, hq, hf, rq, rk, swap(rq), swap(rk), hf, z, hi, hg, rv, rg], 1))
        a[f"w_dt{l}"] = np.ascontiguousarray(dt).reshape(P, KC * 8)
        a[f"ada_w{l}"] = slots(i["w_ada_2"][l])
        a[f"ada_b{l}"] = i["b_ada_2"][l]
        a[f"ng_mix{l}"], a[f"ng_ffn{l}"] = i["norm_mix_g_2"][l], i["norm_ffn_g_2"][l]
        cw = np.concatenate([i["conv_w_2"][l], i["conv_b_2"][l][None]], 0)
        a[f"conv{l}"] = np.ascontiguousarray(cw.reshape(5, 6, P).transpose(2, 1, 0)).reshape(P, 30)
        a[f"ssd{l}"] = np.concatenate([i["ssd_dt_bias_2"][l], i["ssd_a_log_2"][l], i["ssd_d_2"][l]])
        a[f"ng_ssd{l}"], a[f"ng_hgrn{l}"] = i["ssd_norm_g_2"][l], i["hgrn_norm_g_2"][l]
        a[f"w_out{l}"] = slots(i["w_out_2"][l])
        a[f"w_rt{l}"] = np.concatenate([i["w_grp_2"][l], i["w_exp_2"][l]], 1).reshape(P, KC * 36)
        a[f"b_rt{l}"] = np.concatenate([i["b_grp_2"][l], i["b_exp_2"][l]])
        a[f"w_gate{l}"] = i["w_gate_2"][l].reshape(NEXP, P, KC * FE)
        a[f"w_up{l}"] = i["w_up_2"][l].reshape(NEXP, P, KC * FE)
        a[f"w_down{l}"] = i["w_down_2"][l]
    a["lbs"] = i["hgrn_lower_bounds_2"]
    a["lbsT"] = np.ascontiguousarray(i["hgrn_lower_bounds_2"].reshape(2, 2, P).transpose(2, 0, 1)).reshape(P, 4)
    a["c2"] = i["c_2"].reshape(P, KC)
    a["final2"] = i["final_norm_g_2"]
    return a


def kernel(**inputs):
    import concourse.bacc as bacc
    from concourse.bass_utils import run_bass_kernel_spmd as run

    arrays = layout({k: np.asarray(v) for k, v in inputs.items()})
    arrays = {f"in_{k}": np.ascontiguousarray(v) for k, v in arrays.items()}
    nc = bacc.Bacc("TRN2", target_bir_lowering=False, num_devices=1)
    io = {k[3:]: nc.dram_tensor(k, v.shape, mybir.dt.from_np(v.dtype), kind="ExternalInput").ap()
          for k, v in arrays.items()}
    io["out"] = nc.dram_tensor("out", (1, T, D), F32, kind="ExternalOutput").ap()
    build(nc, io)
    r = run(nc, [arrays], core_ids=[0])
    return r.results[0]["out"]
```

```python
from contextlib import ExitStack

import numpy as np

import concourse.bass as bass
from concourse import mybir

F32 = mybir.dt.float32
U32 = mybir.dt.uint32
F32R = mybir.dt.float32r
ALU = mybir.AluOpType
ACT = mybir.ActivationFunctionType
AX = mybir.AxisListType.X

P = 128
T = 256
NT = T // P
D = 1024
KC = D // P
EPS = 1e-6
CW = 512
SLOT = KC * CW
NRING = 3

DN_H = 8
DN_BLOCK = 64
ROWS, ROW_W = 4, 64
DN_TAPS = 5
DN_PAD = (DN_TAPS - 1) // 2
PH, NK, TOPK = 8, 128, 16
LAYERS = 2
SSD_H, HG_H, RE_H, HD = 8, 4, 4, 64
TAPS2 = 4
GATE_FLOOR = 1e-30
NGRP, EPG, NEXP, FE = 4, 8, 32, 256
LEVELS = 7
TRI = P * 3
NEG = -3.0e38



def shape_constants():
    i = np.arange(P)
    row, col = i[:, None], i[None, :]
    parts = {}
    parts["ident"] = row == col
    parts["ones"] = np.ones((P, P))
    parts["inc_f"] = row <= col
    parts["inc_b"] = row >= col
    parts["strict_f"] = row < col
    parts["strict_b"] = row > col
    same = row // DN_BLOCK == col // DN_BLOCK
    parts["block"] = same
    parts["off"] = ~same
    lm = [row == col]
    em = []
    for lev in range(LEVELS):
        half, size = 1 << lev, 2 << lev
        blk = row // size == col // size
        left_r, right_c = row % size < half, col % size >= half
        lm.append(blk & left_r & right_c)
        right = right_c & (row % size >= half) & (row <= col)
        left = ~right_c & left_r & (row > col)
        em.append(blk & (right | left))
    em.append(row > col)
    em.append(row <= col)
    parts["lev_mask"] = np.concatenate(lm, 1)
    parts["lev_sum"] = np.concatenate(em, 1)
    half = HD // 2
    inv = (np.float32(10000.0) ** (-np.arange(half, dtype=np.float32) / np.float32(half))).astype(np.float32)
    ang = (np.arange(T, dtype=np.float32)[:, None] * inv[None, :]).astype(np.float32)
    cos, sin = np.cos(ang.astype(np.float64)).T, np.sin(ang.astype(np.float64)).T
    parts["cos"] = np.tile(cos, (4, 1))
    parts["sin"] = np.tile(np.concatenate([-sin, sin], 0), (2, 1))
    lg = np.log1p(-np.exp2(-5.0 - np.arange(RE_H)))
    dd = []
    for h in range(RE_H):
        a = np.where(row <= col, np.exp(lg[h] * np.maximum(col - row, 0)), 0.0)
        b = np.exp(lg[h] * (col + P - row))
        dd += [a, b, a]
    parts["ret_decay"] = np.concatenate(dd, 1)
    parts["iota"] = np.broadcast_to(col, (P, P))
    out, at = [], {}
    n = 0
    for k, v in parts.items():
        at[k] = (n, v.shape[1])
        n += v.shape[1]
        out.append(v.astype(np.float32))
    return np.ascontiguousarray(np.concatenate(out, 1)), at


CONST, CAT = shape_constants()


class Steps:

    def __init__(self, sem, names, base=0, done=None):
        self.sem, self.names, self.at = sem, names, {n: base + i + 1 for i, n in enumerate(names)}
        assert len(self.at) == len(names)
        self.n, self.base, self.done = 0, base, done if done is not None else [base]

    def mark(self, ins, name):
        assert self.names[self.n] == name, (self.n, self.names[self.n], name)
        assert self.done[0] == self.base + self.n
        self.done[0] += 1
        self.n += 1
        ins.then_inc(self.sem, 1)

    def wait(self, eng, name):
        eng.wait_ge(self.sem, self.at[name])


class Chain:

    def __init__(self, eng, sem):
        self.eng, self.sem, self.n = eng, sem, 0

    def __call__(self, ins):
        self.n += 1
        ins.then_inc(self.sem, 1)
        self.eng.wait_ge(self.sem, self.n)


def bc(ap, axis, n):
    v = ap.unsqueeze(axis)
    shape = list(v.shape)
    shape[axis] = n
    return v.broadcast_to(shape)


def build(nc, io):
    ctx = ExitStack()
    with ctx:
        def sb(name, shape, dt=F32):
            return ctx.enter_context(nc.sbuf_tensor(name, shape, dt))

        def sem(name):
            return ctx.enter_context(nc.semaphore(name))

        WORDS = NRING * SLOT + 32768 + 3 * P + 2 * NT * D + D + 3 * T + 256 + 1536
        slab_at = (nc.sbuf_base + 31) // 32 * 32
        ring = sb("ring", [P, WORDS])
        RB = NRING * SLOT
        taken = [RB + 32768]

        def fixed(n):
            taken[0] += n
            assert taken[0] <= WORDS
            return ring[:, taken[0] - n:taken[0]]

        over = []

        def r32(word, *shape):
            over.append(nc.alloc_sbuf_tensor_at(f"over{len(over)}", [P, *shape], F32R, offset=slab_at + 4 * word))
            v = over[-1][tuple(slice(None) for _ in range(len(shape) + 1))]
            return v, v.bitcast(F32)
        cst = fixed(3 * P)
        ident, ones, iota = cst[:, 0:P], cst[:, P:2 * P], cst[:, 2 * P:3 * P]
        X_at = taken[0]
        X = fixed(NT * D).rearrange("p (t d) -> p t d", t=NT)
        hT_at = taken[0]
        hT = fixed(KC * T).rearrange("p (k t) -> p k t", k=KC)
        GT_at = taken[0]
        GT = fixed(D)
        idx = fixed(3 * T).rearrange("p (a t) -> p a t", a=3)
        sm = fixed(256)
        spare_at = taken[0]
        PS = ctx.enter_context(nc.psum_tensor("PS", [P, 8, 512], F32))

        def arena(off, *shape):
            n = int(np.prod(shape))
            v = ring[:, RB + off:RB + off + n]
            if len(shape) == 1:
                return v
            names = "abcd"[:len(shape)]
            return v.rearrange(f"p ({' '.join(names)}) -> p {' '.join(names)}",
                               **{names[i]: shape[i] for i in range(1, len(shape))})

        MOD = arena(26624, 6, D)

        s_bar = sem("s_bar")
        s_ring = [sem(f"s_ring{i}") for i in range(NRING)]
        s_v, s_a, s_g = sem("s_v"), sem("s_a"), sem("s_g")
        s_steps = {who: sem(f"s_{who}_steps") for who in ("pe", "act", "dve")}
        n_steps = {who: 0 for who in s_steps}
        steps_done = {who: [0] for who in s_steps}

        def steps(who, names):
            st = Steps(s_steps[who], names, n_steps[who], steps_done[who])
            n_steps[who] += len(names)
            return st

        s_gain = sem("s_gain")
        s_cst = sem("s_cst")
        stream = []
        free_at = []
        stages = []

        def stage(name, **progs):
            stages.append((name, progs))

        def ring_load(src):
            n = len(free_at)
            free_at.append(None)

            def load(sp):
                if n >= NRING:
                    steps, name = free_at[n - NRING]
                    steps.wait(sp, name)
                dst = ring[:, (n % NRING) * SLOT:(n % NRING + 1) * SLOT]
                if len(src.shape) == 3:
                    dst = dst.rearrange("p (k c) -> p k c", c=CW)[:, 0:src.shape[1], :]
                sp.dma_start(dst, src).then_inc(s_ring[n % NRING], 16)
            stream.append(load)
            return n

        def ring_loads(src, count):
            first = len(free_at)
            for j in range(count):
                ring_load(src[j])
            return first

        def slot(n):
            return ring[:, (n % NRING) * SLOT:(n % NRING) * SLOT + SLOT].rearrange("p (k c) -> p k c", k=KC)

        def ring_wait(eng, n):
            eng.wait_ge(s_ring[n % NRING], 16 * (n // NRING + 1))

        def exact3(out, lhs, rhs, start, stop):
            nc.tensor.matmul(out, lhs[0], rhs[0], start=start, stop=False)
            nc.tensor.matmul(out, lhs[0], rhs[1], start=False, stop=False)
            return nc.tensor.matmul(out, lhs[1], rhs[0], start=False, stop=stop)

        NOW, LATER = 4, 8 + 12 * LAYERS
        silu_c = sm[:, 184:184 + 3 * KC].rearrange("p (a k) -> p a k", a=3)

        def ada_stage(modc):
            stream.append(lambda sp: sp.dma_start(silu_c, io["c_all"].rearrange("p (a k) -> p a k", a=3)).then_inc(s_in, 16))
            first = ring_loads(io["ada_w"], NOW)
            s_in, s_bias = sem("ada_in"), sem("ada_bias")
            rep = arena(0, 2, KC, P)
            mm_names = [(who, n) for n in range(NOW) for who in ("c", "ctx")]
            pe_s = steps("pe", mm_names)
            dv_s = steps("dve", ["rep"] + mm_names)
            ac_s = steps("act", ["silu"])
            for n in range(NOW):
                free_at[first + n] = (pe_s, ("ctx", n))

            def pool(e, c):
                for mod in (MOD[:, 0:2, :], modc):
                    e.dma_start(mod.rearrange("p a b -> p (a b)"),
                                io["ada_b"][0:2 * D].unsqueeze(0).broadcast_to([P, 2 * D])).then_inc(s_bias, 16)
                e.wait_ge(s_bias, 32)
                load_start(e, c)

            def act(e, c):
                e.wait_ge(s_in, 16)
                ac_s.mark(nc.scalar.activation(silu_c, silu_c, ACT.Silu), "silu")
                return ac_s

            def dve(e, c):
                c(nc.vector.memset(eps_col, EPS))
                ac_s.wait(e, "silu")
                dv_s.mark(nc.vector.tensor_copy(rep, bc(silu_c[:, 0:2, :], 3, P)), "rep")
                e.wait_ge(s_bias, 32)
                for i, (who, n) in enumerate(mm_names):
                    pe_s.wait(e, (who, n))
                    dst = (MOD if who == "c" else modc)[:, n // 2, (n % 2) * CW:(n % 2) * CW + CW]
                    dv_s.mark(nc.vector.tensor_tensor(dst, dst, PS[:, i % 4, :], ALU.add), (who, n))
                dv_s.wait(e, mm_names[-1])
                c(nc.vector.tensor_scalar_add(MOD[:, 1, :], MOD[:, 1, :], 1.0))
                c(nc.vector.tensor_scalar_add(modc[:, 1, :], modc[:, 1, :], 1.0))

            def pe(e, c):
                dv_s.wait(e, "rep")
                for i, (who, n) in enumerate(mm_names):
                    ring_wait(e, first + n)
                    if i >= 4:
                        dv_s.wait(e, mm_names[i - 4])
                    for k in range(KC):
                        ins = nc.tensor.matmul(PS[:, i % 4, :], rep[:, int(who == "ctx"), k, :],
                                               slot(first + n)[:, k, :], start=(k == 0), stop=(k == KC - 1))
                    pe_s.mark(ins, (who, n))
                return pe_s

            stage("ada_a", pool=pool, act=act, dve=dve, pe=pe)

        mod_part = nc.dram_tensor("mod_part", (LATER, P, CW), F32).ap()
        QW = SLOT // 4

        def mod_job(tag, at, which, raw, acc, tmp, bias, own_loads):
            count = len(which)
            s_w, s_b, s_st = ([sem(f"{tag}_{w}{q}") for q in range(2)] for w in ("w", "b", "st"))
            s_free, s_acc = sem(f"{tag}_free"), sem(f"{tag}_acc")
            at_c = [n for n in range(2, count - 2, 2) if which[n] != which[n - 2]]
            bounds = [2] + [n for n in at_c if n > 2] + [count - 2]

            def blocks(e, body):
                for n in range(2):
                    body(n, n)
                for lo, hi in zip(bounds, bounds[1:]):
                    with e.Fori(0, (hi - lo) // 2) as i:
                        for b in range(2):
                            body(i * 2 + (lo + b), lo + b)
                for n in range(count - 2, count):
                    body(n, n)

            def load_quarter(e, n, q):
                e.dma_start(raw[q % 2], io["mod_w"][n + at, :, q * QW:(q + 1) * QW]).then_inc(s_w[q % 2], 16)

            def load_bias(e, n, b):
                e.dma_start(bias[:, b, :], io["mod_b"][n + at].unsqueeze(0)).then_inc(s_b[b], 16)

            def load(sp):
                def body(n, nn):
                    for q in range(4):
                        if nn or q >= 2:
                            sp.wait_ge(s_free, n * 4 + (q - 1))
                        load_quarter(sp, n, q)
                    load_bias(sp, n, nn % 2)
                blocks(sp, body)

            def pool(e, c):
                G = nc.gpsimd

                def body(n, nn):
                    b = nn % 2
                    total = acc[b].rearrange("p (a c) -> p a c", a=2)
                    if own_loads:
                        load_bias(e, n, b)
                    if nn >= 2:
                        e.wait_ge(s_st[b], n * 8 - 8 * b)
                    for q in range(4):
                        e.wait_ge(s_w[q % 2], n * 32 + 16 * (q // 2 + 1))
                        if q:
                            e.wait_ge(s_acc, n * 9 + (2 * q - 1))
                        G.tensor_tensor(tmp if q else total, raw[q % 2].rearrange("p (a c) -> p a c", a=2),
                                        silu_c[:, which[nn], 2 * q:2 * q + 2].unsqueeze(2).broadcast_to([P, 2, CW]),
                                        ALU.mult).then_inc(s_acc, 1)
                        e.wait_ge(s_acc, n * 9 + max(2 * q, 1))
                        if not own_loads:
                            e.sem_inc(s_free, 1)
                        elif q < 2:
                            load_quarter(e, n, q + 2)
                        elif nn + 1 < count:
                            load_quarter(e, n + 1, q - 2)
                        if q:
                            G.tensor_tensor(total, total, tmp, ALU.add).then_inc(s_acc, 1)
                    e.wait_ge(s_acc, n * 9 + 7)
                    G.tensor_tensor(total[:, 0, :], total[:, 0, :], total[:, 1, :], ALU.add).then_inc(s_acc, 1)
                    e.wait_ge(s_b[b], n * 8 + (16 - 8 * b))
                    e.wait_ge(s_acc, n * 9 + 8)
                    G.tensor_tensor(total[0:1, 0, :], total[0:1, 0, :], bias[:, b, :], ALU.add).then_inc(s_acc, 1)
                    e.wait_ge(s_acc, n * 9 + 9)
                    e.dma_start(mod_part[n + at], total[:, 0, :]).then_inc(s_st[b], 16)
                if own_loads:
                    for q in range(2):
                        load_quarter(e, 0, q)
                blocks(e, body)
                for b in range(2):
                    e.wait_ge(s_st[b], 16 * (count // 2))
            return load, pool

        def pairs_of(words):
            return words.rearrange("p (b c) -> p b c", b=2)
        load_mod, pool_mod = mod_job("mod", 0, [0] * 8 + [2] * 12, [GT, arena(9216, QW)], [MOD[:, 0, :], MOD[:, 1, :]],
                                     pairs_of(ring[:, spare_at:spare_at + QW]), pairs_of(ring[0:1, 2 * D:3 * D]), False)
        _, pool_mod1 = mod_job("mod1", 20, [2] * 12, [GT, MOD[:, 4, :]], [MOD[:, 0, :], MOD[:, 1, :]],
                               pairs_of(MOD[:, 2, :]), pairs_of(MOD[0:1, 3, :]), True)

        def mod_sum(at, blocks):
            count = len(blocks)
            first = [ring_load(mod_part[at + j:at + min(j + KC, count)].rearrange("n p c -> p n c"))
                     for j in range(0, count, KC)]
            scale = [n for n in blocks if n // 2 in (1, 4)]
            rest = [n for n in blocks if n not in scale]
            pe_s, ac_s, dv_s = steps("pe", blocks), steps("act", rest), steps("dve", scale)
            for j, f in enumerate(first):
                free_at[f] = (pe_s, blocks[min(j * KC + KC, count) - 1])

            def pe(e, c):
                for i, n in enumerate(blocks):
                    ring_wait(e, first[i // KC])
                    if i >= 8:
                        who = dv_s if blocks[i - 8] in scale else ac_s
                        who.wait(e, blocks[i - 8])
                    pe_s.mark(nc.tensor.matmul(PS[:, i % 8, :], ones, slot(first[i // KC])[:, i % KC, :],
                                               start=True, stop=True), n)
                return pe_s

            def dest(n):
                return MOD[:, n // 2, (n % 2) * CW:(n % 2) * CW + CW], PS[:, blocks.index(n) % 8, :]

            def act(e, c):
                for n in rest:
                    pe_s.wait(e, n)
                    ac_s.mark(nc.scalar.copy(*dest(n)), n)
                return ac_s

            def dve(e, c):
                for n in scale:
                    pe_s.wait(e, n)
                    dv_s.mark(nc.vector.tensor_scalar_add(*dest(n), 1.0), n)
                return dv_s
            return dict(pe=pe, act=act, dve=dve)

        gain_loads = []

        def load_gain(g_dram):
            gain_loads.append(g_dram)
            n = len(gain_loads)

            def pool(e, c):
                e.dma_start(GT, g_dram.unsqueeze(0).broadcast_to([P, D])).then_inc(s_gain, 16)
                e.wait_ge(s_gain, 16 * n)
            return pool

        def norm_T_stage(tag, srcs, dest, off):
            n = len(srcs)
            gb = GT
            A = arena(off + D, 2, D)
            sq = arena(off + 3 * D, D)
            HN = arena(off + 4 * D, n, D)
            ac_s = steps("act", [x for t in range(n) for x in (("ss", t), ("rt", t))] +
                         [("ev", t, 1) for t in range(n)])
            dv_s = steps("dve", [("hn", t) for t in range(n)] + [("ev", t, 0) for t in range(n)])
            pe_s = steps("pe", [("tr", t, b) for t in range(n) for b in range(2)])

            def act(e, c):
                for t in range(n):
                    if t:
                        ac_s.wait(e, ("ss", t - 1))
                    ac_s.mark(nc.scalar.activation(sq, srcs[t][0], ACT.Square, accum_out=sm[:, t:t + 1]), ("ss", t))
                    ac_s.wait(e, ("ss", t))
                    ac_s.mark(nc.scalar.activation(sm[:, 8 + t:9 + t], sm[:, t:t + 1], ACT.Sqrt,
                                                   bias=eps_col, scale=1.0 / D), ("rt", t))
                for t in range(n):
                    pe_s.wait(e, ("tr", t, 1))
                    ac_s.mark(nc.scalar.copy(dest[:, 4:8, t * P:(t + 1) * P],
                                             PS[:, (2 * t + 1) % 8, :].rearrange("p (k t) -> p k t", k=4)),
                              ("ev", t, 1))
                return ac_s

            def dve(e, c):
                for a in range(n // NT):
                    c(nc.vector.tensor_tensor(A[:, a, :], gb, srcs[a * NT][1], ALU.mult))
                for t, (rows, sc, sh) in enumerate(srcs):
                    ac_s.wait(e, ("rt", t))
                    c(nc.vector.reciprocal(sm[:, 16 + t:17 + t], sm[:, 8 + t:9 + t]))
                    c(nc.vector.scalar_tensor_tensor(HN[:, t, :], rows, sm[:, 16 + t:17 + t],
                                                     A[:, t // NT, :], ALU.mult, ALU.mult))
                    dv_s.mark(nc.vector.tensor_tensor(HN[:, t, :], HN[:, t, :], sh, ALU.add), ("hn", t))
                for t in range(n):
                    pe_s.wait(e, ("tr", t, 0))
                    dv_s.mark(nc.vector.tensor_copy(dest[:, 0:4, t * P:(t + 1) * P],
                                                    PS[:, (2 * t) % 8, :].rearrange("p (k t) -> p k t", k=4)),
                              ("ev", t, 0))
                return dv_s

            def pe(e, c):
                for t in range(n):
                    dv_s.wait(e, ("hn", t))
                    v = HN[:, t, :].rearrange("p (c k) -> p k c", k=KC)
                    for b in range(2):
                        for k in range(4):
                            ins = nc.tensor.transpose(PS[:, (2 * t + b) % 8, k * P:(k + 1) * P], v[:, 4 * b + k, :],
                                                      ident)
                        pe_s.mark(ins, ("tr", t, b))
                return pe_s

            stage(tag, act=act, dve=dve, pe=pe)

        eps_col = sm[:, 255:256]

        ctxr = arena(24576 - 2 * D, NT, D)
        modc = arena(24576 - 4 * D, 2, D)
        s_x = sem("s_x")
        gain_a = load_gain(io["norm_g0"])

        def load_start(e, c):
            for n, name in enumerate(("ident", "ones", "iota")):
                e.dma_start(cst[:, n * P:(n + 1) * P], io["const"][:, CAT[name][0]:CAT[name][0] + P]).then_inc(s_cst, 16)
            e.dma_start(X, io["x"].rearrange("o (t p) d -> p (o t) d", p=P)).then_inc(s_x, 16)
            e.dma_start(ctxr, io["ctx"].rearrange("o (t p) d -> p (o t) d", p=P)).then_inc(s_x, 16)
            gain_a(e, c)
            e.wait_ge(s_x, 32)
            e.wait_ge(s_cst, 48)

        ada_stage(modc)
        hnT = arena(0, KC, 2 * T)
        sc_x, sh_x, sc_c, sh_c = MOD[:, 1, :], MOD[:, 0, :], modc[:, 1, :], modc[:, 0, :]
        norm_T_stage("norm_a", [(X[:, 0, :], sc_x, sh_x), (X[:, 1, :], sc_x, sh_x),
                                (ctxr[:, 0, :], sc_c, sh_c), (ctxr[:, 1, :], sc_c, sh_c)],
                     hnT, 4096)


        def release_ring(after):
            k = [s[0] for s in stages].index(after) + 1
            stream.append(lambda sp: sp.wait_ge(s_bar, 4 * k))

        def out_proj_stage(tag, rows, rT, first, gain, tmp, pool):
            tr = [("tr", t, b) for t in range(NT) for b in range(2)]
            mmn = [("mm", s, t) for s in range(2) for t in range(NT)]
            pe_s = steps("pe", tr + mmn)
            dv_s = steps("dve", tr[0::2] + mmn)
            ac_s = steps("act", tr[1::2])
            for s in range(2):
                free_at[first + s] = (pe_s, ("mm", s, NT - 1))

            def pe(e, c):
                for i, (_, t, b) in enumerate(tr):
                    v = rows[:, t, :].rearrange("p (c k) -> p k c", k=KC)
                    for k in range(4):
                        ins = nc.tensor.transpose(PS[:, i, k * P:(k + 1) * P], v[:, 4 * b + k, :], ident)
                    pe_s.mark(ins, tr[i])
                dv_s.wait(e, tr[2])
                ac_s.wait(e, tr[3])
                for i, (_, s, t) in enumerate(mmn):
                    ring_wait(e, first + s)
                    for k in range(KC):
                        ins = nc.tensor.matmul(PS[:, 4 + i, :], rT[:, k, t * P:(t + 1) * P], slot(first + s)[:, k, :],
                                               start=(k == 0), stop=(k == KC - 1))
                    pe_s.mark(ins, mmn[i])
                return pe_s

            def evac(op, i):
                _, t, b = tr[i]
                return op(rT[:, 4 * b:4 * b + 4, t * P:(t + 1) * P], PS[:, i, :].rearrange("p (k t) -> p k t", k=4))

            def act(e, c):
                for i in (1, 3):
                    pe_s.wait(e, tr[i])
                    ac_s.mark(evac(nc.scalar.copy, i), tr[i])
                return ac_s

            def dve(e, c):
                for i in (0, 2):
                    pe_s.wait(e, tr[i])
                    dv_s.mark(evac(nc.vector.tensor_copy, i), tr[i])
                for i, (_, s, t) in enumerate(mmn):
                    pe_s.wait(e, mmn[i])
                    cols = slice(s * CW, (s + 1) * CW)
                    c(nc.vector.tensor_tensor(tmp, PS[:, 4 + i, :], gain[:, cols], ALU.mult))
                    dv_s.mark(nc.vector.tensor_tensor(X[:, t, cols], X[:, t, cols], tmp, ALU.add), mmn[i])
                    dv_s.wait(e, mmn[i])
                return dv_s

            stage(tag, pe=pe, act=act, dve=dve, pool=pool)

        NQ = 4
        kT = arena(10240, DN_H, 2 * T)
        qT = arena(14336, DN_H, T)
        Krow = arena(16384, NQ, DN_H, P)
        Vrow = arena(20480, NQ, DN_H, P)
        gate = arena(24576, NT, D)
        vT = arena(4096, DN_H, 2 * T)
        XPAD = ROWS * (ROW_W + 2 * DN_PAD)
        CPAD = T + 2 * DN_PAD
        zpad = arena(16384, 2, XPAD + CPAD)
        conv = arena(16384 + 2 * (XPAD + CPAD), 2, 2 * T)
        cw = arena(19000, 24, DN_TAPS)
        wba = arena(19200, KC, 32)
        first_w = ring_loads(io["dn_w"], 8)
        s_dnin = sem("s_dnin")
        ba = sm[:, 0:NQ * 32].rearrange("p (t c) -> p t c", t=NQ)
        rows_ev = [("row", s, t) for s in range(2) for t in range(NT)]
        dn1_pe = steps("pe", [("z", n) for n in range(24)] + rows_ev + ["ba"])
        dn1_ac = steps("act", [x for n in range(24) for x in ([("pad", n)] + ([("silu", n - 1)] if n else []))] +
                       [("silu", 23)] + rows_ev)
        dn1_dv = steps("dve", ["zero"] + [("conv", n) for n in range(24)] + ["ba"])
        for s in range(6):
            free_at[first_w + s] = (dn1_pe, ("z", 4 * s + 3))
        for s in range(2):
            free_at[first_w + 6 + s] = (dn1_pe, ("row", s, NT - 1))

        def pool_dn1(e, c):
            e.dma_start(cw, io["dn_cw"].rearrange("p (n t) -> p n t", n=24)).then_inc(s_dnin, 16)
            e.dma_start(wba, io["dn_wba"].rearrange("p (k n) -> p k n", k=KC)).then_inc(s_dnin, 16)
            e.wait_ge(s_dnin, 32)

        def pe_dn1(e, c):
            for n in range(24):
                s = n // 4
                ring_wait(e, first_w + s)
                if n >= 4:
                    dn1_ac.wait(e, ("pad", n - 4))
                w = slot(first_w + s)
                toks = T if n < DN_H else 2 * T
                for k in range(KC):
                    ins = nc.tensor.matmul(PS[:, n % 4, 0:toks], w[:, k, (n % 4) * P:(n % 4 + 1) * P],
                                           hnT[:, k, 0:toks], start=(k == 0), stop=(k == KC - 1))
                dn1_pe.mark(ins, ("z", n))
            for s in range(2):
                ring_wait(e, first_w + 6 + s)
                for t in range(NT):
                    for k in range(KC):
                        ins = nc.tensor.matmul(PS[:, 4 + 2 * s + t, :], hnT[:, k, t * P:(t + 1) * P],
                                               slot(first_w + 6 + s)[:, k, :], start=(k == 0), stop=(k == KC - 1))
                    dn1_pe.mark(ins, ("row", s, t))
            e.wait_ge(s_dnin, 32)
            dn1_ac.wait(e, ("pad", 20))
            for t in range(NQ):
                for k in range(KC):
                    ins = nc.tensor.matmul(PS[:, 0, t * 32:(t + 1) * 32], hnT[:, k, t * P:(t + 1) * P], wba[:, k, :],
                                           start=(k == 0), stop=(k == KC - 1))
            dn1_pe.mark(ins, "ba")
            return dn1_pe

        def pad_views(buf):
            return (buf[:, 0:XPAD].rearrange("p (r w) -> p r w", r=ROWS), buf[:, XPAD:XPAD + CPAD])

        def act_dn1(e, c):
            dn1_dv.wait(e, "zero")

            def silu(n):
                dn1_dv.wait(e, ("conv", n))
                toks = T if n < DN_H else 2 * T
                dest = (qT, kT, vT)[n // DN_H]
                dn1_ac.mark(nc.scalar.activation(dest[:, n % DN_H, :], conv[:, n % 2, 0:toks], ACT.Silu), ("silu", n))
            for n in range(24):
                dn1_pe.wait(e, ("z", n))
                if n >= 2:
                    dn1_dv.wait(e, ("conv", n - 2))
                xv, cv = pad_views(zpad[:, n % 2])
                ins = nc.scalar.copy(xv[:, :, DN_PAD:DN_PAD + ROW_W],
                                     PS[:, n % 4, 0:T].rearrange("p (r w) -> p r w", r=ROWS))
                if n >= DN_H:
                    ins = nc.scalar.copy(cv[:, DN_PAD:DN_PAD + T], PS[:, n % 4, T:2 * T])
                dn1_ac.mark(ins, ("pad", n))
                if n:
                    silu(n - 1)
            silu(23)
            for s in range(2):
                for t in range(NT):
                    dn1_pe.wait(e, ("row", s, t))
                    dn1_ac.mark(nc.scalar.activation(gate[:, t, s * CW:(s + 1) * CW], PS[:, 4 + 2 * s + t, :], ACT.Silu),
                                ("row", s, t))
            return dn1_ac

        def dve_dn1(e, c):
            dn1_dv.mark(nc.vector.memset(zpad, 0.0), "zero")
            e.wait_ge(s_dnin, 32)
            for n in range(24):
                dn1_ac.wait(e, ("pad", n))
                if n >= 2:
                    dn1_ac.wait(e, ("silu", n - 2))
                xv, cv = pad_views(zpad[:, n % 2])
                xo = conv[:, n % 2, 0:T].rearrange("p (r w) -> p r w", r=ROWS)
                co = conv[:, n % 2, T:2 * T]
                pairs = [(xo, xv)] + ([(co, cv)] if n >= DN_H else [])
                for j in range(DN_TAPS):
                    for o, v in pairs:
                        src = v[:, :, j:j + ROW_W] if o is xo else v[:, j:j + T]
                        tap = cw[:, n, j:j + 1]
                        if j == 0:
                            ins = nc.vector.tensor_scalar(o, src, tap, None, ALU.mult)
                        else:
                            ins = nc.vector.scalar_tensor_tensor(o, src, tap, o, ALU.mult, ALU.add)
                        if j == DN_TAPS - 1 and o is pairs[-1][0]:
                            dn1_dv.mark(ins, ("conv", n))
                        else:
                            c(ins)
            dn1_pe.wait(e, "ba")
            dn1_dv.mark(nc.vector.tensor_copy(ba, PS[:, 0, 0:NQ * 32].rearrange("p (t c) -> p t c", t=NQ)), "ba")
            return dn1_dv

        stage("dn_proj", pool=pool_dn1, pe=pe_dn1, act=act_dn1, dve=dve_dn1)

        masks = idx.rearrange("p a t -> p (a t)")
        MASK = {n: masks[:, i * P:(i + 1) * P]
                for i, n in enumerate(("inc_f", "inc_b", "strict_f", "strict_b", "block", "off"))}
        sq = hT.rearrange("p k t -> p (k t)")[:, 0:1024].rearrange("p (a c) -> p a c", a=2)
        rn = hT.rearrange("p k t -> p (k t)")[:, 1024:2048].rearrange("p (a c) -> p a c", a=2)
        units = [(qT[:, 2 * b:2 * b + 2, :], True) for b in range(4)] + [(kT[:, h, :], False) for h in range(DN_H)]
        NU = len(units)
        dec = arena(8192, 8, NQ, 16)
        beta, g16, Gc, Gtot, eG, ekd, egl, nbeG = [dec[:, j] for j in range(8)]
        scr = arena(8192 + 512, 4, NQ, 16)
        dtb, ala = arena(8192 + 768, 16), arena(8192 + 784, 16)
        s_dn2in = sem("s_dn2in")
        trs = [(w, t, b) for w in ("k", "v") for t in range(NQ) for b in range(2)]
        dn2_pe = steps("pe", ["G"] + [("ss", i) for i in range(NU)] + trs)
        dn2_ac = steps("act", ["beta", "alog", "abs_e", "ln"] + [x for i in range(NU) for x in (("sq", i), ("rt", i))] +
                       ["eG", "ekd", "egl"] + trs[1::2])
        dn2_dv = steps("dve", ["neg", "ln1", "g", "Gc"] + [("unit", i) for i in range(NU)] + ["dec"] + trs[0::2])

        def pool_dn2(e, c):
            for n, m in MASK.items():
                e.dma_start(m, io["const"][:, CAT[n][0]:CAT[n][0] + P]).then_inc(s_dn2in, 16)
            e.dma_start(dtb, io["dn_dt"].unsqueeze(0).broadcast_to([P, 16])).then_inc(s_dn2in, 16)
            e.dma_start(ala, io["dn_alog"].unsqueeze(0).broadcast_to([P, 16])).then_inc(s_dn2in, 16)
            e.wait_ge(s_dn2in, 128)

        def act_dn2(e, c):
            e.wait_ge(s_dn2in, 128)
            dn2_ac.mark(nc.scalar.activation(beta, ba[:, :, 0:16], ACT.Sigmoid), "beta")
            dn2_ac.mark(nc.scalar.activation(ala, ala, ACT.Exp), "alog")
            dn2_dv.wait(e, "neg")
            dn2_ac.mark(nc.scalar.activation(scr[:, 1], scr[:, 1], ACT.Exp), "abs_e")
            dn2_dv.wait(e, "ln1")
            dn2_ac.mark(nc.scalar.activation(scr[:, 1], scr[:, 1], ACT.Ln), "ln")
            for i, (u, _) in enumerate(units):
                if i >= 2:
                    dn2_dv.wait(e, ("unit", i - 2))
                    dn2_pe.wait(e, ("ss", i - 2))
                shape = sq[:, i % 2, :].rearrange("p (a c) -> p a c", a=2) if i < 4 else sq[:, i % 2, :]
                dn2_ac.mark(nc.scalar.activation(shape, u, ACT.Square), ("sq", i))
                dn2_pe.wait(e, ("ss", i))
                dn2_ac.mark(nc.scalar.activation(rn[:, i % 2, :], PS[:, 1 + i % 3, :], ACT.Sqrt, bias=eps_col), ("rt", i))
            dn2_dv.wait(e, "Gc")
            dn2_ac.mark(nc.scalar.activation(eG, Gc, ACT.Exp), "eG")
            dn2_ac.mark(nc.scalar.activation(ekd, ekd, ACT.Exp), "ekd")
            dn2_ac.mark(nc.scalar.activation(egl, Gtot, ACT.Exp), "egl")
            for i, (w, t, b) in list(enumerate(trs))[1::2]:
                dn2_pe.wait(e, (w, t, b))
                dst = (Krow if w == "k" else Vrow)[:, t, 4 * b:4 * b + 4, :]
                dn2_ac.mark(nc.scalar.copy(dst, PS[:, 4 + i % 4, :].rearrange("p (h d) -> p h d", h=4)), (w, t, b))
            return dn2_ac

        def dve_dn2(e, c):
            e.wait_ge(s_dn2in, 128)
            c(nc.vector.tensor_tensor(scr[:, 0], ba[:, :, 16:32], bc(dtb, 1, NQ), ALU.add))
            c(nc.vector.tensor_scalar(scr[:, 2], scr[:, 0], -1.0, None, ALU.mult))
            dn2_dv.mark(nc.vector.tensor_tensor(scr[:, 1], scr[:, 0], scr[:, 2], ALU.min), "neg")
            dn2_ac.wait(e, "abs_e")
            dn2_dv.mark(nc.vector.tensor_scalar_add(scr[:, 1], scr[:, 1], 1.0), "ln1")
            dn2_ac.wait(e, "ln")
            c(nc.vector.scalar_tensor_tensor(scr[:, 1], scr[:, 0], 0.0, scr[:, 1], ALU.max, ALU.add))
            c(nc.vector.tensor_scalar(ala, ala, -1.0, None, ALU.mult))
            dn2_dv.mark(nc.vector.tensor_tensor(g16, scr[:, 1], bc(ala, 1, NQ), ALU.mult), "g")
            dn2_pe.wait(e, "G")
            c(nc.vector.tensor_copy(Gc, PS[:, 0, 0:64].rearrange("p (t c) -> p t c", t=NQ)))
            c(nc.vector.tensor_copy(Gtot, PS[:, 0, 64:128].rearrange("p (t c) -> p t c", t=NQ)))
            dn2_dv.mark(nc.vector.tensor_tensor(ekd, Gtot, Gc, ALU.subtract), "Gc")
            for i, (u, is_q) in enumerate(units):
                dn2_ac.wait(e, ("rt", i))
                c(nc.vector.reciprocal(rn[:, i % 2, :], rn[:, i % 2, :]))
                r = rn[:, i % 2, :]
                if i < 4:
                    r = r.rearrange("p (a c) -> p a c", a=2)
                ins = nc.vector.scalar_tensor_tensor(u, u, float(P) ** -0.5 if is_q else 1.0, r, ALU.mult, ALU.mult)
                dn2_dv.mark(ins, ("unit", i))
            dn2_ac.wait(e, "eG")
            dn2_dv.mark(nc.vector.scalar_tensor_tensor(nbeG, beta, -1.0, eG, ALU.mult, ALU.mult), "dec")
            for i, (w, t, b) in list(enumerate(trs))[0::2]:
                dn2_pe.wait(e, (w, t, b))
                dst = (Krow if w == "k" else Vrow)[:, t, 4 * b:4 * b + 4, :]
                dn2_dv.mark(nc.vector.tensor_copy(dst, PS[:, 4 + i % 4, :].rearrange("p (h d) -> p h d", h=4)), (w, t, b))
            return dn2_dv

        def pe_dn2(e, c):
            dn2_dv.wait(e, "g")
            e.wait_ge(s_dn2in, 128)
            for t in range(NQ):
                for d, m in enumerate(("inc_f", "inc_b")):
                    o = t * 16 + d * 8
                    nc.tensor.matmul(PS[:, 0, o:o + 8], MASK[m], g16[:, t, d * 8:d * 8 + 8], start=True, stop=True)
                ins = nc.tensor.matmul(PS[:, 0, 64 + t * 16:80 + t * 16], ones, g16[:, t, :], start=True, stop=True)
            dn2_pe.mark(ins, "G")
            for i in range(NU):
                dn2_ac.wait(e, ("sq", i))
                if i >= 3:
                    dn2_ac.wait(e, ("rt", i - 3))
                dn2_pe.mark(nc.tensor.matmul(PS[:, 1 + i % 3, :], ones, sq[:, i % 2, :], start=True, stop=True), ("ss", i))
            dn2_dv.wait(e, ("unit", NU - 1))
            for i, (w, t, b) in enumerate(trs):
                if i >= 4:
                    (dn2_dv if i % 2 == 0 else dn2_ac).wait(e, trs[i - 4])
                src = kT if w == "k" else vT
                for h in range(4):
                    ins = nc.tensor.transpose(PS[:, 4 + i % 4, h * P:(h + 1) * P],
                                              src[:, 4 * b + h, t * P:(t + 1) * P], ident)
                dn2_pe.mark(ins, (w, t, b))
            return dn2_pe

        stage("dn_unit", pool=pool_dn2, pe=pe_dn2, act=act_dn2, dve=dve_dn2)

        HG = 4
        NAMES = ("E", "DT", "A", "Aoff", "p0", "p1", "q0", "q1", "t0", "t1", "kb", "vb", "kd", "wT", "qg", "qa")

        def four(base, i):
            return ring[:, base + i * 512:base + (i + 1) * 512].rearrange("p (h c) -> p h c", h=HG)
        buf = [{n: four(SLOT, i) for i, n in enumerate(NAMES)}, {n: four(RB, i) for i, n in enumerate(NAMES)}]
        state = ring[:, 0:2 * DN_H * P].rearrange("p (d h c) -> p d h c", d=2, h=DN_H)
        O = hT.rearrange("p k t -> p (k t)").rearrange("p (t h d) -> p t h d", t=NT, h=DN_H)
        ORDER = [[2, 3, 0, 1], [3, 2, 1, 0]]
        groups = [(st, hg) for st in range(4) for hg in range(DN_H // HG)]
        ROUNDS = 5
        pe_names, ac_names, dv_names = [], [], []
        for gi, (st, hg) in enumerate(groups):
            xt = st >= 2
            pn = ["Gr", "KK"] + (["QK"] if xt else []) + ["A", "q0"]
            for r in range(ROUNDS):
                pn += [("p", r)] + ([("q", r)] if r < ROUNDS - 1 else []) + [("t", r)]
            pn += ["Tb", "Z", "R", "wT", "vn", "ds"] + (["o"] if xt else [])
            an = ["DT"] + (["eG"] if xt else []) + ["q0"] + [("p", r) for r in range(ROUNDS)] + ["Tb", "wT"]
            dn = ["R", "E", "Araw", "A", "p0", "t0"] + (["qx"] if xt else [])
            for r in range(ROUNDS):
                dn += ([("q", r)] if r < ROUNDS - 1 else []) + [("t", r)]
            dn += ["Z", "Tinv", "vn", "s"] + (["o"] if xt else [])
            pe_names += [(gi, n) for n in pn]
            ac_names += [(gi, n) for n in an]
            dv_names += [(gi, n) for n in dn]
        dl_pe = [Steps(sem(f"dl_pe{d}"), pe_names) for d in range(2)]
        dl_ac = [Steps(sem(f"dl_act{d}"), ac_names) for d in range(2)]
        dl_dv = [Steps(sem(f"dl_dve{d}"), dv_names) for d in range(2)]
        BANK = {"Gr": 0, "KK": 1, "QK": 2, "A": 3, "q0": 1, "Tb": 1, "Z": 2, "R": 3, "wT": 1, "vn": 2, "ds": 3, "o": 0}

        def bank(d, name):
            if isinstance(name, tuple):
                b = {"p": 2, "q": 3, "t": 0}[name[0]]
            else:
                b = BANK[name]
            return PS[:, 4 * d + b, :].rearrange("p (h c) -> p h c", h=HG)

        def dl_pe_prog(e, c):
            for gi, (st, hg) in enumerate(groups):
                xt = st >= 2
                heads = [hg * HG + h for h in range(HG)]
                tile = [ORDER[d][st] for d in range(2)]

                def each(name, f, before=()):
                    for d in range(2):
                        for s, n in before:
                            s[d].wait(e, (gi, n))
                        for h in range(HG):
                            ins = f(d, h, bank(d, name)[:, h, :])
                        dl_pe[d].mark(ins, (gi, name))

                def mm(d, o, a, b_):
                    return nc.tensor.matmul(o, a, b_, start=True, stop=True)

                if gi:
                    for d in range(2):
                        last = "o" if groups[gi - 1][0] >= 2 else "s"
                        dl_dv[d].wait(e, (gi - 1, last))
                for d in range(2):
                    dl_dv[d].wait(e, (gi, "R"))
                    dl_pe[d].mark(nc.tensor.matmul(PS[:, 4 * d, :], ones, buf[d]["E"].rearrange("p h c -> p (h c)"),
                                                   start=True, stop=True), (gi, "Gr"))
                tk = [slice(t * P, (t + 1) * P) for t in tile]
                each("KK", lambda d, h, o: mm(d, o, kT[:, heads[h], tk[d]], kT[:, heads[h], tk[d]]))
                if xt:
                    each("QK", lambda d, h, o: mm(d, o, kT[:, heads[h], tk[d]], qT[:, heads[h], tk[d]]))
                each("A", lambda d, h, o: nc.tensor.transpose(o, buf[d]["wT"][:, h, :], ident), [(dl_dv, "Araw")])
                each("q0", lambda d, h, o: nc.tensor.transpose(o, buf[d]["p0"][:, h, :], ident), [(dl_dv, "p0")])
                for r in range(ROUNDS):
                    cur, new = r % 2, 1 - r % 2
                    need = [(dl_ac, "q0"), (dl_dv, "p0")] if r == 0 else [(dl_ac, ("p", r - 1)), (dl_dv, ("q", r - 1))]
                    if r == 0 and xt:
                        need.append((dl_dv, "qx"))
                    each(("p", r), lambda d, h, o: mm(d, o, buf[d][f"q{cur}"][:, h, :], buf[d][f"p{cur}"][:, h, :]), need)
                    if r < ROUNDS - 1:
                        each(("q", r), lambda d, h, o: mm(d, o, buf[d][f"p{cur}"][:, h, :], buf[d][f"q{cur}"][:, h, :]),
                             [(dl_dv, "A")] if r == 0 else [])
                    each(("t", r), lambda d, h, o: mm(d, o, buf[d][f"p{new}"][:, h, :], buf[d][f"t{cur}"][:, h, :]),
                         [(dl_ac, ("p", r)), (dl_dv, "t0" if r == 0 else ("t", r - 1))])
                tl = f"t{ROUNDS % 2}"
                each("Tb", lambda d, h, o: nc.tensor.transpose(o, buf[d][tl][:, h, :], ident), [(dl_dv, ("t", ROUNDS - 1))])
                each("Z", lambda d, h, o: mm(d, o, buf[d]["Aoff"][:, h, :], buf[d][tl][:, h, :]))
                each("R", lambda d, h, o: mm(d, o, buf[d]["q0"][:, h, :], buf[d]["q1"][:, h, :]),
                     [(dl_ac, "Tb"), (dl_dv, "Z")])
                tf = "p0"
                each("wT", lambda d, h, o: mm(d, o, buf[d]["kb"][:, h, :], buf[d][tf][:, h, :]), [(dl_dv, "Tinv")])

                def vn(d, h, o):
                    nc.tensor.matmul(o, buf[d][tf][:, h, :], buf[d]["vb"][:, h, :], start=True, stop=False)
                    return nc.tensor.matmul(o, buf[d]["wT"][:, h, :], state[:, d, heads[h], :], start=False, stop=True)
                each("vn", vn, [(dl_ac, "wT")])
                each("ds", lambda d, h, o: mm(d, o, buf[d]["kd"][:, h, :], buf[d]["A"][:, h, :]), [(dl_dv, "vn")])
                if xt:
                    def out(d, h, o):
                        nc.tensor.matmul(o, buf[d]["qg"][:, h, :], buf[d]["t0"][:, h, :], start=True, stop=False)
                        return nc.tensor.matmul(o, buf[d]["qa"][:, h, :], buf[d]["A"][:, h, :], start=False, stop=True)
                    each("o", out)
            e.wait_ge(dl_pe[0].sem, dl_pe[0].n)
            return dl_pe[1]

        def dl_act_prog(e, c):
            for gi, (st, hg) in enumerate(groups):
                xt = st >= 2
                for d in range(2):
                    dl_dv[d].wait(e, (gi, "E"))
                    dl_ac[d].mark(nc.scalar.activation(buf[d]["DT"], buf[d]["DT"], ACT.Exp), (gi, "DT"))
                    if xt:
                        dl_ac[d].mark(nc.scalar.activation(buf[d]["qg"], bank(d, "Gr"), ACT.Exp), (gi, "eG"))
                for d in range(2):
                    dl_pe[d].wait(e, (gi, "q0"))
                    dl_ac[d].mark(nc.scalar.copy(buf[d]["q0"], bank(d, "q0")), (gi, "q0"))
                for r in range(ROUNDS):
                    new = 1 - r % 2
                    for d in range(2):
                        dl_pe[d].wait(e, (gi, ("p", r)))
                        if r:
                            dl_pe[d].wait(e, (gi, ("t", r - 1)))
                        dl_ac[d].mark(nc.scalar.copy(buf[d][f"p{new}"], bank(d, ("p", r))), (gi, ("p", r)))
                for d in range(2):
                    dl_pe[d].wait(e, (gi, "Tb"))
                    dl_ac[d].mark(nc.scalar.copy(buf[d]["q0"], bank(d, "Tb")), (gi, "Tb"))
                for d in range(2):
                    dl_pe[d].wait(e, (gi, "wT"))
                    dl_ac[d].mark(nc.scalar.copy(buf[d]["wT"], bank(d, "wT")), (gi, "wT"))
            e.wait_ge(dl_ac[0].sem, dl_ac[0].n)
            return dl_ac[1]

        def dl_dve_prog(e, c):
            c(nc.vector.memset(state, 0.0))
            V = nc.vector
            for gi, (st, hg) in enumerate(groups):
                xt = st >= 2
                hs = slice(hg * HG, hg * HG + HG)
                tile = [ORDER[d][st] for d in range(2)]
                col = [slice(d * DN_H + hg * HG, d * DN_H + hg * HG + HG) for d in range(2)]
                fb = "fb"
                for d in range(2):
                    if gi and groups[gi - 1][0] >= 2:
                        dl_pe[d].wait(e, (gi - 1, "o"))
                    dl_dv[d].mark(V.tensor_tensor(buf[d]["E"], bc(MASK["inc_" + fb[d]], 1, HG),
                                                  bc(g16[:, tile[d], col[d]], 2, P), ALU.mult), (gi, "R"))
                    B = buf[d]
                    dec = lambda a: bc(a[:, tile[d], col[d]], 2, P)
                    c(V.tensor_tensor(B["kb"], Krow[:, tile[d], hs, :], dec(nbeG), ALU.mult))
                    c(V.tensor_tensor(B["vb"], Vrow[:, tile[d], hs, :], dec(beta), ALU.mult))
                    c(V.tensor_tensor(B["kd"], Krow[:, tile[d], hs, :], dec(ekd), ALU.mult))
                for d in range(2):
                    dec = lambda a: bc(a[:, tile[d], col[d]], 2, P)
                    dl_pe[d].wait(e, (gi, "Gr"))
                    c(V.tensor_tensor(buf[d]["DT"], bank(d, "Gr"), dec(Gc), ALU.subtract))
                    dl_dv[d].mark(V.tensor_scalar_min(buf[d]["DT"], buf[d]["DT"], 0.0), (gi, "E"))
                for d in range(2):
                    B = buf[d]
                    dl_ac[d].wait(e, (gi, "DT"))
                    c(V.tensor_tensor(B["DT"], B["DT"], bc(MASK["inc_" + fb[d]], 1, HG), ALU.mult))
                    dl_pe[d].wait(e, (gi, "KK"))
                    c(V.tensor_tensor(B["wT"], bank(d, "KK"), B["DT"], ALU.mult))
                    dl_dv[d].mark(V.tensor_tensor(B["wT"], B["wT"], bc(MASK["strict_" + fb[d]], 1, HG), ALU.mult),
                                  (gi, "Araw"))
                for d in range(2):
                    B = buf[d]
                    dl_pe[d].wait(e, (gi, "A"))
                    dl_dv[d].mark(V.tensor_tensor(B["A"], bank(d, "A"), bc(beta[:, tile[d], col[d]], 2, P), ALU.mult),
                                  (gi, "A"))
                    dl_dv[d].wait(e, (gi, "A"))
                    dl_dv[d].mark(V.tensor_tensor(B["p0"], B["A"], bc(MASK["block"], 1, HG), ALU.mult), (gi, "p0"))
                    c(V.tensor_tensor(B["Aoff"], B["A"], bc(MASK["off"], 1, HG), ALU.mult))
                for d in range(2):
                    dl_ac[d].wait(e, (gi, "q0"))
                    dl_dv[d].mark(V.tensor_tensor(buf[d]["t0"], bc(ident, 1, HG), buf[d]["q0"], ALU.subtract),
                                  (gi, "t0"))
                    if xt:
                        dl_ac[d].wait(e, (gi, "eG"))
                        tk = slice(tile[d] * P, tile[d] * P + P)
                        c(V.tensor_tensor(buf[d]["qg"], buf[d]["qg"], qT[:, hs, tk], ALU.mult))
                        dl_dv[d].mark(V.tensor_tensor(buf[d]["qa"], bank(d, "QK"), buf[d]["DT"], ALU.mult), (gi, "qx"))
                for r in range(ROUNDS):
                    cur, new = r % 2, 1 - r % 2
                    for d in range(2):
                        if r < ROUNDS - 1:
                            dl_pe[d].wait(e, (gi, ("q", r)))
                            dl_dv[d].mark(V.tensor_copy(buf[d][f"q{new}"], bank(d, ("q", r))), (gi, ("q", r)))
                    for d in range(2):
                        dl_pe[d].wait(e, (gi, ("t", r)))
                        dl_dv[d].mark(V.tensor_tensor(buf[d][f"t{new}"], buf[d][f"t{cur}"], bank(d, ("t", r)), ALU.add),
                                      (gi, ("t", r)))
                tl = f"t{ROUNDS % 2}"
                for d in range(2):
                    dl_pe[d].wait(e, (gi, "Z"))
                    dl_dv[d].mark(V.tensor_copy(buf[d]["q1"], bank(d, "Z")), (gi, "Z"))
                for d in range(2):
                    dl_pe[d].wait(e, (gi, "R"))
                    dl_dv[d].mark(V.tensor_tensor(buf[d]["p0"], buf[d][tl], bank(d, "R"), ALU.subtract), (gi, "Tinv"))
                    if xt:
                        c(V.tensor_copy(buf[d]["t0"], state[:, d, hs, :]))
                for d in range(2):
                    dl_pe[d].wait(e, (gi, "vn"))
                    dl_dv[d].mark(V.tensor_copy(buf[d]["A"], bank(d, "vn")), (gi, "vn"))
                    c(V.tensor_tensor(state[:, d, hs, :], state[:, d, hs, :], bc(egl[:, tile[d], col[d]], 2, P),
                                      ALU.mult))
                for d in range(2):
                    dl_pe[d].wait(e, (gi, "ds"))
                    dl_dv[d].mark(V.tensor_tensor(state[:, d, hs, :], state[:, d, hs, :], bank(d, "ds"), ALU.add),
                                  (gi, "s"))
                if xt:
                    for d in range(2):
                        dl_pe[d].wait(e, (gi, "o"))
                        o = O[:, tile[d], hs, :]
                        if st == 2:
                            ins = V.tensor_copy(o, bank(d, "o"))
                        else:
                            ins = V.tensor_tensor(o, o, bank(d, "o"), ALU.add)
                        dl_dv[d].mark(ins, (gi, "o"))
            e.wait_ge(dl_dv[0].sem, dl_dv[0].n)
            return dl_dv[1]

        ngb = arena(8192 + 800, P)
        s_ng = sem("s_ng")

        def pool_delta(e, c):
            e.dma_start(ngb, io["dn_ng"].unsqueeze(0).broadcast_to([P, P])).then_inc(s_ng, 16)
            pool_mod(e, c)
            e.wait_ge(s_ng, 16)
        stage("dn_delta", pe=dl_pe_prog, act=dl_act_prog, dve=dl_dve_prog, pool=pool_delta)

        release_ring("dn_proj")
        stream.append(load_mod)
        release_ring("dn_delta")
        osq = arena(10240 + P, 2, DN_H, P)
        dno_dv = steps("dve", ["ss"] + ["y"])
        dno_ac = steps("act", ["rt"])
        mod_mlp = mod_sum(0, list(range(NOW, 12)))
        first_wo = ring_loads(io["dn_wo"], 2)

        def dve_dno(e, c):
            V = nc.vector
            c(V.tensor_tensor(osq, O, O, ALU.mult))
            ss = sm[:, 128:144].rearrange("p (t h) -> p t h", t=NT)
            dno_dv.mark(V.tensor_reduce(ss, osq, AX, ALU.add), "ss")
            e.wait_ge(s_ng, 16)
            g4 = gate.rearrange("p t (h d) -> p (t h) d", h=DN_H)
            c(V.tensor_tensor(g4, g4, bc(ngb, 1, NT * DN_H), ALU.mult))
            dno_ac.wait(e, "rt")
            c(V.reciprocal(sm[:, 128:144], sm[:, 128:144]))
            o16 = O.rearrange("p t h d -> p (t h) d")
            c(V.tensor_tensor(o16, o16, bc(sm[:, 128:144], 2, P), ALU.mult))
            dno_dv.mark(V.tensor_tensor(g4, o16, g4, ALU.mult), "y")
            return dno_dv

        def act_dno(e, c):
            dno_dv.wait(e, "ss")
            dno_ac.mark(nc.scalar.activation(sm[:, 128:144], sm[:, 128:144], ACT.Sqrt, bias=eps_col, scale=1.0 / P), "rt")
            return dno_ac

        def both(*progs):
            def run_both(e, c):
                for p in progs:
                    st = p(e, c)
                    e.wait_ge(st.sem, st.base + st.n)
                return st
            return run_both
        stage("dn_gate", pe=mod_mlp["pe"], dve=both(dve_dno, mod_mlp["dve"]), act=both(act_dno, mod_mlp["act"]))
        out_proj_stage("dn_out", gate, arena(16384, KC, T), first_wo, MOD[:, 2, :], arena(12800, CW),
                       pool=load_gain(io["norm_g1"]))

        first_q = ring_loads(io["peer_wq"], 4)
        norm_T_stage("norm_b", [(X[:, t, :], MOD[:, 4, :], MOD[:, 3, :]) for t in range(NT)], hT, 12288)
        NPH = 2 * PH
        QT = arena(0, NPH, T)
        keysT = arena(4096, NPH, NK)
        S = arena(6144, NT, NPH, NK)
        V1 = arena(10240, NT, NPH, TOPK)
        U1 = arena(10752, NT, NPH, TOPK)
        U1f = arena(11264, NT, NPH, TOPK)
        cand = arena(11776, PH, TOPK, TOPK)
        eqs = arena(13824, PH, TOPK, TOPK)
        TS = arena(15872, NT, PH, TOPK)
        pos = arena(16128, NT, PH, TOPK)
        part = arena(16384, 2, NT, PH, TOPK)
        partf = arena(16896, 2, NT, PH, TOPK)
        sel = arena(17408, 3, NT, PH * TOPK)
        s_pk = sem("s_pk")
        sq_names = [("q", n) for n in range(NPH)]
        ss_names = [("s", t, b) for t in range(NT) for b in range(4)]
        tr_names = [("tr", a) for a in range(3)]
        pq_pe = steps("pe", sq_names + ss_names + tr_names)
        pq_ac = steps("act", ["gt"] + sq_names + ss_names + ["exp"])
        pq_dv = steps("dve", ["max", "sel"] + tr_names)
        for s in range(4):
            free_at[first_q + s] = (pq_pe, ("q", 4 * s + 3))

        def pool_pq(e, c):
            e.dma_start(keysT, io["peer_kT"].rearrange("p (n k) -> p n k", n=NPH)).then_inc(s_pk, 16)
            e.wait_ge(s_pk, 16)

        def pe_pq(e, c):
            for n in range(NPH):
                ring_wait(e, first_q + n // 4)
                if n >= 4:
                    pq_ac.wait(e, ("q", n - 4))
                for k in range(KC):
                    ins = nc.tensor.matmul(PS[:, n % 4, 0:T], slot(first_q + n // 4)[:, k, (n % 4) * P:(n % 4 + 1) * P],
                                           hT[:, k, :], start=(k == 0), stop=(k == KC - 1))
                pq_pe.mark(ins, ("q", n))
            e.wait_ge(s_pk, 16)
            for i, (_, t, b) in enumerate(ss_names):
                pq_ac.wait(e, ("q", NPH - 1) if i < 4 else ss_names[i - 4])
                for n in range(4):
                    ins = nc.tensor.matmul(PS[:, 4 + i % 4, n * NK:(n + 1) * NK], QT[:, 4 * b + n, t * P:(t + 1) * P],
                                           keysT[:, 4 * b + n, :], start=True, stop=True)
                pq_pe.mark(ins, ss_names[i])
            pq_dv.wait(e, "sel")
            for a in range(3):
                for t in range(NT):
                    ins = nc.tensor.transpose(PS[:, a, t * P:(t + 1) * P], sel[:, a, t, :], ident)
                pq_pe.mark(ins, ("tr", a))
            return pq_pe

        def act_pq(e, c):
            pq_ac.mark(nc.scalar.copy(GT, MOD[:, 5, :]), "gt")
            for n in range(NPH):
                pq_pe.wait(e, ("q", n))
                pq_ac.mark(nc.scalar.copy(QT[:, n, :], PS[:, n % 4, 0:T]), ("q", n))
            for i, (_, t, b) in enumerate(ss_names):
                pq_pe.wait(e, ss_names[i])
                pq_ac.mark(nc.scalar.copy(S[:, t, 4 * b:4 * b + 4, :],
                                          PS[:, 4 + i % 4, :].rearrange("p (n k) -> p n k", n=4)), ss_names[i])
            pq_dv.wait(e, "max")
            pq_ac.mark(nc.scalar.activation(sel[:, 2], sel[:, 2], ACT.Exp), "exp")
            return pq_ac

        def dve_pq(e, c):
            V = nc.vector

            def top16(srcs, vals, ids):
                for lo in (0, 8):
                    for s, v in zip(srcs, vals):
                        ins = V.max(v[:, lo:lo + 8], s)
                    c(ins)
                    for s, v, u in zip(srcs, vals, ids):
                        ins = V.max_index(u[:, lo:lo + 8], v[:, lo:lo + 8], s)
                    c(ins)
                    if lo == 0:
                        for s, v in zip(srcs, vals):
                            ins = V.match_replace(s, v[:, 0:8], s, NEG)
                        c(ins)
            Uu = U1.bitcast(U32)
            for t in range(NT):
                pq_ac.wait(e, ("s", t, 3))
                top16([S[:, t, n, :] for n in range(NPH)], [V1[:, t, n, :] for n in range(NPH)],
                      [Uu[:, t, n, :] for n in range(NPH)])
            c(V.tensor_copy(U1f, Uu))
            posu, partu = pos.bitcast(U32), part.bitcast(U32)
            V1h = V1.rearrange("p t (h a) k -> p t h a k", a=2)
            U1h = U1f.rearrange("p t (h a) k -> p t h a k", a=2)
            for t in range(NT):
                c(V.tensor_tensor(cand, bc(V1h[:, t, :, 0, :], 3, TOPK), bc(V1h[:, t, :, 1, :], 2, TOPK), ALU.add))
                flat = cand.rearrange("p h a b -> p h (a b)")
                top16([flat[:, h, :] for h in range(PH)], [TS[:, t, h, :] for h in range(PH)],
                      [posu[:, t, h, :] for h in range(PH)])
            c(V.tensor_scalar(partu[:, 0], posu, 4, None, ALU.logical_shift_right))
            c(V.tensor_scalar(partu[:, 1], posu, TOPK - 1, None, ALU.bitwise_and))
            c(V.tensor_copy(partf, partu))
            g = sel[:, 2].rearrange("p t (h k) -> p t h k", h=PH)
            for t in range(NT):
                ins = V.tensor_tensor(g[:, t], TS[:, t], TS[:, t, :, 0:1].broadcast_to([P, PH, TOPK]), ALU.subtract)
            pq_dv.mark(ins, "max")
            for t in range(NT):
                for a in range(2):
                    c(V.tensor_tensor(eqs, bc(partf[:, a, t], 3, TOPK),
                                      iota[:, 0:TOPK].unsqueeze(1).unsqueeze(1).broadcast_to([P, PH, TOPK, TOPK]),
                                      ALU.is_equal))
                    c(V.tensor_tensor(eqs, eqs, bc(U1h[:, t, :, a, :], 2, TOPK), ALU.mult))
                    c(V.tensor_reduce(sel[:, a, t, :].rearrange("p (h k) -> p h k", h=PH), eqs, AX, ALU.add))
            pq_ac.wait(e, "exp")
            g16v = sel[:, 2].rearrange("p t (h k) -> p (t h) k", h=PH)
            c(V.tensor_reduce(sm[:, 144:160], g16v, AX, ALU.add))
            c(V.reciprocal(sm[:, 144:160], sm[:, 144:160]))
            pq_dv.mark(V.tensor_tensor(g16v, g16v, bc(sm[:, 144:160], 2, TOPK), ALU.mult), "sel")
            for a in range(3):
                pq_pe.wait(e, ("tr", a))
                pq_dv.mark(V.tensor_copy(idx[:, a, :], PS[:, a, 0:T]), ("tr", a))
            return pq_dv

        stage("peer_route", pool=pool_pq, pe=pe_pq, act=act_pq, dve=dve_pq)

        G = arena(0, NK, T)
        GQ = 4
        hotA = ring[:, 8192:8192 + 1024].rearrange("p (b q k) -> p b q k", b=2, q=GQ)
        hotB = ring[:, 9216:9216 + 1024].rearrange("p (b q k) -> p b q k", b=2, q=GQ)
        s_hot, s_gmm, s_gev = sem("s_hot"), sem("s_gmm"), sem("s_gev")
        NG2 = T // GQ // 2

        def groups_loop(e, body):
            for b in range(2):
                body(b, b, True)
            with e.Fori(1, NG2) as i:
                for b in range(2):
                    body(i * 2 + b, b, False)

        def dve_g(e, c):
            def body(n, b, first):
                if not first:
                    e.wait_ge(s_gmm, n - 1)
                nc.vector.tensor_tensor(hotA[:, b], bc(iota, 1, GQ), bc(idx[:, 0, bass.ds(n * GQ, GQ)], 2, P),
                                        ALU.is_equal)
                for q in range(GQ):
                    t = n * GQ + q
                    ins = nc.vector.tensor_scalar(hotB[:, b, q, :], iota, idx[:, 1, bass.ds(t, 1)],
                                                  idx[:, 2, bass.ds(t, 1)], ALU.is_equal, ALU.mult)
                ins.then_inc(s_hot, 1)
            groups_loop(e, body)
            e.wait_ge(s_hot, 2 * NG2)

        def pe_g(e, c):
            def body(n, b, first):
                e.wait_ge(s_hot, n + 1)
                if not first:
                    e.wait_ge(s_gev, n - 1)
                for q in range(GQ):
                    ins = nc.tensor.matmul(PS[:, b, q * NK:(q + 1) * NK], hotA[:, b, q, :], hotB[:, b, q, :],
                                           start=True, stop=True)
                ins.then_inc(s_gmm, 1)
            groups_loop(e, body)
            e.wait_ge(s_gmm, 2 * NG2)

        def act_g(e, c):
            def body(n, b, first):
                e.wait_ge(s_gmm, n + 1)
                nc.scalar.copy(G[:, :, bass.ds(n * GQ, GQ)].rearrange("p j q -> p q j"),
                               PS[:, b, :].rearrange("p (q j) -> p q j", q=GQ)).then_inc(s_gev, 1)
            groups_loop(e, body)
            e.wait_ge(s_gev, 2 * NG2)

        stage("peer_weights", dve=dve_g, pe=pe_g, act=act_g)

        NPART = 2 * NK
        PW = KC * P
        PRAW = [ring[:, q * PW:(q + 1) * PW] for q in range(4)]
        PSPL = [r32(4 * PW + q * 2 * PW, 2, PW) for q in range(4)]
        xs_hi, xs_hi32 = r32(X_at, KC, T)
        xs_lo, _ = r32(hT_at, KC, T)
        act_h = ring[:, spare_at:spare_at + 2 * T].rearrange("p (b t) -> p b t", b=2)
        coef, coef32 = r32(spare_at + 2 * T, 2, 2, T)
        x_home = nc.dram_tensor("x_home", (P, NT * D), F32).ap()
        p_ld = [sem(f"p_ld{q}") for q in range(4)]
        s_px, s_hi, s_lo, s_use = sem("p_x"), sem("p_hi"), sem("p_lo"), sem("p_use")
        s_gelu, s_coef, s_chi, s_xhi, s_xlo = sem("p_gelu"), sem("p_coef"), sem("p_chi"), sem("p_xhi"), sem("p_xlo")
        s_cs = sem("p_cs")
        PEEL = 3

        def pairs(e, body):
            for m in range(PEEL):
                body(m, 2 * m + 1, m)
            with e.Fori(0, (NK - 1 - PEEL) // 4) as i:
                for q in range(4):
                    body(i * 4 + (PEEL + q), i * 8 + (2 * (PEEL + q) + 1), 4 + PEEL + q)

        def load_peer(sp):
            for n in range(first_q + 1, first_q + 4):
                free_at[n][0].wait(sp, free_at[n][1])

            def part(src, n, s, turn):
                if s >= 4:
                    sp.wait_ge(s_lo, n - 3)
                sp.dma_start(PRAW[s % 4], src).then_inc(p_ld[s % 4], 16)
            part(io["peer_u"][0], 0, 0, 0)

            def body(m, n, mm):
                s = 2 * mm + 1
                part(io["peer_u"][m + 1], n, s, 0)
                part(io["peer_v"][:, m, :], n + 1, s + 1, 0)
            pairs(sp, body)
            part(io["peer_v"][:, NK - 1, :], NPART - 1, NPART - 1, 0)
        stream.append(load_peer)

        def ld_wait(e, n, s):
            if isinstance(n, int):
                e.wait_ge(p_ld[n % 4], 16 * (n // 4 + 1))
            else:
                e.wait_ge(p_ld[s % 4], n * 4 + (16 - 4 * (s % 4)))

        def pool_x(e, c):
            e.dma_start(x_home, X.rearrange("p t d -> p (t d)")).then_inc(s_px, 16)
            e.wait_ge(s_px, 16)

        def act_x(e, c):
            def hi(n, s):
                ld_wait(e, n, s)
                if s >= 4:
                    e.wait_ge(s_use, n - 3)
                nc.scalar.copy(PSPL[s % 4][0][:, 0, :], PRAW[s % 4]).then_inc(s_hi, 1)

            def gelu(m, mm):
                e.wait_ge(s_use, 1 if mm == 0 else m * 2)
                if mm >= 2:
                    e.wait_ge(s_coef, m - 1)
                nc.scalar.activation(act_h[:, mm % 2, :], PS[:, mm % 2, 0:T], ACT.Gelu).then_inc(s_gelu, 1)
            e.wait_ge(s_px, 16)
            nc.scalar.copy(xs_hi, hT).then_inc(s_xhi, 1)
            hi(0, 0)

            def body(m, n, mm):
                s = 2 * mm + 1
                hi(n, s)
                hi(n + 1, s + 1)
                gelu(m, mm)
            pairs(e, body)
            hi(NPART - 1, NPART - 1)
            gelu(NK - 1, NK - 1)
            e.wait_ge(s_gelu, NK)

        def dve_x(e, c):
            V = nc.vector

            def lo(n, s):
                e.wait_ge(s_hi, n + 1)
                V.tensor_tensor(PSPL[s % 4][0][:, 1, :], PRAW[s % 4], PSPL[s % 4][1][:, 0, :],
                                ALU.subtract).then_inc(s_lo, 1)

            def coefs(m, mm):
                b = mm % 2
                e.wait_ge(s_gelu, m + 1)
                V.tensor_tensor(act_h[:, b, :], act_h[:, b, :], G[:, bass.ds(m, 1), :].rearrange("p a t -> p (a t)"),
                                ALU.mult).then_inc(s_cs, 1)
                e.wait_ge(s_cs, m + 1)
                if mm >= 2:
                    e.wait_ge(s_use, m * 2 - 1)
                V.tensor_copy(coef[:, b, 0, :], act_h[:, b, :]).then_inc(s_chi, 1)
                e.wait_ge(s_chi, m + 1)
                V.tensor_tensor(coef[:, b, 1, :], act_h[:, b, :], coef32[:, b, 0, :], ALU.subtract).then_inc(s_coef, 1)
            e.wait_ge(s_xhi, 1)
            V.tensor_tensor(xs_lo, hT, xs_hi32, ALU.subtract).then_inc(s_xlo, 1)
            lo(0, 0)

            def body(m, n, mm):
                s = 2 * mm + 1
                lo(n, s)
                lo(n + 1, s + 1)
                coefs(m, mm)
            pairs(e, body)
            lo(NPART - 1, NPART - 1)
            coefs(NK - 1, NK - 1)
            e.wait_ge(s_coef, NK)

        def pe_x(e, c):
            def hid(j, n, s, jj):
                e.wait_ge(s_lo, n + 1)
                if jj >= 2:
                    e.wait_ge(s_gelu, j - 1)
                w = PSPL[s % 4][0].rearrange("p h (k e) -> p h k e", k=KC)
                for k in range(KC):
                    ins = exact3(PS[:, jj % 2, 0:T], (w[:, 0, k, :], w[:, 1, k, :]), (xs_hi[:, k, :], xs_lo[:, k, :]),
                                 k == 0, k == KC - 1)
                ins.then_inc(s_use, 1)

            def y(m, n, s, mm, start=False, stop=False):
                e.wait_ge(s_lo, n + 1)
                e.wait_ge(s_coef, m + 1)
                v, cf = PSPL[s % 4][0], coef[:, mm % 2]
                for t in range(NT):
                    for h in range(2):
                        cols, tk = slice(h * CW, (h + 1) * CW), slice(t * P, (t + 1) * P)
                        ins = exact3(PS[:, 4 + 2 * t + h, :], (cf[:, 0, tk], cf[:, 1, tk]), (v[:, 0, cols], v[:, 1, cols]),
                                     start, stop)
                ins.then_inc(s_use, 1)
            e.wait_ge(s_xlo, 1)
            hid(0, 0, 0, 0)

            def body(m, n, mm):
                hid(m + 1, n, 2 * mm + 1, mm + 1)
                y(m, n + 1, 2 * mm + 2, mm, start=mm == 0)
            pairs(e, body)
            y(NK - 1, NPART - 1, NPART - 1, NK - 1, stop=True)
            e.wait_ge(s_use, NPART)

        stage("peer_experts", pool=pool_x, pe=pe_x, act=act_x, dve=dve_x)

        def pool_back(e, c):
            e.dma_start(X.rearrange("p t d -> p (t d)"), x_home).then_inc(s_px, 16)
            e.wait_ge(s_px, 32)
        stage("x_back", pool=pool_back)

        def add_norm_stage(tag, gain, g_dram, off):
            tmp, gb, sq2 = arena(off, 2, CW), arena(off + D, D), arena(off + 2 * D, D)
            s_in = sem(f"{tag}_in")
            dv_s = steps("dve", [("add", t) for t in range(NT)] +
                         ([("n", t) for t in range(NT)] if g_dram is not None else []))
            ac_s = steps("act", [x for t in range(NT) for x in (("ss", t), ("rt", t))] if g_dram is not None else [])

            def dve(e, c):
                for t in range(NT):
                    for h in range(2):
                        cols = slice(h * CW, (h + 1) * CW)
                        c(nc.vector.tensor_tensor(tmp[:, h, :], PS[:, 4 + 2 * t + h, :], gain[:, cols], ALU.mult))
                        ins = nc.vector.tensor_tensor(X[:, t, cols], X[:, t, cols], tmp[:, h, :], ALU.add)
                        if h == 0:
                            c(ins)
                    dv_s.mark(ins, ("add", t))
                if g_dram is None:
                    return dv_s
                e.wait_ge(s_in, 16)
                for t in range(NT):
                    ac_s.wait(e, ("rt", t))
                    c(nc.vector.reciprocal(sm[:, 16 + t:17 + t], sm[:, 8 + t:9 + t]))
                    dv_s.mark(nc.vector.scalar_tensor_tensor(X[:, t, :], X[:, t, :], sm[:, 16 + t:17 + t], gb,
                                                             ALU.mult, ALU.mult), ("n", t))
                return dv_s

            def act(e, c):
                for t in range(NT):
                    dv_s.wait(e, ("add", t))
                    if t:
                        ac_s.wait(e, ("ss", t - 1))
                    ac_s.mark(nc.scalar.activation(sq2, X[:, t, :], ACT.Square, accum_out=sm[:, t:t + 1]), ("ss", t))
                    ac_s.wait(e, ("ss", t))
                    ac_s.mark(nc.scalar.activation(sm[:, 8 + t:9 + t], sm[:, t:t + 1], ACT.Sqrt, bias=eps_col,
                                                   scale=1.0 / D), ("rt", t))
                return ac_s

            def pool(e, c):
                e.dma_start(gb, g_dram.unsqueeze(0).broadcast_to([P, D])).then_inc(s_in, 16)
                e.wait_ge(s_in, 16)
            if g_dram is None:
                stage(tag, dve=dve)
            else:
                stage(tag, dve=dve, act=act, pool=pool)

        add_norm_stage("peer_out", GT, io["final_g"], 0)

        NSEG = 3
        SEG = ((0, 0), (0, 1), (1, 1))

        for layer in range(LAYERS):
            L = f"l{layer}_"
            release_ring("peer_experts" if layer == 0 else "l0_experts")
            s_wdt = sem(L + "wdt")

            def pool_ada(e, c, layer=layer, s_wdt=s_wdt, gain=load_gain(io[f"ng_mix{layer}"])):
                e.dma_start(ring[:, spare_at:spare_at + 64], io[f"w_dt{layer}"]).then_inc(s_wdt, 16)
                gain(e, c)
                e.wait_ge(s_wdt, 16)
            stage(L + "ada", pool=pool_ada, **mod_sum(8 + 12 * layer, list(range(12))))
            first_in = ring_loads(io[f"w_in{layer}"], 8)
            norm_T_stage(L + "norm_mix", [(X[:, t, :], MOD[:, 1, :], MOD[:, 0, :]) for t in range(NT)],
                         hT, 12288)

            mcn = ("lev_mask", "lev_sum", "cos", "sin", "ret_decay", "inc_f")
            mc_at, off = {}, 0
            for n in mcn:
                mc_at[n] = off
                off += CAT[n][1]
            lev_mask = arena(mc_at["lev_mask"], LEVELS + 1, P)
            lev_sum = arena(mc_at["lev_sum"], LEVELS + 2, P)
            cos, sin = arena(mc_at["cos"], T), arena(mc_at["sin"], T)
            ret_decay = arena(mc_at["ret_decay"], RE_H, NSEG, P)
            inc = arena(mc_at["inc_f"], P)
            XBCp, XBC = arena(4352, 6, TAPS2 - 1 + T), arena(5920, 6, T)
            hqT, kinT = arena(7456, 2, T), arena(7968, 2, T)
            RT, rot = arena(8480, 8, T), arena(10528, 4, T)
            zrow, logf, hi = arena(11552, NT, 512), arena(12576, NT, T), arena(13088, NT, T)
            hg, rv, rg = arena(13600, NT, T), arena(14112, NT, T), arena(14624, NT, T)
            dtr, g8, Gc8 = arena(15136, NT, 8), arena(15152, NT, 8), arena(15168, NT, 8)
            spar, sscr = arena(15200, 3, 8), arena(15224, 3, NT, 8)
            ngs, lb, oml, ngh = arena(15400, 512), arena(15912, T + 2), arena(16170, T + 2), arena(16432, T)
            cw2, wdt = arena(16690, 6, TAPS2 + 1), ring[:, spare_at:spare_at + 64].rearrange("p (k n) -> p k n", k=KC)
            xs, xdt = arena(16820, NT, 512), arena(17844, NT, 512)
            WS = arena(18868, SSD_H, NSEG, P)
            EX = arena(21940, 4, LEVELS + 1, P)
            Rg = arena(21940, SSD_H, NSEG, P)
            mtmp = arena(26036, HG_H, P)
            WH, WR = arena(8480, HG_H, NSEG, P), arena(4352, RE_H, NSEG, P)
            lbr = ring[:, spare_at + 64:spare_at + 64 + 2 * (T + 2)].rearrange("p (a b) -> p a b", a=2)
            lbs2 = ring[:, spare_at + 640:spare_at + 640 + T + 2]
            MIX = hT.rearrange("p k t -> p (k t)").rearrange("p (t d) -> p t d", t=NT)

            def proj(L=L, layer=layer, first_in=first_in):
                s_in = sem(L + "proj_in")
                pairs = [("T", i) for i in range(9)]
                rows = [("r", j, t) for j in range(4) for t in range(NT)]
                slots_mm = [pairs[2 * s:2 * s + 2] for s in range(4)] + [[pairs[8]] + rows[0:2]] + \
                           [rows[2 * s:2 * s + 2] for s in range(1, 4)]
                pe_s = steps("pe", ["dt"] + sum(slots_mm, []))
                lo_s = Steps(sem(L + "wlo"), [(s, q) for s in range(8) for q in range(4)])
                s_whi, s_wuse, s_xhi, s_xlo = (sem(L + n) for n in ("whi", "wuse", "phi", "plo"))
                whi_at = [RB + 20928, RB + 22976, RB + 25024]
                wlo_at = [RB + 21952, RB + 24000, GT_at]
                whi, wlo = [r32(w, 2, CW) for w in whi_at], [r32(w, 2, CW)[0] for w in wlo_at]
                xhi, xhi32 = r32(RB + 18880, KC, T)
                xlo, _ = r32(hT_at, KC, T)
                ac_s = steps("act", sum(slots_mm[:2], []) + ["lbe", "alog"] + sum(slots_mm[2:], []) + ["conv", "dte", "ln", "logf"])
                dv_s = steps("dve", ["dt", "lb0", "lb", "conv", "dt0", "dt1", "logf0", "done"])
                for s in range(8):
                    free_at[first_in + s] = (lo_s, (s, 3))

                def raw(u):
                    return slot(first_in + u // 4)[:, 2 * (u % 4):2 * (u % 4) + 2, :]

                def split_hi(e, u):
                    ring_wait(e, first_in + u // 4)
                    if u >= 3 and (u - 3) % 4 == 3:
                        pe_s.wait(e, slots_mm[(u - 3) // 4][-1])
                    elif u >= 3:
                        e.wait_ge(s_wuse, (u - 3) // 4 * 3 + (u - 3) % 4 + 1)
                    nc.scalar.copy(whi[u % 3][0], raw(u)).then_inc(s_whi, 1)

                def split_lo(e, u):
                    e.wait_ge(s_whi, u + 1)
                    lo_s.mark(nc.gpsimd.tensor_tensor(wlo[u % 3], raw(u), whi[u % 3][1], ALU.subtract),
                              (u // 4, u % 4))

                def loads(e):
                    n = 0

                    def load(dst, src):
                        e.dma_start(dst, src).then_inc(s_in, 16)
                        return 1

                    def row(a, k):
                        return a.unsqueeze(0).broadcast_to([P, k])
                    n += load(lbr[:, :, 0:T], io["lbs"].unsqueeze(0).broadcast_to([P, 2, T]))
                    n += load(lbr[:, :, T:T + 2], io["lbsT"].rearrange("p (a b) -> p a b", a=2))
                    n += load(cw2, io[f"conv{layer}"].rearrange("p (a b) -> p a b", a=6))
                    n += load(spar.rearrange("p a b -> p (a b)"), row(io[f"ssd{layer}"], 24))
                    n += load(ngs, row(io[f"ng_ssd{layer}"], 512))
                    n += load(ngh, row(io[f"ng_hgrn{layer}"], T))
                    for m in mcn:
                        n += load(arena(mc_at[m], CAT[m][1]), io["const"][:, CAT[m][0]:CAT[m][0] + CAT[m][1]])
                    assert n == 12

                def pool(e, c):
                    for u in range(32):
                        split_lo(e, u)
                    return lo_s

                def pe(e, c):
                    for t in range(NT):
                        for k in range(KC):
                            ins = nc.tensor.matmul(PS[:, 7, t * 8:t * 8 + 8], hT[:, k, t * P:(t + 1) * P], wdt[:, k, :],
                                                   start=(k == 0), stop=(k == KC - 1))
                    pe_s.mark(ins, "dt")
                    e.wait_ge(s_xlo, 1)
                    for s, groups in enumerate(slots_mm):
                        if s == 1:
                            dv_s.wait(e, "dt")
                        if s >= 2:
                            ac_s.wait(e, slots_mm[s - 2][-1])
                        for q in range(4):
                            lo_s.wait(e, (s, q))
                            w = whi[(4 * s + q) % 3][0], wlo[(4 * s + q) % 3]
                            for k2 in range(2):
                                k = 2 * q + k2
                                for g in groups:
                                    if g[0] == "T":
                                        for a in range(2):
                                            cs = slice((2 * g[1] + a) % 4 * P, ((2 * g[1] + a) % 4 + 1) * P)
                                            ins = exact3(PS[:, bank(s, g) + a, 0:T],
                                                         (w[0][:, k2, cs], w[1][:, k2, cs]), (xhi[:, k, :], xlo[:, k, :]),
                                                         k == 0, k == KC - 1)
                                    else:
                                        _, j, t = g
                                        cs, tk = slice(T if j == 0 else 0, CW), slice(t * P, (t + 1) * P)
                                        ins = exact3(PS[:, bank(s, g), cs], (xhi[:, k, tk], xlo[:, k, tk]),
                                                     (w[0][:, k2, cs], w[1][:, k2, cs]), k == 0, k == KC - 1)
                                    if k == KC - 1:
                                        pe_s.mark(ins, g)
                            if q < 3:
                                ins.then_inc(s_wuse, 1)
                    return pe_s

                def bank(s, g):
                    return 4 * (s % 2) + (2 * (g[1] % 2) if g[0] == "T" else g[2] + (2 if s == 4 else 0))

                def out_of_psum(e, s, g):
                    A = nc.scalar
                    pe_s.wait(e, g)
                    if g[0] == "T":
                        i = g[1]
                        src = PS[:, bank(s, g):bank(s, g) + 2, 0:T]
                        if i < 3:
                            ins = A.copy(XBCp[:, 2 * i:2 * i + 2, TAPS2 - 1:], src)
                        elif i == 3:
                            ins = A.copy(hqT, src)
                        elif i == 4:
                            ins = A.activation(kinT, src, ACT.Sigmoid)
                        else:
                            ins = A.copy(RT[:, 2 * i - 10:2 * i - 8, :], src)
                    else:
                        _, j, t = g
                        b = PS[:, bank(s, g), :]
                        if j == 0:
                            ins = A.activation(logf[:, t, :], b[:, T:CW], ACT.Sigmoid)
                        elif j == 1:
                            ins = A.activation(zrow[:, t, :], b, ACT.Silu)
                        elif j == 2:
                            A.copy(hi[:, t, :], b[:, 0:T])
                            ins = A.activation(hg[:, t, :], b[:, T:CW], ACT.Sigmoid)
                        else:
                            A.copy(rv[:, t, :], b[:, 0:T])
                            ins = A.activation(rg[:, t, :], b[:, T:CW], ACT.Silu)
                    ac_s.mark(ins, g)

                def act(e, c):
                    A = nc.scalar
                    A.copy(xhi, hT).then_inc(s_xhi, 1)
                    loads(e)
                    for s in range(9):
                        for q in range(4 if s < 8 else 0):
                            split_hi(e, 4 * s + q)
                        for g in slots_mm[s - 1] if s else []:
                            out_of_psum(e, s - 1, g)
                        if s == 2:
                            dv_s.wait(e, "lb0")
                            ac_s.mark(A.activation(lbr, lbr, ACT.Exp), "lbe")
                            ac_s.mark(A.activation(spar[:, 1], spar[:, 1], ACT.Exp), "alog")
                    dv_s.wait(e, "conv")
                    ac_s.mark(A.activation(XBC, XBC, ACT.Silu), "conv")
                    dv_s.wait(e, "dt0")
                    ac_s.mark(A.activation(sscr[:, 1], sscr[:, 1], ACT.Exp), "dte")
                    dv_s.wait(e, "dt1")
                    ac_s.mark(A.activation(sscr[:, 1], sscr[:, 1], ACT.Ln), "ln")
                    dv_s.wait(e, "logf0")
                    ac_s.mark(A.activation(logf, logf, ACT.Ln), "logf")
                    return ac_s

                def dve(e, c):
                    V = nc.vector
                    e.wait_ge(s_xhi, 1)
                    pe_s.wait(e, "dt")
                    V.tensor_tensor(xlo, hT, xhi32, ALU.subtract).then_inc(s_xlo, 1)
                    dv_s.mark(V.tensor_copy(sscr[:, 0], PS[:, 7, 0:16].rearrange("p (t h) -> p t h", t=NT)), "dt")
                    c(V.memset(XBCp[:, :, 0:TAPS2 - 1], 0.0))
                    e.wait_ge(s_in, 16 * 12)
                    c(V.tensor_tensor(lbs2, lbr[:, 0], lbr[:, 1], ALU.max))
                    dv_s.mark(V.tensor_tensor(lbr, lbr, bc(lbs2, 1, 2), ALU.subtract), "lb0")
                    ac_s.wait(e, "lbe")
                    c(V.tensor_tensor(lbs2, lbr[:, 0], lbr[:, 1], ALU.add))
                    c(V.reciprocal(lbs2, lbs2))
                    c(V.tensor_tensor(lbr, lbr, bc(lbs2, 1, 2), ALU.mult))
                    if layer == 0:
                        c(V.tensor_tensor(lb, lbr[:, 0], lbr[:, 0], ALU.subtract))
                    else:
                        c(V.tensor_tensor(lb, lbr[:, 0], lbr[:, 1], ALU.add))
                        c(V.tensor_tensor(lb, lb, lbr[:, 0], ALU.subtract))
                    dv_s.mark(V.tensor_scalar(oml, lb, -1.0, 1.0, ALU.mult, ALU.add), "lb")
                    dv_s.wait(e, "lb")
                    ac_s.wait(e, ("T", 2))
                    for n in range(6):
                        for j in range(TAPS2):
                            if j == 0:
                                ins = V.tensor_scalar(XBC[:, n, :], XBCp[:, n, 0:T], cw2[:, n, 0:1],
                                                      cw2[:, n, TAPS2:TAPS2 + 1], ALU.mult, ALU.add)
                            else:
                                ins = V.scalar_tensor_tensor(XBC[:, n, :], XBCp[:, n, j:j + T], cw2[:, n, j:j + 1],
                                                             XBC[:, n, :], ALU.mult, ALU.add)
                            if (n, j) == (5, TAPS2 - 1):
                                dv_s.mark(ins, "conv")
                            else:
                                c(ins)
                    ac_s.wait(e, ("T", 4))
                    for a in range(2):
                        c(V.tensor_scalar(kinT[:, a, :], kinT[:, a, :], oml[:, T + a:T + a + 1], lb[:, T + a:T + a + 1],
                                          ALU.mult, ALU.add))
                    c(V.tensor_scalar(kinT, kinT, -1.0, 1.0, ALU.mult, ALU.add))
                    ac_s.wait(e, ("T", 8))
                    c(V.tensor_tensor(rot, RT[:, 0:4, :], bc(cos, 1, 4), ALU.mult))
                    c(V.tensor_tensor(RT[:, 4:8, :], RT[:, 4:8, :], bc(sin, 1, 4), ALU.mult))
                    c(V.tensor_tensor(rot, rot, RT[:, 4:8, :], ALU.add))
                    c(V.tensor_scalar(rot[:, 2:4, :], rot[:, 2:4, :], float(HD) ** -0.5, None, ALU.mult))
                    c(V.tensor_tensor(sscr[:, 0], sscr[:, 0], bc(spar[:, 0], 1, NT), ALU.add))
                    c(V.tensor_scalar(sscr[:, 2], sscr[:, 0], -1.0, None, ALU.mult))
                    dv_s.mark(V.tensor_tensor(sscr[:, 1], sscr[:, 0], sscr[:, 2], ALU.min), "dt0")
                    ac_s.wait(e, "dte")
                    dv_s.mark(V.tensor_scalar_add(sscr[:, 1], sscr[:, 1], 1.0), "dt1")
                    ac_s.wait(e, ("r", 0, NT - 1))
                    c(V.tensor_tensor(logf, logf, bc(oml[:, 0:T], 1, NT), ALU.mult))
                    c(V.tensor_tensor(logf, logf, bc(lb[:, 0:T], 1, NT), ALU.add))
                    dv_s.mark(V.tensor_scalar_max(logf, logf, GATE_FLOOR), "logf0")
                    ac_s.wait(e, "ln")
                    c(V.scalar_tensor_tensor(dtr, sscr[:, 0], 0.0, sscr[:, 1], ALU.max, ALU.add))
                    c(V.tensor_scalar(spar[:, 1], spar[:, 1], -1.0, None, ALU.mult))
                    dv_s.mark(V.tensor_tensor(g8, dtr, bc(spar[:, 1], 1, NT), ALU.mult), "done")
                    return dv_s

                stage(L + "proj", pool=pool, pe=pe, act=act, dve=dve)
            proj()

            def value_products(W, val, bank, heads, width):
                for h in range(heads):
                    cols = slice(h * HD, (h + 1) * HD)
                    nc.tensor.matmul(PS[:, bank, cols], W[:, h, 0, :], val[:, 0, cols], start=True, stop=True)
                    nc.tensor.matmul(PS[:, bank + 1, cols], W[:, h, 1, :], val[:, 0, cols], start=True, stop=False)
                    ins = nc.tensor.matmul(PS[:, bank + 1, cols], W[:, h, 2, :], val[:, 1, cols], start=False, stop=True)
                return ins

            def score_products(bank, k, q):
                nc.tensor.matmul(PS[:, bank, 0:T], k[:, 0:P], q, start=True, stop=True)
                return nc.tensor.matmul(PS[:, bank, T:TRI], k[:, P:T], q[:, P:T], start=True, stop=True)

            def ssd(L=L):
                pe_s = steps("pe", ["xs", "Gc", "CB", "Gr", "o"])
                dv_s = steps("dve", ["xs", "R", "E", "W", "o"])
                ac_s = steps("act", ["exp"])
                GRB = (0, 1, 5, 6)

                def pe(e, c):
                    for t in range(NT):
                        for n in range(4):
                            ins = nc.tensor.transpose(PS[:, t, n * P:(n + 1) * P], XBC[:, n, t * P:(t + 1) * P], ident)
                    pe_s.mark(ins, "xs")
                    nc.tensor.matmul(PS[:, 2, 0:8], inc, g8[:, 0, :], start=True, stop=True)
                    nc.tensor.matmul(PS[:, 2, 8:16], ones, g8[:, 0, :], start=True, stop=False)
                    pe_s.mark(nc.tensor.matmul(PS[:, 2, 8:16], inc, g8[:, 1, :], start=False, stop=True), "Gc")
                    for g in range(2):
                        rows = slice(g * HD, (g + 1) * HD)
                        ins = score_products(3 + g, XBC[rows, 4, :], XBC[rows, 5, :])
                    pe_s.mark(ins, "CB")
                    dv_s.wait(e, "xs")
                    dv_s.wait(e, "R")
                    for h in range(SSD_H):
                        o = PS[:, GRB[h // 2], (h % 2) * T:(h % 2) * T + T]
                        nc.tensor.matmul(o[:, 0:P], ones, Rg[:, h, 0, :], start=True, stop=True)
                        nc.tensor.matmul(o[:, P:T], ones, Rg[:, h, 1, :], start=True, stop=False)
                        ins = nc.tensor.matmul(o[:, P:T], ones, Rg[:, h, 2, :], start=False, stop=True)
                    pe_s.mark(ins, "Gr")
                    dv_s.wait(e, "W")
                    pe_s.mark(value_products(WS, xdt, 0, SSD_H, 512), "o")
                    return pe_s

                def act(e, c):
                    dv_s.wait(e, "E")
                    ac_s.mark(nc.scalar.activation(WS, WS, ACT.Exp), "exp")
                    return ac_s

                def dve(e, c):
                    V = nc.vector
                    c(V.tensor_tensor(Rg[:, :, 0, :], bc(inc, 1, SSD_H), bc(g8[:, 0, :], 2, P), ALU.mult))
                    c(V.tensor_copy(Rg[:, :, 1, :], bc(g8[:, 0, :], 2, P)))
                    c(V.tensor_tensor(Rg[:, :, 2, :], bc(inc, 1, SSD_H), bc(g8[:, 1, :], 2, P), ALU.mult))
                    pe_s.wait(e, "xs")
                    for t in range(NT):
                        ins = V.tensor_copy(xs[:, t, :], PS[:, t, :])
                    dv_s.mark(ins, "xs")
                    dv_s.wait(e, "xs")
                    for t in range(NT):
                        c(V.tensor_tensor(xdt[:, t, :].rearrange("p (h d) -> p h d", h=SSD_H),
                                          xs[:, t, :].rearrange("p (h d) -> p h d", h=SSD_H),
                                          bc(dtr[:, t, :], 2, HD), ALU.mult))
                    pe_s.wait(e, "Gc")
                    dv_s.mark(V.tensor_copy(Gc8, PS[:, 2, 0:16].rearrange("p (t h) -> p t h", t=NT)), "R")
                    dv_s.wait(e, "R")
                    pe_s.wait(e, "Gr")
                    for h in range(SSD_H):
                        o = PS[:, GRB[h // 2], (h % 2) * T:(h % 2) * T + T]
                        V.tensor_scalar(WS[:, h, 0:2, :].rearrange("p a t -> p (a t)"), o, Gc8[:, 0, h:h + 1], 0.0,
                                        ALU.subtract, ALU.min)
                        ins = V.tensor_scalar(WS[:, h, 2, :], o[:, P:T], Gc8[:, 1, h:h + 1], 0.0, ALU.subtract, ALU.min)
                    dv_s.mark(ins, "E")
                    ac_s.wait(e, "exp")
                    for s in (0, 2):
                        c(V.tensor_tensor(WS[:, :, s, :], WS[:, :, s, :], bc(inc, 1, SSD_H), ALU.mult))
                    pe_s.wait(e, "CB")
                    for g in range(2):
                        w = WS[:, 4 * g:4 * g + 4].rearrange("p h a t -> p h (a t)")
                        ins = V.tensor_tensor(w, w, bc(PS[:, 3 + g, 0:TRI], 1, 4), ALU.mult)
                    dv_s.mark(ins, "W")
                    for t in range(NT):
                        m = MIX[:, t, 0:512].rearrange("p (h d) -> p h d", h=SSD_H)
                        c(V.tensor_tensor(m, xs[:, t, :].rearrange("p (h d) -> p h d", h=SSD_H), bc(spar[:, 2], 2, HD),
                                          ALU.mult))
                    pe_s.wait(e, "o")
                    for t in range(NT):
                        c(V.tensor_tensor(MIX[:, t, 0:512], MIX[:, t, 0:512], PS[:, t, :], ALU.add))
                        ins = V.tensor_tensor(MIX[:, t, 0:512], MIX[:, t, 0:512], zrow[:, t, :], ALU.mult)
                        if t == 0:
                            c(ins)
                    dv_s.mark(ins, "o")
                    return dv_s
                stage(L + "ssd", pe=pe, act=act, dve=dve)
            ssd()

            def ret(L=L):
                pe_s = steps("pe", ["qk", "o"])
                dv_s = steps("dve", ["W", "o"])

                def pe(e, c):
                    for h in range(RE_H):
                        rows = slice((h % 2) * HD, (h % 2) * HD + HD)
                        ins = score_products(h, rot[rows, 2 + h // 2, :], rot[rows, h // 2, :])
                    pe_s.mark(ins, "qk")
                    dv_s.wait(e, "W")
                    pe_s.mark(value_products(WR, rv, 4, RE_H, T), "o")
                    return pe_s

                def dve(e, c):
                    pe_s.wait(e, "qk")
                    for h in range(RE_H):
                        ins = nc.vector.tensor_tensor(WR[:, h].rearrange("p a t -> p (a t)"), PS[:, h, 0:TRI],
                                                      ret_decay[:, h].rearrange("p a t -> p (a t)"), ALU.mult)
                    dv_s.mark(ins, "W")
                    pe_s.wait(e, "o")
                    for t in range(NT):
                        ins = nc.vector.tensor_copy(MIX[:, t, 768:1024], PS[:, 4 + t, 0:T])
                    dv_s.mark(ins, "o")
                    return dv_s
                stage(L + "ret", pe=pe, dve=dve)
            ret()

            def hgrn(L=L):
                sums = [("sum", a, b) for a in range(4) for b in range(2)]
                scs = [("sc", t, m) for t in range(NT) for m in range(LEVELS + 1)] + [("sc", 2, 0)]
                pe_s = steps("pe", sums + scs + ["o"])
                ac_s = steps("act", sums)
                dv_s = steps("dve", ["qk"] + scs + ["o"])

                def pe(e, c):
                    for _, a, b in sums:
                        hp, t = a // 2, a % 2
                        lf = logf[:, t, hp * P:(hp + 1) * P]
                        bank = PS[:, 2 * a + b, :]
                        if b == 0:
                            ins = nc.tensor.matmul(bank, lf, lev_sum[:, 0:4, :], start=True, stop=True)
                        else:
                            nc.tensor.matmul(bank[:, 0:3 * P], lf, lev_sum[:, 4:7, :], start=True, stop=True)
                            ins = nc.tensor.matmul(bank[:, 3 * P:], lf, lev_sum[:, 7 + t, :], start=True, stop=True)
                        pe_s.mark(ins, ("sum", a, b))
                    dv_s.wait(e, "qk")
                    for i, (_, t, m) in enumerate(scs):
                        if i >= 4:
                            dv_s.wait(e, scs[i - 4])
                        for h in range(HG_H):
                            rows, hp = slice((h % 2) * HD, (h % 2) * HD + HD), h // 2
                            tk = slice(t * P, (t + 1) * P)
                            if t == 2:
                                a, b = EX[rows, 2 * hp, LEVELS, :], EX[rows, 2 * hp + 1, LEVELS, :]
                            elif m == 0:
                                a, b = kinT[rows, hp, tk], hqT[rows, hp, tk]
                            else:
                                a = b = EX[rows, 2 * hp + t, m - 1, :]
                            ins = nc.tensor.matmul(PS[:, 2 * (i % 4) + h % 2, hp * P:(hp + 1) * P], a, b,
                                                   start=True, stop=True)
                        pe_s.mark(ins, scs[i])
                    dv_s.wait(e, scs[-1])
                    pe_s.mark(value_products(WH, hi, 2, HG_H, T), "o")
                    return pe_s

                def act(e, c):
                    for _, a, b in sums:
                        pe_s.wait(e, ("sum", a, b))
                        ac_s.mark(nc.scalar.activation(EX[:, a, 4 * b:4 * b + 4, :],
                                                       PS[:, 2 * a + b, :].rearrange("p (l t) -> p l t", l=4), ACT.Exp),
                                  ("sum", a, b))
                    return ac_s

                def dve(e, c):
                    V = nc.vector
                    ac_s.wait(e, sums[-1])
                    q4 = hqT.rearrange("p h (t c) -> p (h t) c", t=NT)
                    k4 = kinT.rearrange("p h (t c) -> p (h t) c", t=NT)
                    for lev in range(LEVELS):
                        half, size = 1 << lev, 2 << lev
                        for src, lo in ((k4, 0), (q4, half)):
                            ex = EX[:, :, lev, :].rearrange("p a (n s) -> p a n s", s=size)[:, :, :, lo:lo + half]
                            sv = src.rearrange("p a (n s) -> p a n s", s=size)[:, :, :, lo:lo + half]
                            V.tensor_tensor(ex, ex, sv, ALU.mult)
                    V.tensor_tensor(EX[:, 0:4:2, LEVELS, :], EX[:, 0:4:2, LEVELS, :], k4[:, 0:4:2, :], ALU.mult)
                    dv_s.mark(V.tensor_tensor(EX[:, 1:4:2, LEVELS, :], EX[:, 1:4:2, LEVELS, :], q4[:, 1:4:2, :], ALU.mult), "qk")
                    mt4 = mtmp.rearrange("p (h r) t -> p r h t", r=2)

                    def lmask(m):
                        return lev_mask[:, m, :].unsqueeze(1).unsqueeze(1).broadcast_to([P, 2, 2, P])
                    for i, (_, t, m) in enumerate(scs):
                        pe_s.wait(e, scs[i])
                        b2 = 2 * (i % 4)
                        bank = PS[:, b2:b2 + 2, 0:2 * P].rearrange("p r (h t) -> p r h t", h=2)
                        dst = WH[:, :, (0, 2, 1)[t], :].rearrange("p (h r) t -> p r h t", r=2)
                        if t == 2:
                            ins = V.tensor_copy(dst, bank)
                        elif m == 0:
                            ins = V.tensor_tensor(dst, bank, lmask(0), ALU.mult)
                        else:
                            c(V.tensor_tensor(mt4, bank, lmask(m), ALU.mult))
                            ins = V.tensor_tensor(dst, dst, mt4, ALU.add)
                        dv_s.mark(ins, scs[i])
                        dv_s.wait(e, scs[i])
                    pe_s.wait(e, "o")
                    for t in range(NT):
                        ins = V.tensor_copy(MIX[:, t, 512:768], PS[:, 2 + t, 0:T])
                    dv_s.mark(ins, "o")
                    return dv_s
                stage(L + "hgrn", pe=pe, act=act, dve=dve)
            hgrn()

            def mixnorm(L=L):
                dv_s = steps("dve", ["ss", "y"])
                ac_s = steps("act", ["rt"])
                sq2 = arena(18868, NT, D)
                ssg, ssh = sm[:, 160:164], sm[:, 164:180]
                big = MIX[:, :, 0:512].rearrange("p t (g d) -> p t g d", g=2)
                small = MIX[:, :, 512:1024].rearrange("p t (h d) -> p t h d", h=8)

                def dve(e, c):
                    V = nc.vector
                    c(V.tensor_tensor(sq2, MIX, MIX, ALU.mult))
                    c(V.tensor_reduce(ssg.rearrange("p (t g) -> p t g", t=NT),
                                      sq2[:, :, 0:512].rearrange("p t (g d) -> p t g d", g=2), AX, ALU.add))
                    dv_s.mark(V.tensor_reduce(ssh.rearrange("p (t g) -> p t g", t=NT),
                                              sq2[:, :, 512:1024].rearrange("p t (g d) -> p t g d", g=8), AX, ALU.add), "ss")
                    c(V.tensor_tensor(hg, hg, bc(ngh, 1, NT), ALU.mult))
                    ac_s.wait(e, "rt")
                    c(V.reciprocal(sm[:, 160:180], sm[:, 160:180]))
                    c(V.tensor_tensor(big, big, bc(ssg.rearrange("p (t g) -> p t g", t=NT), 3, 256), ALU.mult))
                    c(V.tensor_tensor(small, small, bc(ssh.rearrange("p (t g) -> p t g", t=NT), 3, HD), ALU.mult))
                    c(V.tensor_tensor(MIX[:, :, 0:512], MIX[:, :, 0:512], bc(ngs, 1, NT), ALU.mult))
                    c(V.tensor_tensor(MIX[:, :, 512:768], MIX[:, :, 512:768], hg, ALU.mult))
                    dv_s.mark(V.tensor_tensor(MIX[:, :, 768:1024], MIX[:, :, 768:1024], rg, ALU.mult), "y")
                    return dv_s

                def act(e, c):
                    dv_s.wait(e, "ss")
                    nc.scalar.activation(ssg, ssg, ACT.Sqrt, bias=eps_col, scale=1.0 / 256)
                    ac_s.mark(nc.scalar.activation(ssh, ssh, ACT.Sqrt, bias=eps_col, scale=1.0 / HD), "rt")
                    return ac_s
                stage(L + "mixnorm", dve=dve, act=act)
            mixnorm()
            first_wo2 = ring_loads(io[f"w_out{layer}"], 2)
            out_proj_stage(L + "out", MIX, arena(18868, KC, T), first_wo2, MOD[:, 2, :], arena(21940, CW),
                           pool=load_gain(io[f"ng_ffn{layer}"]))

            EW = KC * FE
            ERAW = [ring[:, q * EW:(q + 1) * EW] for q in range(3)]
            ESPL = [r32(3 * EW + q * 2 * EW, 2, EW) for q in range(4)]
            hs, hs32 = r32(11 * EW, 2, KC, T)
            hidr, hidr32 = r32(RB + 23552, 2, 2, 2 * T)
            e_ld = [sem(L + f"e_ld{q}") for q in range(3)]
            s_ehi, s_elo, s_euse, s_silu, s_t, s_hm, s_hh, s_hs, s_xs, s_xl = (
                sem(L + n) for n in ("ehi", "elo", "euse", "silu", "t", "hm", "hh", "hs", "xs", "xl"))
            release_ring(L + "out")

            def triples(e, body):
                for m in range(PEEL):
                    body(m, 3 * m + 2, m)
                with e.Fori(0, (NEXP - 1 - PEEL) // 4) as i:
                    for q in range(4):
                        body(i * 4 + (PEEL + q), i * 12 + (3 * (PEEL + q) + 2), PEEL + q)

            def load_experts(sp, layer=layer, e_ld=e_ld, s_elo=s_elo, ERAW=ERAW, triples=triples):
                def part(kind, x, n, s):
                    if s >= 3:
                        sp.wait_ge(s_elo, n - 2)
                    src = io[f"w_{kind}{layer}"][x]
                    dst = ERAW[s % 3]
                    if kind == "down":
                        src = src.rearrange("(k p) n -> p k n", p=P)
                        dst = dst.rearrange("p (k n) -> p k n", k=2)
                    sp.dma_start(dst, src).then_inc(e_ld[s % 3], 16)
                part("gate", 0, 0, 0)
                part("up", 0, 1, 1)

                def body(m, n, mm):
                    s = 3 * mm + 2
                    part("gate", m + 1, n, s)
                    part("up", m + 1, n + 1, s + 1)
                    part("down", m, n + 2, s + 2)
                triples(sp, body)
                part("down", NEXP - 1, 3 * NEXP - 1, 3 * NEXP - 1)

            norm_T_stage(L + "norm_ffn", [(X[:, t, :], MOD[:, 4, :], MOD[:, 3, :]) for t in range(NT)],
                         hT, 14336)
            CMB = arena(14336, NEXP, T)
            sg = arena(22528, 2, 512)
            wrt, brt = arena(22528, KC, 36), arena(22816, 36)
            lgt, comb = arena(22860, NT, 36), arena(22940, NT, NEXP)
            r1, r2 = arena(23010, NT, 4, 8), arena(23080, NT, 8)
            selr, _ = r32(RB + 24064, P)
            cTr, cTr32 = r32(RB + 24192, 2, T)
            rr = arena(23500, 200)

            def router(L=L, layer=layer, selr=selr, cTr=cTr, cTr32=cTr32):
                s_in = sem(L + "rt_in")
                bcs = [("b", i) for i in range(16)]
                pe_s = steps("pe", ["lg", "tr"] + bcs)
                ac_s = steps("act", ["e0", "e1"] + bcs[1::2])
                dv_s = steps("dve", ["x0", "x1", "comb", "tr"] + bcs[0::2])

                def pool(e, c):
                    e.dma_start(wrt, io[f"w_rt{layer}"].rearrange("p (k n) -> p k n", k=KC)).then_inc(s_in, 16)
                    e.dma_start(brt, io[f"b_rt{layer}"].unsqueeze(0).broadcast_to([P, 36])).then_inc(s_in, 16)
                    e.wait_ge(s_in, 32)

                def pe(e, c):
                    e.wait_ge(s_in, 32)
                    for t in range(NT):
                        for k in range(KC):
                            ins = nc.tensor.matmul(PS[:, 0, t * 36:(t + 1) * 36], hT[:, k, t * P:(t + 1) * P], wrt[:, k, :],
                                                   start=(k == 0), stop=(k == KC - 1))
                    pe_s.mark(ins, "lg")
                    dv_s.wait(e, "comb")
                    for t in range(NT):
                        ins = nc.tensor.transpose(PS[0:NEXP, 1, t * P:(t + 1) * P], comb[:, t, :], ident)
                    pe_s.mark(ins, "tr")
                    dv_s.wait(e, "tr")
                    for i in range(16):
                        if i >= 4:
                            (dv_s if i % 2 == 0 else ac_s).wait(e, ("b", i - 4))
                        for a in range(2):
                            x = 2 * i + a
                            for half in range(2):
                                ins = nc.tensor.matmul(PS[:, 2 + i % 4, a * T:(a + 1) * T],
                                                       selr[0:NEXP, x:x + 1].broadcast_to([NEXP, P]), cTr[0:NEXP, half, :],
                                                       start=half == 0, stop=half == 1)
                        pe_s.mark(ins, ("b", i))
                    return pe_s

                def dst(i):
                    return CMB[:, 2 * i:2 * i + 2, :], PS[:, 2 + i % 4, :].rearrange("p (a t) -> p a t", a=2)

                def act(e, c):
                    dv_s.wait(e, "x0")
                    ac_s.mark(nc.scalar.activation(rr[:, 8:16], rr[:, 8:16], ACT.Exp), "e0")
                    dv_s.wait(e, "x1")
                    ac_s.mark(nc.scalar.activation(rr[:, 66:68], rr[:, 66:68], ACT.Exp), "e1")
                    for i in range(1, 16, 2):
                        pe_s.wait(e, ("b", i))
                        ac_s.mark(nc.scalar.copy(*dst(i)), ("b", i))
                    return ac_s

                def dve(e, c):
                    V = nc.vector

                    def v(lo, n):
                        return rr[:, lo:lo + n].rearrange("p (t k) -> p t k", t=NT)
                    c(V.tensor_copy(selr[0:NEXP, 0:NEXP], ident[0:NEXP, 0:NEXP]))
                    e.wait_ge(s_in, 32)
                    pe_s.wait(e, "lg")
                    c(V.tensor_tensor(lgt, PS[:, 0, 0:72].rearrange("p (t k) -> p t k", t=NT), bc(brt, 1, NT), ALU.add))
                    grp = lgt[:, :, 0:NGRP]
                    c(V.tensor_reduce(rr[:, 0:2], grp, AX, ALU.max))
                    dv_s.mark(V.tensor_tensor(v(8, 8), grp, bc(rr[:, 0:2], 2, NGRP), ALU.subtract), "x0")
                    c(V.tensor_tensor(v(16, 8), grp, bc(rr[:, 0:2], 2, NGRP), ALU.is_equal))
                    c(V.scalar_tensor_tensor(v(16, 8), v(16, 8), -1000.0, bc(iota[:, 0:NGRP], 1, NT), ALU.mult, ALU.add))
                    c(V.tensor_reduce(rr[:, 2:4], v(16, 8), AX, ALU.min))
                    c(V.tensor_tensor(v(16, 8), v(16, 8), bc(rr[:, 2:4], 2, NGRP), ALU.is_equal))
                    ac_s.wait(e, "e0")
                    c(V.tensor_reduce(rr[:, 4:6], v(8, 8), AX, ALU.add))
                    c(V.reciprocal(rr[:, 4:6], rr[:, 4:6]))
                    ex = lgt[:, :, NGRP:].rearrange("p t (g x) -> p t g x", g=NGRP)
                    c(V.tensor_tensor(r1, ex, bc(v(16, 8), 3, EPG), ALU.mult))
                    c(V.tensor_reduce(r2, r1.rearrange("p t g x -> p t x g"), AX, ALU.add))
                    for t in range(NT):
                        ins = V.max(v(24, 16)[:, t, :], r2[:, t, :])
                    c(ins)
                    for t in range(NT):
                        ins = V.max_index(v(40, 16).bitcast(U32)[:, t, :], v(24, 16)[:, t, :], r2[:, t, :])
                    c(ins)
                    dv_s.mark(V.tensor_tensor(rr[:, 66:68], v(24, 16)[:, :, 1], v(24, 16)[:, :, 0], ALU.subtract), "x1")
                    c(V.tensor_copy(v(70, 16), v(40, 16).bitcast(U32)))
                    ac_s.wait(e, "e1")
                    c(V.tensor_scalar_add(rr[:, 68:70], rr[:, 66:68], 1.0))
                    c(V.reciprocal(rr[:, 68:70], rr[:, 68:70]))
                    c(V.tensor_tensor(rr[:, 68:70], rr[:, 68:70], rr[:, 4:6], ALU.mult))
                    c(V.tensor_tensor(rr[:, 66:68], rr[:, 66:68], rr[:, 68:70], ALU.mult))
                    io8 = bc(iota[:, 0:EPG], 1, NT)
                    for j, w in ((0, 68), (1, 66)):
                        o = v(90 + 16 * j, 16)
                        c(V.tensor_tensor(o, io8, bc(v(70, 16)[:, :, j], 2, EPG), ALU.is_equal))
                        c(V.tensor_tensor(o, o, bc(rr[:, w:w + 2], 2, EPG), ALU.mult))
                    c(V.tensor_tensor(v(90, 16), v(90, 16), v(106, 16), ALU.add))
                    dv_s.mark(V.tensor_tensor(comb.rearrange("p t (g x) -> p t g x", g=NGRP), bc(v(16, 8), 3, EPG),
                                              bc(v(90, 16), 2, NGRP), ALU.mult), "comb")
                    pe_s.wait(e, "tr")
                    c(V.tensor_copy(cTr[0:NEXP, 0, :], PS[0:NEXP, 1, 0:T]))
                    dv_s.mark(V.tensor_tensor(cTr[0:NEXP, 1, :], PS[0:NEXP, 1, 0:T], cTr32[0:NEXP, 0, :], ALU.subtract), "tr")
                    for i in range(0, 16, 2):
                        pe_s.wait(e, ("b", i))
                        dv_s.mark(V.tensor_copy(*dst(i)), ("b", i))
                    return dv_s
                stage(L + "router", pool=pool, pe=pe, act=act, dve=dve)
            router()

            def experts(L=L, e_ld=e_ld, ESPL=ESPL, hs=hs, hs32=hs32, hidr=hidr, hidr32=hidr32, s_ehi=s_ehi, s_elo=s_elo,
                        s_euse=s_euse, s_silu=s_silu, s_t=s_t, s_hm=s_hm, s_hh=s_hh, s_hs=s_hs, s_xs=s_xs, s_xl=s_xl,
                        triples=triples, ERAW=ERAW):
                def act(e, c):
                    def hi(n, s):
                        if isinstance(n, int):
                            e.wait_ge(e_ld[n % 3], 16 * (n // 3 + 1))
                        else:
                            e.wait_ge(e_ld[s[0] % 3], s[1] * 16)
                            s = s[0]
                        if s >= 4:
                            e.wait_ge(s_euse, n - 3)
                        nc.scalar.copy(ESPL[s % 4][0][:, 0, :], ERAW[s % 3]).then_inc(s_ehi, 1)

                    def silu(x, xx):
                        e.wait_ge(s_euse, 1 if xx == 0 else x * 3)
                        if xx >= 2:
                            e.wait_ge(s_hs, x - 1)
                        nc.scalar.activation(sg[:, xx % 2, :], PS[:, 2 * (xx % 2), :], ACT.Silu).then_inc(s_silu, 1)
                    nc.scalar.copy(hs[:, 0], hT).then_inc(s_xs, 1)
                    hi(0, 0)
                    hi(1, 1)

                    def body(m, n, mm):
                        s = 3 * mm + 2
                        for j in range(3):
                            hi(n + j, s + j if isinstance(n, int) else (s + j, m + (1 + (2 + j) // 3)))
                        silu(m, mm)
                    triples(e, body)
                    hi(3 * NEXP - 1, 3 * NEXP - 1)
                    silu(NEXP - 1, NEXP - 1)
                    e.wait_ge(s_silu, NEXP)

                def dve(e, c):
                    V = nc.vector

                    def lo(n, s):
                        e.wait_ge(s_ehi, n + 1)
                        V.tensor_tensor(ESPL[s % 4][0][:, 1, :], ERAW[s % 3], ESPL[s % 4][1][:, 0, :],
                                        ALU.subtract).then_inc(s_elo, 1)

                    def hidden(x, xx):
                        b = xx % 2
                        s2 = sg[:, b, :].rearrange("p (f t) -> p f t", f=2)
                        e.wait_ge(s_silu, x + 1)
                        V.tensor_tensor(s2, s2, CMB[:, bass.ds(x, 1), :].broadcast_to([P, 2, T]), ALU.mult).then_inc(s_t, 1)
                        e.wait_ge(s_t, x + 1)
                        e.wait_ge(s_euse, 2 if xx == 0 else x * 3 + 1)
                        V.tensor_tensor(sg[:, b, :], sg[:, b, :], PS[:, 2 * b + 1, :], ALU.mult).then_inc(s_hm, 1)
                        e.wait_ge(s_hm, x + 1)
                        if xx >= 2:
                            e.wait_ge(s_euse, x * 3 - 1)
                        V.tensor_copy(hidr[:, b, 0, :], sg[:, b, :]).then_inc(s_hh, 1)
                        e.wait_ge(s_hh, x + 1)
                        V.tensor_tensor(hidr[:, b, 1, :], sg[:, b, :], hidr32[:, b, 0, :], ALU.subtract).then_inc(s_hs, 1)
                    e.wait_ge(s_xs, 1)
                    V.tensor_tensor(hs[:, 1], hT, hs32[:, 0], ALU.subtract).then_inc(s_xl, 1)
                    lo(0, 0)
                    lo(1, 1)

                    def body(m, n, mm):
                        s = 3 * mm + 2
                        for j in range(3):
                            lo(n + j, s + j)
                        hidden(m, mm)
                    triples(e, body)
                    lo(3 * NEXP - 1, 3 * NEXP - 1)
                    hidden(NEXP - 1, NEXP - 1)
                    e.wait_ge(s_hs, NEXP)

                def pe(e, c):
                    def up(x, n, s, bank):
                        e.wait_ge(s_elo, n + 1)
                        w = ESPL[s % 4][0].rearrange("p h (k f) -> p h k f", k=KC)
                        for f in range(2):
                            fs = slice(f * P, (f + 1) * P)
                            for k in range(KC):
                                ins = exact3(PS[:, bank, f * T:(f + 1) * T], (w[:, 0, k, fs], w[:, 1, k, fs]),
                                             (hs[:, 0, k, :], hs[:, 1, k, :]), k == 0, k == KC - 1)
                        ins.then_inc(s_euse, 1)

                    def gate_up(x, n, s, xx):
                        if xx >= 2:
                            e.wait_ge(s_hm, x - 1)
                        up(x, n, s, 2 * (xx % 2))
                        up(x, n + 1, s + 1, 2 * (xx % 2) + 1)

                    def down(x, n, s, xx, start=False, stop=False):
                        e.wait_ge(s_elo, n + 1)
                        e.wait_ge(s_hs, x + 1)
                        w = ESPL[s % 4][0].rearrange("p h (k n) -> p h k n", k=2)
                        h = hidr[:, xx % 2].rearrange("p s (f t) -> p s f t", f=2)
                        for f in range(2):
                            for t in range(NT):
                                for n2 in range(2):
                                    tk, cols = slice(t * P, (t + 1) * P), slice(n2 * CW, (n2 + 1) * CW)
                                    ins = exact3(PS[:, 4 + 2 * t + n2, :], (h[:, 0, f, tk], h[:, 1, f, tk]),
                                                 (w[:, 0, f, cols], w[:, 1, f, cols]), start and f == 0, stop and f == 1)
                        ins.then_inc(s_euse, 1)
                    e.wait_ge(s_xl, 1)
                    gate_up(0, 0, 0, 0)

                    def body(m, n, mm):
                        s = 3 * mm + 2
                        gate_up(m + 1, n, s, mm + 1)
                        down(m, n + 2, s + 2, mm, start=mm == 0)
                    triples(e, body)
                    down(NEXP - 1, 3 * NEXP - 1, 3 * NEXP - 1, NEXP - 1, stop=True)
                    e.wait_ge(s_euse, 3 * NEXP)
                stage(L + "experts", pe=pe, act=act, dve=dve, **({"pool": pool_mod1} if L == "l0_" else {}))
            stream.append(load_experts)
            experts()
            add_norm_stage(L + "moe_out", MOD[:, 5, :], io["final2"] if layer == LAYERS - 1 else None, 20480)

        s_store = sem("s_store")

        def pool_out(e, c):
            e.dma_start(io["out"].rearrange("o (t p) d -> p (o t) d", p=P), X[:]).then_inc(s_store, 16)
            e.wait_ge(s_store, 16)
        stage("store", pool=pool_out)

        block = ctx.enter_context(nc.Block())

        def run(eng, kind, chain):
            for k, (name, progs) in enumerate(stages):
                if kind in progs:
                    steps = progs[kind](eng, chain)
                    if steps is not None:
                        assert steps.n == len(steps.names), (name, kind, steps.n)
                        eng.wait_ge(steps.sem, steps.base + steps.n)
                eng.sem_inc(s_bar, 1)
                eng.wait_ge(s_bar, 4 * (k + 1))

        @block.sync
        def _(sp):
            for load in stream:
                load(sp)

        @block.scalar
        def _(act):
            run(act, "act", Chain(act, s_a))

        @block.vector
        def _(dve):
            run(dve, "dve", Chain(dve, s_v))

        @block.tensor
        def _(pe):
            run(pe, "pe", None)

        @block.gpsimd
        def _(pool):
            run(pool, "pool", Chain(pool, s_g))


def slots(w):
    n = w.shape[1] // CW
    return np.ascontiguousarray(w.reshape(P, KC, n, CW).transpose(2, 0, 1, 3)).reshape(n, P, SLOT)


def layout(i):
    a = {"const": CONST, "x": i["x"], "ctx": i["ctx"]}
    a["c_all"] = np.concatenate([i[n].reshape(P, KC) for n in ("c", "c_ctx", "c_2")], 1)
    ada = slots(i["ada_w"][0])
    a["ada_w"] = ada[:4]
    a["mod_w"] = np.concatenate([ada[4:]] + [slots(i["w_ada_2"][l]) for l in range(LAYERS)])
    a["mod_b"] = np.concatenate([i["ada_b"][0][4 * CW:]] + [i["b_ada_2"][l] for l in range(LAYERS)]).reshape(-1, CW)
    a["ada_b"] = i["ada_b"][0]
    a["norm_g0"], a["norm_g1"] = i["norm_g"][0, 0], i["norm_g"][0, 1]
    w = i["dn_w_in"][0]
    a["dn_w"] = slots(w[:, :4 * D])
    a["dn_wba"] = np.ascontiguousarray(w[:, 4 * D:]).reshape(P, KC * 32)
    a["dn_cw"] = np.ascontiguousarray(i["dn_conv_w"][0].reshape(DN_TAPS, 24, P).transpose(2, 1, 0)).reshape(P, 24 * DN_TAPS)
    a["dn_alog"], a["dn_dt"] = i["dn_a_log"].reshape(16), i["dn_dt_bias"].reshape(16)
    a["dn_ng"] = i["dn_norm_g"][0]
    a["dn_wo"] = slots(i["dn_w_out"][0])
    a["peer_wq"] = slots(i["peer_w_q"][0])
    a["peer_kT"] = np.ascontiguousarray(i["peer_keys"][0].reshape(16, NK, P).transpose(2, 0, 1)).reshape(P, 16 * NK)
    a["peer_u"] = np.ascontiguousarray(i["peer_u"][0].reshape(NK, NK, P, KC).transpose(1, 2, 3, 0)).reshape(NK, P, KC * P)
    a["peer_v"] = i["peer_v"][0].reshape(NK, NK, D)
    a["final_g"] = i["final_g"]
    for l in range(LAYERS):
        w = i["w_in_2"][l]
        cut = np.cumsum([512, 768, 8, 256, 256, 256, 256, 256, 256, 256, 256])[:-1]
        z, xbc, dt, hq, hf, hi, hg, rq, rk, rv, rg = np.split(w, cut, axis=1)

        def swap(m):
            return m.reshape(D, RE_H, 2, HD // 2)[:, :, ::-1].reshape(D, RE_H * HD)
        a[f"w_in{l}"] = slots(np.concatenate([xbc, hq, hf, rq, rk, swap(rq), swap(rk), hf, z, hi, hg, rv, rg], 1))
        a[f"w_dt{l}"] = np.ascontiguousarray(dt).reshape(P, KC * 8)
        a[f"ng_mix{l}"], a[f"ng_ffn{l}"] = i["norm_mix_g_2"][l], i["norm_ffn_g_2"][l]
        cw = np.concatenate([i["conv_w_2"][l], i["conv_b_2"][l][None]], 0)
        a[f"conv{l}"] = np.ascontiguousarray(cw.reshape(5, 6, P).transpose(2, 1, 0)).reshape(P, 30)
        a[f"ssd{l}"] = np.concatenate([i["ssd_dt_bias_2"][l], i["ssd_a_log_2"][l], i["ssd_d_2"][l]])
        a[f"ng_ssd{l}"], a[f"ng_hgrn{l}"] = i["ssd_norm_g_2"][l], i["hgrn_norm_g_2"][l]
        a[f"w_out{l}"] = slots(i["w_out_2"][l])
        a[f"w_rt{l}"] = np.concatenate([i["w_grp_2"][l], i["w_exp_2"][l]], 1).reshape(P, KC * 36)
        a[f"b_rt{l}"] = np.concatenate([i["b_grp_2"][l], i["b_exp_2"][l]])
        a[f"w_gate{l}"] = i["w_gate_2"][l].reshape(NEXP, P, KC * FE)
        a[f"w_up{l}"] = i["w_up_2"][l].reshape(NEXP, P, KC * FE)
        a[f"w_down{l}"] = i["w_down_2"][l]
    a["lbs"] = i["hgrn_lower_bounds_2"]
    a["lbsT"] = np.ascontiguousarray(i["hgrn_lower_bounds_2"].reshape(2, 2, P).transpose(2, 0, 1)).reshape(P, 4)
    a["final2"] = i["final_norm_g_2"]
    return a


def kernel(**inputs):
    import concourse.bacc as bacc
    from concourse.bass_utils import run_bass_kernel_spmd as run

    arrays = layout({k: np.asarray(v) for k, v in inputs.items()})
    arrays = {f"in_{k}": np.ascontiguousarray(v) for k, v in arrays.items()}
    nc = bacc.Bacc("TRN2", target_bir_lowering=False, num_devices=1)
    io = {k[3:]: nc.dram_tensor(k, v.shape, mybir.dt.from_np(v.dtype), kind="ExternalInput").ap()
          for k, v in arrays.items()}
    io["out"] = nc.dram_tensor("out", (1, T, D), F32, kind="ExternalOutput").ap()
    build(nc, io)
    r = run(nc, [arrays], core_ids=[0])
    return r.results[0]["out"]
```
